# Optimizing a Trainium2 kernel written in Bass

```python
import math
import jax, jax.numpy as jnp
from jax import lax
import numpy as np

D_MODEL = 1024
BATCH = 1
SEQ = 512
DEPTH = 2

CTX_LEN = 256
GRID_W = 64

MIX_W = D_MODEL
N_GROUPS = 4
GROUP_W = MIX_W // N_GROUPS
IN_W = 8 * GROUP_W

NA_HEADS = 4
NA_HEAD_DIM = GROUP_W // NA_HEADS
NA_ROWS = 8
NA_COLS = 16

CONV_K = 3

FOURIER_HEADS = 4
FOURIER_DIM = GROUP_W // FOURIER_HEADS

S5_CH = 16
S5_GROUPS = GROUP_W // S5_CH
S5_STATE = 64

PEER_HEADS = 8
PEER_KEYS = 128
PEER_EXPERTS = PEER_KEYS * PEER_KEYS
PEER_TOPK = 16
PEER_QDIM = 256
PEER_HALF = PEER_QDIM // 2
PEER_CHUNK = 128

N_MOD = 6
EPS = 1e-6
NEG = -1e30

kernel_name = "hybrid_natten_conv_fnet_s5_peer_dit"

def rmsnorm(x, g):
    xf = x.astype(jnp.float32)
    y = xf * lax.rsqrt(jnp.mean(xf * xf, axis=-1, keepdims=True) + EPS)
    return y.astype(x.dtype) * g

def split_heads(t, n):
    b, l, _ = t.shape
    return t.reshape(b, l, n, -1).transpose(0, 2, 1, 3)

def neighbourhood_attention(q, k, v, q_c, k_c, v_c, rpb):
    b, s, _ = q.shape
    rows = s // GRID_W
    wr = min(NA_ROWS, rows)
    wc = min(NA_COLS, GRID_W)
    scale = NA_HEAD_DIM ** -0.5
    qg = split_heads(q, NA_HEADS).reshape(b, NA_HEADS, rows, GRID_W, NA_HEAD_DIM)
    kg = split_heads(k, NA_HEADS).reshape(b, NA_HEADS, rows, GRID_W, NA_HEAD_DIM)
    vg = split_heads(v, NA_HEADS).reshape(b, NA_HEADS, rows, GRID_W, NA_HEAD_DIM)
    kh_c = split_heads(k_c, NA_HEADS)
    vh_c = split_heads(v_c, NA_HEADS)

    r = jnp.arange(rows)
    col = jnp.arange(GRID_W)
    row_start = jnp.clip(r - wr // 2, 0, rows - wr)
    key_rows = row_start[:, None] + jnp.arange(wr)[None, :]
    col_start = jnp.clip(col - wc // 2, 0, GRID_W - wc)
    nk = wr * GRID_W
    k_blk = kg[:, :, key_rows].reshape(b, NA_HEADS, rows, nk, NA_HEAD_DIM)
    v_blk = vg[:, :, key_rows].reshape(b, NA_HEADS, rows, nk, NA_HEAD_DIM)
    key_col = jnp.broadcast_to(col[None, :], (wr, GRID_W)).reshape(nk)
    col_ok = (key_col[None, :] >= col_start[:, None]) & (key_col[None, :] < col_start[:, None] + wc)
    d_row = jnp.repeat(key_rows, GRID_W, axis=1) - r[:, None]
    d_col = jnp.clip(key_col[None, :] - col[:, None], -(NA_COLS - 1), NA_COLS - 1)
    bias = rpb[:, (d_row + NA_ROWS - 1)[:, None, :], (d_col + NA_COLS - 1)[None, :, :]]

    s_lat = jnp.einsum('bhrqd,bhrkd->bhrqk', qg, k_blk).astype(jnp.float32) * scale + bias.astype(jnp.float32)
    s_lat = jnp.where(col_ok, s_lat, NEG)
    s_ctx = jnp.einsum('bhrqd,bhcd->bhrqc', qg, kh_c).astype(jnp.float32) * scale
    p = jax.nn.softmax(jnp.concatenate([s_lat, s_ctx], axis=-1), axis=-1).astype(q.dtype)
    o = (jnp.einsum('bhrqk,bhrkd->bhrqd', p[..., :nk], v_blk)
         + jnp.einsum('bhrqc,bhcd->bhrqd', p[..., nk:], vh_c))
    o = o.transpose(0, 2, 3, 1, 4).reshape(b, s, GROUP_W)

    o_c = None
    if q_c is not None:
        lc = q_c.shape[1]
        qh_c = split_heads(q_c, NA_HEADS)
        s_cc = jnp.einsum('bhqd,bhkd->bhqk', qh_c, kh_c).astype(jnp.float32) * scale
        p_cc = jax.nn.softmax(s_cc, axis=-1).astype(q_c.dtype)
        o_c = jnp.einsum('bhqk,bhkd->bhqd', p_cc, vh_c).transpose(0, 2, 1, 3).reshape(b, lc, GROUP_W)
    return o, o_c

def short_gated_conv(gate_b, gate_c, xin, conv_w):
    z = gate_c * xin
    z = lax.conv_general_dilated(z, conv_w[:, None, :], window_strides=(1,),
                                 padding=((CONV_K // 2, CONV_K // 2),),
                                 dimension_numbers=('NWC', 'WIO', 'NWC'),
                                 feature_group_count=GROUP_W)
    return gate_b * z

def fourier_mix(z):
    b, l, _ = z.shape
    zz = z.astype(jnp.float32).reshape(b, l, FOURIER_HEADS, FOURIER_DIM)
    f = jnp.fft.fft2(zz, axes=(1, 3), norm='ortho').real
    return f.reshape(b, l, GROUP_W).astype(z.dtype)

def _linear_combine(e1, e2):
    a1, b1 = e1
    a2, b2 = e2
    return a1 * a2, a2 * b1 + b2

def s5_bidirectional(u, u_c, a_re, a_im, b_re, b_im, c_re, c_im, log_dt, d_skip, w_glu, ctx_out):
    f32 = jnp.float32
    A = lax.complex(a_re.astype(f32), a_im.astype(f32))
    dt = jnp.exp(log_dt.astype(f32))[..., None]
    a_bar = jnp.exp(A * dt)
    b_bar = ((a_bar - 1.0) / A)[..., None] * lax.complex(b_re.astype(f32), b_im.astype(f32))
    c_mat = lax.complex(c_re.astype(f32), c_im.astype(f32))

    def drive(t, dr):
        bz, l, _ = t.shape
        tg = t.astype(f32).reshape(bz, l, S5_GROUPS, S5_CH).astype(jnp.complex64)
        return jnp.einsum('blgh,gph->lbgp', tg, b_bar[dr])

    def scan(bseq, dr, reverse):
        a = jnp.broadcast_to(a_bar[dr][None, None], (bseq.shape[0], 1) + a_bar.shape[1:])
        _, h = lax.associative_scan(_linear_combine, (a, bseq), reverse=reverse)
        return h

    def readout(h, dr):
        return jnp.einsum('lbgp,ghp->blgh', h, c_mat[dr]).real

    def finish(t, y):
        bz, l, _ = t.shape
        y = y.reshape(bz, l, GROUP_W) + d_skip.astype(f32) * t.astype(f32)
        g = jax.nn.gelu(y)
        return (g * jax.nn.sigmoid(g @ w_glu.astype(f32))).astype(t.dtype)

    hf_c = scan(drive(u_c, 0), 0, False)
    hb_c = scan(drive(u_c, 1), 1, True)
    bf = drive(u, 0).at[0].add(a_bar[0] * hf_c[-1])
    bb = drive(u, 1).at[-1].add(a_bar[1] * hb_c[0])
    y_x = finish(u, readout(scan(bf, 0, False), 0) + readout(scan(bb, 1, True), 1))
    y_c = finish(u_c, readout(hf_c, 0) + readout(hb_c, 1)) if ctx_out else None
    return y_x, y_c

def peer_ffn(h, wq, keys, u, v):
    bz, l, d = h.shape
    t = bz * l
    ht = h.reshape(t, d)
    q = (ht @ wq).reshape(t, PEER_HEADS, 2, PEER_HALF)
    s = jnp.einsum('thzd,hznd->thzn', q, keys).astype(jnp.float32)
    s1, i1 = lax.top_k(s[:, :, 0], PEER_TOPK)
    s2, i2 = lax.top_k(s[:, :, 1], PEER_TOPK)
    cand = (s1[..., :, None] + s2[..., None, :]).reshape(t, PEER_HEADS, PEER_TOPK * PEER_TOPK)
    cidx = (i1[..., :, None] * PEER_KEYS + i2[..., None, :]).reshape(t, PEER_HEADS, PEER_TOPK * PEER_TOPK)
    top, pos = lax.top_k(cand, PEER_TOPK)
    eidx = jnp.take_along_axis(cidx, pos, axis=-1)
    gate = jax.nn.softmax(top, axis=-1)
    n_chunks = t // PEER_CHUNK

    def chunk_fn(args):
        xc, ic, gc = args
        act = jax.nn.gelu(jnp.einsum('td,thkd->thk', xc, u[ic]).astype(jnp.float32)) * gc
        return jnp.einsum('thk,thkd->td', act.astype(xc.dtype), v[ic])

    out = lax.map(chunk_fn, (ht.reshape(n_chunks, PEER_CHUNK, d),
                             eidx.reshape(n_chunks, PEER_CHUNK, PEER_HEADS, PEER_TOPK),
                             gate.reshape(n_chunks, PEER_CHUNK, PEER_HEADS, PEER_TOPK)))
    return out.reshape(bz, l, d).astype(h.dtype)

def merge_groups(outs, grp_g, w_out):
    y = rmsnorm(jnp.stack(outs, axis=-2), grp_g)
    return y.reshape(y.shape[:-2] + (MIX_W,)) @ w_out

def hybrid_layer(x, ctx, c, c_ctx, ada_w, ada_b, norm1_g, norm2_g, w_in, na_rpb, conv_w,
                 s5_a_re, s5_a_im, s5_b_re, s5_b_im, s5_c_re, s5_c_im, s5_log_dt, s5_d, s5_w_glu,
                 grp_g, w_out, peer_wq, peer_keys, peer_u, peer_v, update_ctx):
    G = GROUP_W
    mod_x = (jax.nn.silu(c) @ ada_w + ada_b)[:, None, :]
    mod_c = (jax.nn.silu(c_ctx) @ ada_w + ada_b)[None, None, :]
    sh1, sc1, g1, sh2, sc2, g2 = jnp.split(mod_x, N_MOD, axis=-1)
    csh1, csc1, cg1, csh2, csc2, cg2 = jnp.split(mod_c, N_MOD, axis=-1)

    hx = rmsnorm(x, norm1_g) * (1.0 + sc1) + sh1
    hc = rmsnorm(ctx, norm1_g) * (1.0 + csc1) + csh1
    q, k, v, cb, cc, cx, fz, su = jnp.split(hx @ w_in, 8, axis=-1)
    if update_ctx:
        q_c, k_c, v_c, cb_c, cc_c, cx_c, fz_c, su_c = jnp.split(hc @ w_in, 8, axis=-1)
    else:
        q_c = None
        k_c = hc @ w_in[:, 1 * G:2 * G]
        v_c = hc @ w_in[:, 2 * G:3 * G]
        su_c = hc @ w_in[:, 7 * G:8 * G]

    att_x, att_c = neighbourhood_attention(q, k, v, q_c, k_c, v_c, na_rpb)
    conv_x = short_gated_conv(cb, cc, cx, conv_w)
    four_x = fourier_mix(fz)
    ssm_x, ssm_c = s5_bidirectional(su, su_c, s5_a_re, s5_a_im, s5_b_re, s5_b_im, s5_c_re, s5_c_im,
                                    s5_log_dt, s5_d, s5_w_glu, update_ctx)

    x = x + g1 * merge_groups([att_x, conv_x, four_x, ssm_x], grp_g, w_out)
    x = x + g2 * peer_ffn(rmsnorm(x, norm2_g) * (1.0 + sc2) + sh2, peer_wq, peer_keys, peer_u, peer_v)

    if update_ctx:
        conv_c = short_gated_conv(cb_c, cc_c, cx_c, conv_w)
        four_c = fourier_mix(fz_c)
        ctx = ctx + cg1 * merge_groups([att_c, conv_c, four_c, ssm_c], grp_g, w_out)
        ctx = ctx + cg2 * peer_ffn(rmsnorm(ctx, norm2_g) * (1.0 + csc2) + csh2,
                                   peer_wq, peer_keys, peer_u, peer_v)
    return x, ctx

def setup_inputs(seed: int = 0) -> dict:
    key = jax.random.key(seed)
    ks = iter(jax.random.split(key, 40))
    f32 = jnp.float32

    def nrm(shape, s):
        return jax.random.normal(next(ks), shape, f32) * s

    D = D_MODEL
    n_idx = jnp.arange(S5_STATE, dtype=f32)
    return {
        "x": nrm((BATCH, SEQ, D), 1.0),
        "c": nrm((BATCH, D), 1.0),
        "ctx": nrm((BATCH, CTX_LEN, D), 1.0),
        "c_ctx": nrm((D,), 1.0),
        "ada_w": nrm((DEPTH, D, N_MOD * D), 0.5 * D ** -0.5),
        "ada_b": nrm((DEPTH, N_MOD * D), 0.02),
        "norm1_g": 1.0 + nrm((DEPTH, D), 0.02),
        "norm2_g": 1.0 + nrm((DEPTH, D), 0.02),
        "w_in": nrm((DEPTH, D, IN_W), D ** -0.5),
        "na_rpb": nrm((DEPTH, NA_HEADS, 2 * NA_ROWS - 1, 2 * NA_COLS - 1), 0.02),
        "conv_w": nrm((DEPTH, CONV_K, GROUP_W), CONV_K ** -0.5),
        "s5_a_re": -0.5 + nrm((DEPTH, 2, S5_GROUPS, S5_STATE), 0.01),
        "s5_a_im": math.pi * n_idx + nrm((DEPTH, 2, S5_GROUPS, S5_STATE), 0.01),
        "s5_b_re": nrm((DEPTH, 2, S5_GROUPS, S5_STATE, S5_CH), (2.0 * S5_CH) ** -0.5),
        "s5_b_im": nrm((DEPTH, 2, S5_GROUPS, S5_STATE, S5_CH), (2.0 * S5_CH) ** -0.5),
        "s5_c_re": nrm((DEPTH, 2, S5_GROUPS, S5_CH, S5_STATE), (2.0 * S5_STATE) ** -0.5),
        "s5_c_im": nrm((DEPTH, 2, S5_GROUPS, S5_CH, S5_STATE), (2.0 * S5_STATE) ** -0.5),
        "s5_log_dt": jax.random.uniform(next(ks), (DEPTH, 2, S5_GROUPS), f32,
                                        minval=math.log(1e-3), maxval=math.log(1e-1)),
        "s5_d": nrm((DEPTH, GROUP_W), 1.0),
        "s5_w_glu": nrm((DEPTH, GROUP_W, GROUP_W), GROUP_W ** -0.5),
        "grp_g": 1.0 + nrm((DEPTH, N_GROUPS, GROUP_W), 0.02),
        "w_out": nrm((DEPTH, MIX_W, D), MIX_W ** -0.5),
        "peer_wq": nrm((DEPTH, D, PEER_HEADS * PEER_QDIM), D ** -0.5),
        "peer_keys": nrm((DEPTH, PEER_HEADS, 2, PEER_KEYS, PEER_HALF), PEER_HALF ** -0.5),
        "peer_u": nrm((DEPTH, PEER_EXPERTS, D), D ** -0.5),
        "peer_v": nrm((DEPTH, PEER_EXPERTS, D), 1.0),
        "final_g": 1.0 + nrm((D,), 0.02),
    }

def reference(x, c, ctx, c_ctx, ada_w, ada_b, norm1_g, norm2_g, w_in, na_rpb, conv_w,
              s5_a_re, s5_a_im, s5_b_re, s5_b_im, s5_c_re, s5_c_im, s5_log_dt, s5_d, s5_w_glu,
              grp_g, w_out, peer_wq, peer_keys, peer_u, peer_v, final_g):
    for i in range(DEPTH):
        x, ctx = hybrid_layer(x, ctx, c, c_ctx, ada_w[i], ada_b[i], norm1_g[i], norm2_g[i], w_in[i],
                              na_rpb[i], conv_w[i], s5_a_re[i], s5_a_im[i], s5_b_re[i], s5_b_im[i],
                              s5_c_re[i], s5_c_im[i], s5_log_dt[i], s5_d[i], s5_w_glu[i], grp_g[i],
                              w_out[i], peer_wq[i], peer_keys[i], peer_u[i], peer_v[i],
                              update_ctx=(i < DEPTH - 1))
    return rmsnorm(x, final_g)


_drawn_inputs = setup_inputs


def setup_inputs(seed=0):
    import zlib

    import numpy as np

    out = dict(_drawn_inputs(seed))
    spreads = {}
    factors = {}
    for name, (base, spread) in spreads.items():
        noise = np.random.default_rng([zlib.crc32(name.encode()), seed]).standard_normal(out[name].shape)
        drawn = base * np.exp(spread * noise) if base else spread * noise
        out[name] = __import__('jax').numpy.asarray(drawn.astype(out[name].dtype))
    for name, factor in factors.items():
        out[name] = (out[name] * factor).astype(out[name].dtype)
    return out
```

```python
import math
from contextlib import ExitStack

import numpy as np

import concourse.bass as bass
from concourse import mybir

F32 = mybir.dt.float32
U32 = mybir.dt.uint32
ALU = mybir.AluOpType
ACT = mybir.ActivationFunctionType
AX = mybir.AxisListType

P = 128
D = 1024
KC = D // P
SEQ, CTX = 512, 256
TOK = SEQ + CTX
NT, NTL = TOK // P, SEQ // P
DEPTH = 2
N_MOD = 6
GW = 256
NH, DH = 4, 64
GRID_W, ROWS = 64, SEQ // 64
NS = 10
UNITS = 16
EPS = 1e-6
PH, PK, TOPK = 8, 128, 16
HALVES = 2 * PH
SLOTS = PH * TOPK
RING = 8
SH1, SC1, G1, SH2, SC2, G2 = range(N_MOD)


class Signal:

    def __init__(self, sem):
        self.sem, self.n = sem, 0

    def on(self, ins, by=1):
        ins.then_inc(self.sem, by)
        self.n += by
        return self.n


def done(eng, signal, ins):
    eng.wait_ge(signal.sem, signal.on(ins))


class Machine:

    def __init__(self, nc, ctx):
        self.nc = nc
        self.stages = 0
        self.gathered = [Signal(ctx.enter_context(nc.semaphore(f"gathered{j}"))) for j in range(RING)]
        self.spent = []
        self.x = ctx.enter_context(nc.sbuf_tensor("x_stream", [P, NT, D], F32))
        self.ident = ctx.enter_context(nc.sbuf_tensor("ident", [P, P], F32))
        self.cond = ctx.enter_context(nc.sbuf_tensor("cond_silu", [P, KC, 2], F32))
        self.pick = ctx.enter_context(nc.sbuf_tensor("pick_stream", [2, 2, P], F32))
        self.iota = ctx.enter_context(nc.sbuf_tensor("iota16", [P, TOPK], F32))
        self.gate2 = ctx.enter_context(nc.sbuf_tensor("gate2_rows", [P, 2, D], F32))
        self.h = ctx.enter_context(nc.sbuf_tensor("h_tok", [P, NT, D], F32))
        self.big = ctx.enter_context(nc.sbuf_tensor("big", [P, HALVES * TOK], F32))
        self.bank = [ctx.enter_context(nc.psum_tensor(f"bank{i}", [P, 512], F32)) for i in range(8)]


    def part(self, first, pattern, **sizes):
        n = math.prod(sizes.values())
        names = " ".join(sizes)
        return self.big[:, first:first + n].rearrange(f"p ({names}) -> p {pattern}", **sizes)


class Stage:

    def __init__(self, m, last=False):
        self.m, self.nc, self.stack, self.last = m, m.nc, ExitStack(), last
        m.stages += 1

    def __enter__(self):
        return self

    def __exit__(self, *e):
        return self.stack.__exit__(*e)

    def sem(self, name):
        sem = self.stack.enter_context(self.nc.semaphore(name))
        self.m.spent.append(sem.num)
        return Signal(sem)

    def sb(self, name, shape, dtype=F32):
        return self.stack.enter_context(self.nc.sbuf_tensor(f"{name}_{self.m.stages}", shape, dtype))

    def block(self):
        return self.stack.enter_context(self.nc.Block(no_gpsimd_drain=not self.last))


def bcast(ap, shape):
    return ap.broadcast_to(shape)


def stage_clear(m):
    with m.nc.Block(no_gpsimd_drain=True) as block:

        @block.gpsimd
        def _(pool):
            pool.sem_clear(range(min(m.spent), max(m.spent) + 1))

    m.spent.clear()


def stage_load(m, a):
    nc = m.nc
    with Stage(m) as s:
        loads, c_in, c_out = s.sem("loads_done"), s.sem("cond_loaded"), s.sem("silu_done")
        raw = s.sb("cond_raw", [P, KC, 2])
        block = s.block()

        @block.sync
        def _(sp):
            c_in.on(sp.dma_start(raw[:, :, :], a["cond"]), 16)
            loads.on(sp.dma_start(m.x[:, :NTL, :], a["x"].rearrange("(t p) d -> p t d", p=P)), 16)
            loads.on(sp.dma_start(m.x[:, NTL:, :], a["ctx"].rearrange("(t p) d -> p t d", p=P)), 16)
            loads.on(sp.dma_start(m.ident[:, :], a["ident"]), 16)
            loads.on(sp.dma_start(m.pick[:, :, :], a["pick"]), 16)
            loads.on(sp.dma_start(m.iota[:, :], a["iota"]), 16)
            sp.wait_ge(loads.sem, loads.n)

        @block.scalar
        def _(act):
            act.wait_ge(c_in.sem, 16)
            c_out.on(nc.scalar.activation(m.cond[:, :, :], raw[:, :, :], ACT.Silu))


def stage_modulation(m, a, l, rows, ht):
    nc = m.nc
    NB = N_MOD * D // 512
    W = 3
    with Stage(m) as s:
        ring = m.part(0, "w k n", w=W, k=KC, n=512)
        mod = s.sb("mod", [2, N_MOD, D])
        bias = m.h[0:2, :, :]
        gains = ht[0:2, 0:4, :].rearrange("a k t -> a (k t)")[:, 0:2 * D].rearrange("a (g d) -> a g d", g=2)
        w_in = [s.sem(f"ada_w_loaded{j}") for j in range(W)]
        small = s.sem("bias_loaded")
        mm, ev, chain, bc, cp = (s.sem(n) for n in ("mod_mm", "mod_evac", "mod_rows", "row_mm", "row_copied"))
        w = a["ada_w"][l].rearrange("(k p) n -> p k n", p=P)
        modv = mod[:, :, :].rearrange("a j d -> a (j d)")
        biasv = bias[:, :, :].rearrange("a j d -> a (j d)")
        rowv = rows[:, :, :, :].rearrange("p s j d -> p s (j d)")
        block = s.block()

        @block.sync
        def _(sp):
            for r in range(2):
                small.on(sp.dma_start(bias[r:r + 1, :, :].rearrange("a j d -> a (j d)"), a["ada_b"][l:l + 1, :]), 16)
                small.on(sp.dma_start(gains[r:r + 1, 0, :], a["norm1_g"][l:l + 1, :]), 16)
                small.on(sp.dma_start(gains[r:r + 1, 1, :], a["norm2_g"][l:l + 1, :]), 16)
            for j in range(W):
                sp.dma_start(ring[:, j, :, :], w[:, :, 512 * j:512 * (j + 1)]).then_inc(w_in[j].sem, 16)
            with sp.Fori(0, NB // W - 1) as i:
                for j in range(W):
                    sp.wait_ge(mm.sem, i * W + (j + 1))
                    sp.dma_start(ring[:, j, :, :], w[:, :, bass.ds((i + 1) * (W * 512) + 512 * j, 512)]) \
                      .then_inc(w_in[j].sem, 16)

        @block.tensor
        def _(pe):
            for b in range(NB):
                pe.wait_ge(w_in[b % W].sem, 16 * (b // W + 1))
                if b >= 4:
                    pe.wait_ge(ev.sem, b - 3)
                for k in range(KC):
                    last = nc.tensor.matmul(m.bank[b % 4][0:2, :], m.cond[:, k, :], ring[:, b % W, k, :],
                                            start=(k == 0), stop=(k == KC - 1))
                mm.on(last)
            pe.wait_ge(chain.sem, 2)
            for st in range(2):
                for b in range(NB):
                    n = st * NB + b
                    if n >= 4:
                        pe.wait_ge(cp.sem, n - 3)
                    bc.on(nc.tensor.matmul(m.bank[4 + n % 4][:, :], m.pick[:, st, :], modv[:, 512 * b:512 * b + 512],
                                           start=True, stop=True))

        @block.vector
        def _(dve):
            dve.wait_ge(small.sem, small.n)
            for b in range(NB):
                dve.wait_ge(mm.sem, b + 1)
                ev.on(nc.vector.tensor_tensor(modv[:, 512 * b:512 * b + 512], m.bank[b % 4][0:2, :],
                                              biasv[:, 512 * b:512 * b + 512], ALU.add))
            dve.wait_ge(ev.sem, NB)
            for j, g in ((SC1, 0), (SC2, 1)):
                chain.on(nc.vector.scalar_tensor_tensor(out=mod[:, j, :], in0=mod[:, j, :], scalar=1.0,
                                                        in1=gains[:, g, :], op0=ALU.add, op1=ALU.mult))

        @block.scalar
        def _(act):
            for n in range(2 * NB):
                st, b = divmod(n, NB)
                act.wait_ge(bc.sem, n + 1)
                dst = rowv[:, st, 512 * b:512 * b + 512] if b < 10 else m.gate2[:, st, 512 * (b - 10):512 * (b - 9)]
                cp.on(nc.scalar.activation(dst, m.bank[4 + n % 4][:, :], ACT.Copy))


def stage_norm(m, rows, sc, sh, ht, tiles):
    nc = m.nc
    with Stage(m) as s:
        junk, ssq = s.sb("squares", [P, D]), s.sb("ssq", [P, NT])
        sq, ms, rt, hr, tp, ev, ch = (s.sem(n) for n in ("squares_done", "mean_done", "root_done", "h_done",
                                                         "transposed", "t_copied", "norm_chain"))
        n = len(tiles)
        block = s.block()

        @block.scalar
        def _(act):
            for t in tiles:
                done(act, sq, nc.scalar.activation(junk[:, :], m.x[:, t, :], ACT.Square, accum_out=ssq[:, t:t + 1]))
            act.wait_ge(ms.sem, 2)
            rt.on(nc.scalar.activation(ssq[:, :n], ssq[:, :n], ACT.Sqrt))
            for i, t in enumerate(tiles):
                for c in range(2):
                    act.wait_ge(tp.sem, 2 * i + c + 1)
                    ev.on(nc.scalar.activation(ht[:, 4 * c:4 * c + 4, t * P:(t + 1) * P],
                                               m.bank[(2 * i + c) % 8][:, :].rearrange("p (k n) -> p k n", k=4),
                                               ACT.Copy))

        @block.vector
        def _(dve):
            dve.wait_ge(sq.sem, n)
            done(dve, ms, nc.vector.tensor_scalar(ssq[:, :n], ssq[:, :n], 1.0 / D, EPS, ALU.mult, ALU.add))
            ms.on(nc.vector.reciprocal(ssq[:, :n], ssq[:, :n]))
            dve.wait_ge(rt.sem, 1)
            for t in tiles:
                st = t // NTL
                done(dve, ch, nc.vector.scalar_tensor_tensor(out=m.h[:, t, :], in0=m.x[:, t, :], scalar=ssq[:, t:t + 1],
                                                             in1=rows[:, st, sc, :], op0=ALU.mult, op1=ALU.mult))
                hr.on(nc.vector.tensor_tensor(m.h[:, t, :], m.h[:, t, :], rows[:, st, sh, :], ALU.add))

        @block.tensor
        def _(pe):
            for i, t in enumerate(tiles):
                pe.wait_ge(hr.sem, i + 1)
                for c in range(2):
                    u = 2 * i + c
                    if u >= 8:
                        pe.wait_ge(ev.sem, u - 7)
                    for k in range(4):
                        last = nc.tensor.transpose(m.bank[u % 8][:, k * P:(k + 1) * P],
                                                   m.h[:, t, (4 * c + k) * P:(4 * c + k + 1) * P], m.ident[:, :])
                    tp.on(last)


def stage_project(m, w_view, groups, ht):
    nc = m.nc
    W = 3
    with Stage(m) as s:
        ring = s.sb("w_ring", [P, W, KC, GW])
        w_in = [s.sem(f"w_loaded{j}") for j in range(W)]
        used, mm, ev = s.sem("w_used"), s.sem("product_done"), s.sem("product_copied")
        units = []
        for g, (col, dst, feat, spans) in enumerate(groups):
            if feat:
                units.append((g, [(dst[:, b, t0:t0 + n], b, t0, n) for b in range(2) for t0, n in spans]))
            else:
                units.append((g, [(dst[:, t, :], None, t * P, GW) for t in spans]))
        block = s.block()

        @block.sync
        def _(sp):
            for g, (col, *_r) in enumerate(groups):
                if g >= W:
                    sp.wait_ge(used.sem, g - W + 1)
                sp.dma_start(ring[:, g % W, :, :], w_view[:, :, GW * col:GW * (col + 1)]).then_inc(w_in[g % W].sem, 16)

        @block.tensor
        def _(pe):
            u = 0
            for g, outs in units:
                pe.wait_ge(w_in[g % W].sem, 16 * (g // W + 1))
                for i, (_dst, b, t0, n) in enumerate(outs):
                    if u >= 8:
                        pe.wait_ge(ev.sem, u - 7)
                    for k in range(KC):
                        if b is None:
                            lhs, rhs = ht[:, k, t0:t0 + P], ring[:, g % W, k, :]
                        else:
                            lhs, rhs = ring[:, g % W, k, b * P:(b + 1) * P], ht[:, k, t0:t0 + n]
                        last = nc.tensor.matmul(m.bank[u % 8][:, :n], lhs, rhs, start=(k == 0), stop=(k == KC - 1))
                    mm.on(last)
                    u += 1
                pe.wait_ge(mm.sem, u)
                used.on(pe.nop())

        @block.scalar
        def _(act):
            u = 0
            for g, outs in units:
                for dst, _b, _t0, n in outs:
                    act.wait_ge(mm.sem, u + 1)
                    ev.on(nc.scalar.activation(dst, m.bank[u % 8][:, :n], ACT.Copy))
                    u += 1


def stage_attention(m, a, l, qt, kt, v, y, tiles, ht):
    nc = m.nc
    scale = DH ** -0.5
    with Stage(m) as s:
        bias = s.sb("pos_bias", [P, NH, 16, GRID_W])
        falling = ht[:, 0:6, :].rearrange("p k t -> p (k t)")[:, 0:NH * 16 * GRID_W] \
            .rearrange("p (h j c) -> p h j c", h=NH, j=16)
        flip = s.sb("flip", [P, P])
        mask = s.sb("col_mask", [P, GRID_W])
        sc = s.sb("scores", [P, 2, TOK])
        pt = s.sb("probs_T", [P, 2, TOK])
        st = s.sb("softmax_stats", [P, 2, 4])
        loads, biased, turned = s.sem("bias_loaded"), s.sem("bias_masked"), s.sem("bias_turned")
        sm, tp, om = s.sem("scores_mm"), s.sem("probs_transposed"), s.sem("out_mm")
        sb_, mx, od = s.sem("scores_biased"), s.sem("max_done"), s.sem("out_done")
        ex, pc = s.sem("exp_done"), s.sem("probsT_copied")
        todo = [(t, h) for t in tiles for h in range(NH)]
        pad, rows = 2 * GRID_W - 1, 17
        block = s.block()

        def keys(t):
            return (0, TOK) if t < NTL else (SEQ, CTX)

        @block.sync
        def _(sp):
            loads.on(sp.dma_start(mask[:, :], a["col_mask"]), 16)
            loads.on(sp.dma_start(flip[:, :], a["flip"]), 16)
            for h in range(NH):
                for half in range(2):
                    src = bass.AP(tensor=a["rpb"].tensor,
                                  offset=((l * NH + h) * rows + 1 - half) * pad,
                                  ap=[[1, GRID_W], [pad, 16], [1, GRID_W]])
                    loads.on(sp.dma_start(falling[64 * half:64 * half + 64, h, :, :], src), 16)

        @block.vector
        def _(dve):
            dve.wait_ge(loads.sem, loads.n)
            for b in range(2 * NH):
                h, j = b // 2, 8 * (b % 2)
                dve.wait_ge(turned.sem, b + 1)
                biased.on(nc.vector.tensor_tensor(bias[:, h, j:j + 8, :],
                                                  m.bank[b][:, :].rearrange("p (j c) -> p j c", j=8),
                                                  bcast(mask[:, :].unsqueeze(1), [P, 8, GRID_W]), ALU.add))
            dve.wait_ge(biased.sem, 2 * NH)

            def finish(i):
                t, h = todo[i]
                dve.wait_ge(om.sem, i + 1)
                done(dve, od, nc.vector.reciprocal(st[:, i % 2, 2:3], st[:, i % 2, 1:2]))
                od.on(nc.vector.tensor_scalar(y[:, t, h * DH:(h + 1) * DH], m.bank[6 + i % 2][:, 0:DH],
                                              st[:, i % 2, 2:3], None, ALU.mult))

            for i, (t, h) in enumerate(todo):
                dve.wait_ge(sm.sem, i + 1)
                if i >= 2:
                    finish(i - 2)
                k0, n = keys(t)
                if t < NTL:
                    j0 = 7 - 2 * t
                    sb_.on(nc.vector.scalar_tensor_tensor(
                        out=sc[:, i % 2, 0:SEQ], in0=m.bank[i % 2][:, :], scalar=scale,
                        in1=bias[:, h, :, :].rearrange("p j c -> p (j c)")[:, (j0) * GRID_W:(j0 + 8) * GRID_W],
                        op0=ALU.mult, op1=ALU.add))
                sb_.on(nc.vector.tensor_scalar(sc[:, i % 2, SEQ:TOK], m.bank[2 + i % 2][:, 0:CTX], scale, None, ALU.mult))
                dve.wait_ge(sb_.sem, sb_.n)
                mx.on(nc.vector.tensor_reduce(out=st[:, i % 2, 0:1], in_=sc[:, i % 2, k0:TOK], axis=AX.X,
                                              op=ALU.max, negate=True))
            for i in (len(todo) - 2, len(todo) - 1):
                finish(i)

        @block.scalar
        def _(act):
            def copy_t(i):
                t, _h = todo[i]
                act.wait_ge(tp.sem, i + 1)
                if t < NTL:
                    nc.scalar.activation(pt[:, i % 2, 0:SEQ], m.bank[4][:, :], ACT.Copy)
                pc.on(nc.scalar.activation(pt[:, i % 2, SEQ:TOK], m.bank[5][:, 0:CTX], ACT.Copy))

            for i, (t, h) in enumerate(todo):
                k0, n = keys(t)
                act.wait_ge(mx.sem, i + 1)
                if i >= 2:
                    act.wait_ge(od.sem, 2 * (i - 1))
                ex.on(nc.scalar.activation(sc[:, i % 2, k0:TOK], sc[:, i % 2, k0:TOK], ACT.Exp,
                                           bias=st[:, i % 2, 0:1], accum_out=st[:, i % 2, 1:2]))
                if i >= 1:
                    copy_t(i - 1)
            copy_t(len(todo) - 1)

        @block.tensor
        def _(pe):
            def scores(i):
                t, h = todo[i]
                r = slice(DH * (h % 2), DH * (h % 2) + DH)
                if i >= 2:
                    pe.wait_ge(mx.sem, i - 1)
                q = qt[r, h // 2, t * P:(t + 1) * P]
                if t < NTL:
                    nc.tensor.matmul(m.bank[i % 2][:, :], q, kt[r, h // 2, 0:SEQ], start=True, stop=True)
                sm.on(nc.tensor.matmul(m.bank[2 + i % 2][:, 0:CTX], q, kt[r, h // 2, SEQ:TOK], start=True, stop=True))

            def weighted(i):
                t, h = todo[i]
                tiles_k = range(NT) if t < NTL else range(NTL, NT)
                pe.wait_ge(pc.sem, i + 1)
                if i >= 2:
                    pe.wait_ge(od.sem, 2 * (i - 1))
                for n, kt_ in enumerate(tiles_k):
                    last = nc.tensor.matmul(m.bank[6 + i % 2][:, 0:DH], pt[:, i % 2, kt_ * P:(kt_ + 1) * P],
                                            v[:, kt_, h * DH:(h + 1) * DH], start=(n == 0), stop=(n == len(tiles_k) - 1))
                om.on(last)

            pe.wait_ge(loads.sem, loads.n)
            for b in range(2 * NH):
                h, j = b // 2, 8 * (b % 2)
                turned.on(nc.tensor.matmul(m.bank[b][:, :], flip[:, :],
                                           falling[:, h, j:j + 8, :].rearrange("p j c -> p (j c)"),
                                           start=True, stop=True))
            pe.wait_ge(biased.sem, 2 * NH)
            scores(0)
            for i, (t, h) in enumerate(todo):
                if i + 1 < len(todo):
                    scores(i + 1)
                pe.wait_ge(ex.sem, i + 1)
                if i >= 1:
                    pe.wait_ge(pc.sem, i)
                for kt_ in range(0 if t < NTL else NTL, NT):
                    dst = m.bank[4][:, kt_ * P:(kt_ + 1) * P] if kt_ < NTL else m.bank[5][:, (kt_ - NTL) * P:(kt_ - NTL + 1) * P]
                    last = nc.tensor.transpose(dst, sc[:, i % 2, kt_ * P:(kt_ + 1) * P], m.ident[:, :])
                tp.on(last)
                if i >= 1:
                    weighted(i - 1)
            weighted(len(todo) - 1)


def spans_of(tiles):
    return [(0, 0, SEQ)] + ([(1, SEQ, CTX)] if len(tiles) > NTL else [])


def stage_conv(m, a, l, cb, cc, cx, y, tiles):
    nc = m.nc
    with Stage(m) as s:
        z = s.sb("conv_z", [P, 2, TOK + 4])
        w = s.sb("conv_w", [P, 2, 3])
        loads, ch, fin = s.sem("conv_w_loaded"), s.sem("conv_chain"), s.sem("conv_done")
        tp, cp = s.sem("conv_transposed"), s.sem("conv_copied")
        spans = spans_of(tiles)
        block = s.block()

        @block.sync
        def _(sp):
            loads.on(sp.dma_start(w[:, :, :], a["conv_w"][l]), 16)

        @block.vector
        def _(dve):
            for n in range(2):
                ch.on(nc.vector.memset(z[:, n, :], 0.0))
            dve.wait_ge(ch.sem, ch.n)
            dve.wait_ge(loads.sem, 16)
            for f in range(2):
                for st, t0, n in spans:
                    z0 = t0 + 1 + 2 * st
                    t = slice(t0, t0 + n)
                    done(dve, ch, nc.vector.tensor_tensor(z[:, f, z0:z0 + n], cc[:, f, t], cx[:, f, t], ALU.mult))
                    done(dve, ch, nc.vector.tensor_scalar(cx[:, f, t], z[:, f, z0 - 1:z0 - 1 + n], w[:, f, 0:1], None, ALU.mult))
                    for j in (1, 2):
                        done(dve, ch, nc.vector.scalar_tensor_tensor(out=cx[:, f, t], in0=z[:, f, z0 - 1 + j:z0 - 1 + j + n],
                                                                     scalar=w[:, f, j:j + 1], in1=cx[:, f, t],
                                                                     op0=ALU.mult, op1=ALU.add))
                    fin.on(nc.vector.tensor_tensor(cx[:, f, t], cx[:, f, t], cb[:, f, t], ALU.mult))

        @block.tensor
        def _(pe):
            pe.wait_ge(fin.sem, 2 * len(spans))
            for i, t in enumerate(tiles):
                for f in range(2):
                    last = nc.tensor.transpose(m.bank[i][:, f * P:(f + 1) * P], cx[:, f, t * P:(t + 1) * P], m.ident[:, :])
                tp.on(last)

        @block.scalar
        def _(act):
            for i, t in enumerate(tiles):
                act.wait_ge(tp.sem, i + 1)
                cp.on(nc.scalar.activation(y[:, t, GW:2 * GW], m.bank[i][:, 0:GW], ACT.Copy))


def stage_fourier(m, a, fz, y, tiles):
    nc = m.nc
    with Stage(m) as s:
        tab = [s.sb("dft_lat", [P, NTL, 2, SEQ]), s.sb("dft_ctx", [P, NT - NTL, 2, CTX])]
        ch = s.sb("dft_channels", [P, 2, P])
        pf = s.sb("dft_positions", [P, 2, 2, TOK])
        loads, mm, cp, om, oc = (s.sem(n) for n in ("dft_loaded", "pos_mm", "pos_copied", "chan_mm", "four_copied"))
        spans = spans_of(tiles)
        block = s.block()
        first = [(st, t0, n, f, c) for st, t0, n in spans for f in range(2) for c in range(2)]

        @block.sync
        def _(sp):
            loads.on(sp.dma_start(ch[:, :, :], a["dft_chan"]), 16)
            loads.on(sp.dma_start(tab[0][:, :, :, :], a["dft_lat"]), 16)
            if len(spans) > 1:
                loads.on(sp.dma_start(tab[1][:, :, :, :], a["dft_ctx"]), 16)

        @block.tensor
        def _(pe):
            pe.wait_ge(loads.sem, loads.n)
            for i, (st, t0, n, f, c) in enumerate(first):
                if i >= 4:
                    pe.wait_ge(cp.sem, i - 3)
                for lt in range(n // P):
                    last = nc.tensor.matmul(m.bank[i % 4][:, :n], fz[:, t0 // P + lt, f * P:(f + 1) * P],
                                            tab[st][:, lt, c, :], start=(lt == 0), stop=(lt == n // P - 1))
                mm.on(last)
            pe.wait_ge(cp.sem, len(first))
            for i, t in enumerate(tiles):
                if i >= 4:
                    pe.wait_ge(oc.sem, i - 3)
                for f in range(2):
                    for c in range(2):
                        last = nc.tensor.matmul(m.bank[4 + i % 4][:, f * P:(f + 1) * P], pf[:, f, c, t * P:(t + 1) * P],
                                                ch[:, c, :], start=(c == 0), stop=(c == 1))
                om.on(last)

        @block.scalar
        def _(act):
            for i, (st, t0, n, f, c) in enumerate(first):
                act.wait_ge(mm.sem, i + 1)
                cp.on(nc.scalar.activation(pf[:, f, c, t0:t0 + n], m.bank[i % 4][:, :n], ACT.Copy))
            for i, t in enumerate(tiles):
                act.wait_ge(om.sem, i + 1)
                oc.on(nc.scalar.activation(y[:, t, 2 * GW:3 * GW], m.bank[4 + i % 4][:, 0:GW], ACT.Copy))


def reversed_columns(ap3, f, n):
    v = ap3[:, f, n - 1:n]
    return bass.AP(tensor=v.tensor, offset=v.offset, ap=[v.ap[0], [-1, n]])


def stage_s5_weights(m, a, l, seeds, tmp, lb, lc):
    nc = m.nc
    K = 10
    with Stage(m) as s:
        pr = s.sb("s5_params", [P, 3, UNITS])
        bw = s.sb("s5_b", [P, 2, UNITS, 16])
        cw = s.sb("s5_c", [P, 2, UNITS, 16])
        bb = s.sb("s5_b_bar", [P, 3, UNITS, 16])
        wide = s.sb("s5_b_wide", [P, UNITS, 2, P])
        loads, ch, wd, tp, cp = (s.sem(n) for n in ("s5_loaded", "s5_chain", "wide_done", "b_transposed", "b_copied"))
        block = s.block()

        @block.sync
        def _(sp):
            loads.on(sp.dma_start(pr[:, :, :], a["s5_params"][l]), 16)
            loads.on(sp.dma_start(bw[:, :, :, :], a["s5_b"][l]), 16)
            loads.on(sp.dma_start(cw[:, :, :, :], a["s5_c"][l]), 16)

        @block.vector
        def _(dve):
            V = nc.vector
            T = lambda i: tmp[:, i, :]

            def tt(o, x, z, op):
                done(dve, ch, V.tensor_tensor(o, x, z, op))

            def ts(o, x, s1, op0, s2=None, op1=None):
                done(dve, ch, V.tensor_scalar(o, x, s1, s2, op0, op1) if op1 else V.tensor_scalar(o, x, s1, None, op0))

            def stt(o, x, c, z, op0, op1):
                done(dve, ch, V.scalar_tensor_tensor(out=o, in0=x, scalar=c, in1=z, op0=op0, op1=op1))

            def real_expm1(o, x):
                ts(x, x, 2.0 ** -K, ALU.mult)
                ts(o, x, 1.0 / 4, ALU.mult, 1.0, ALU.add)
                for c in (3, 2):
                    tt(o, o, x, ALU.mult)
                    ts(o, o, 1.0 / c, ALU.mult, 1.0, ALU.add)
                tt(o, o, x, ALU.mult)
                for _ in range(K):
                    stt(o, o, 2.0, o, ALU.add, ALU.mult)

            for c in range(2):
                ch.on(V.memset(wide[:, :, c, :], 0.0))
                ch.on(V.memset(lc[:, :, c, :], 0.0))
            dve.wait_ge(loads.sem, loads.n)
            dve.wait_ge(ch.sem, ch.n)
            a_re, a_im, log_dt = pr[:, 0, :], pr[:, 1, :], pr[:, 2, :]
            dt, x, th, mr, mi, er, w2 = (T(i) for i in range(7))
            ts(x, log_dt, -1.0, ALU.mult)
            real_expm1(dt, x)
            ts(dt, dt, 1.0, ALU.add)
            done(dve, ch, V.reciprocal(dt, dt))
            tt(x, a_re, dt, ALU.mult)
            real_expm1(er, x)
            tt(th, a_im, dt, ALU.mult)
            ts(th, th, 2.0 ** -K, ALU.mult)
            tt(w2, th, th, ALU.mult)
            ts(mr, w2, -1.0 / 30, ALU.mult, 1.0, ALU.add)
            tt(mr, mr, w2, ALU.mult)
            ts(mr, mr, -1.0 / 12, ALU.mult, 1.0, ALU.add)
            tt(mr, mr, w2, ALU.mult)
            ts(mr, mr, -0.5, ALU.mult)
            ts(mi, w2, -1.0 / 20, ALU.mult, 1.0, ALU.add)
            tt(mi, mi, w2, ALU.mult)
            ts(mi, mi, -1.0 / 6, ALU.mult, 1.0, ALU.add)
            tt(mi, mi, th, ALU.mult)
            for _ in range(K):
                tt(w2, mi, mi, ALU.mult)
                stt(mi, mr, 1.0, mi, ALU.add, ALU.mult)
                ts(mi, mi, 2.0, ALU.mult)
                stt(mr, mr, 2.0, mr, ALU.add, ALU.mult)
                tt(mr, mr, w2, ALU.subtract)
            nr, ni, den, fr, fi, t1 = (T(i) for i in range(7, 13))
            stt(nr, er, 1.0, mr, ALU.add, ALU.mult)
            tt(nr, nr, er, ALU.add)
            stt(ni, er, 1.0, mi, ALU.add, ALU.mult)
            tt(den, a_re, a_re, ALU.mult)
            tt(t1, a_im, a_im, ALU.mult)
            tt(den, den, t1, ALU.add)
            done(dve, ch, V.reciprocal(den, den))
            tt(fr, nr, a_re, ALU.mult)
            tt(t1, ni, a_im, ALU.mult)
            tt(fr, fr, t1, ALU.add)
            tt(fr, fr, den, ALU.mult)
            tt(fi, ni, a_re, ALU.mult)
            tt(t1, nr, a_im, ALU.mult)
            tt(fi, fi, t1, ALU.subtract)
            tt(fi, fi, den, ALU.mult)
            wide_f = lambda f: bcast(f.unsqueeze(2), [P, UNITS, 16])
            for o, f0, f1, op in ((0, fr, fi, ALU.subtract), (1, fi, fr, ALU.add)):
                tt(bb[:, o, :, :], bw[:, 0, :, :], wide_f(f0), ALU.mult)
                tt(bb[:, 2, :, :], bw[:, 1, :, :], wide_f(f1), ALU.mult)
                tt(bb[:, o, :, :], bb[:, o, :, :], bb[:, 2, :, :], op)
            for un in range(UNITS):
                for half in range(2):
                    c0 = 32 * (un % 4) + 16 * half
                    r = slice(64 * half, 64 * half + 64)
                    wd.on(V.tensor_copy(wide[r, un, :, c0:c0 + 16], bb[r, 0:2, un, :]))
                    wd.on(V.tensor_copy(lc[r, un, 0, c0:c0 + 16], cw[r, 0, un, :]))
                    wd.on(V.tensor_scalar(lc[r, un, 1, c0:c0 + 16], cw[r, 1, un, :], -1.0, None, ALU.mult))
            ts(seeds[:, 0, 0, :], mr, 1.0, ALU.add)
            ts(seeds[:, 0, 1, :], mi, 1.0, ALU.mult)
            for j in range(NS):
                cr, ci = seeds[:, j, 0, :], seeds[:, j, 1, :]
                if j:
                    pr_, pi_ = seeds[:, j - 1, 0, :], seeds[:, j - 1, 1, :]
                    tt(cr, pr_, pr_, ALU.mult)
                    tt(t1, pi_, pi_, ALU.mult)
                    tt(cr, cr, t1, ALU.subtract)
                    stt(ci, pr_, 2.0, pi_, ALU.mult, ALU.mult)
                tt(x, cr, cr, ALU.mult)
                tt(t1, ci, ci, ALU.mult)
                tt(x, x, t1, ALU.add)
                ts(x, x, -0.5, ALU.mult, 1.5, ALU.add)
                tt(cr, cr, x, ALU.mult)
                tt(ci, ci, x, ALU.mult)
                ts(seeds[:, j, 2, :], ci, -1.0, ALU.mult)
            ts(er, er, 1.0, ALU.add)

        @block.tensor
        def _(pe):
            pe.wait_ge(wd.sem, 6 * UNITS)
            for un in range(UNITS):
                if un >= 8:
                    pe.wait_ge(cp.sem, un - 7)
                for c in range(2):
                    last = nc.tensor.transpose(m.bank[un % 8][:, c * P:(c + 1) * P], wide[:, un, c, :], m.ident[:, :])
                tp.on(last)

        @block.scalar
        def _(act):
            for un in range(UNITS):
                act.wait_ge(tp.sem, un + 1)
                cp.on(nc.scalar.activation(lb[:, un, :, :], m.bank[un % 8][:, 0:2 * P].rearrange("p (c n) -> p c n", c=2),
                                           ACT.Copy))


def stage_s5(m, a, l, u, y, tiles, seeds, radius, lb, lc, ht, gl, sg):
    nc = m.nc
    with Stage(m) as s:
        tab = ht[:, 0:4, :].rearrange("p (a c) t -> p a c t", a=2)
        dsk = s.sb("s5_d", [P, 2])
        tt_ = s.sb("table_tmp", [P, 2, 512])
        bu = s.sb("drive", [P, 2, TOK])
        wr = s.sb("scan_in", [P, 2, TOK])
        t_ = s.sb("scan_tmp", [P, 2, TOK])
        hh = ht[:, 4:8, :].rearrange("p (a c) t -> p a c t", a=2)
        ur = s.sb("u_reversed", [P, 2, TOK])
        loads, tb, bm, be, ch, hd, ym, rv, tch = (s.sem(n) for n in (
            "s5w_loaded", "table_done", "drive_mm", "drive_copied", "scan_chain", "states_done", "readout_done",
            "u_reversed_done", "table_chain"))
        bu2, rt = s.sb("rotate_tmp", [P, 2, TOK]), s.sem("rotate_chain")
        sk, ge, gm, gt, si, go = (s.sem(n) for n in ("skip_added", "gelu_done", "glu_mm", "gelu_T", "sigmoid_done",
                                                     "glu_done"))
        drive = [m.bank[0], m.bank[1], m.bank[2], m.bank[3]]
        read = [[m.bank[4], m.bank[5]], [m.bank[6], m.bank[7]]]
        block = s.block()

        @block.sync
        def _(sp):
            loads.on(sp.dma_start(dsk[:, :], a["s5_d"][l]), 16)
            loads.on(sp.dma_start(gl[:, :, :], a["s5_w_glu"][l].rearrange("(f p) n -> p f n", p=P)), 16)

        @block.gpsimd
        def _(pool):
            G = nc.gpsimd
            for un in range(UNITS):
                c, sn = tab[:, un % 2, 0, :], tab[:, un % 2, 1, :]
                if un >= 2:
                    pool.wait_ge(hd.sem, 2 * (un - 1))
                tch.on(G.memset(c[:, 0:1], 1.0))
                done(pool, tch, G.memset(sn[:, 0:1], 0.0))
                n, j = 1, 0
                while n < TOK:
                    w = min(n, TOK - n)
                    E = [seeds[:, j, q, un:un + 1] for q in range(3)]
                    a0, a1 = c[:, 0:w], sn[:, 0:w]
                    tch.on(G.tensor_scalar(tt_[:, 0, :w], a0, E[0], None, ALU.mult))
                    done(pool, tch, G.tensor_scalar(tt_[:, 1, :w], a1, E[2], None, ALU.mult))
                    done(pool, tch, G.tensor_tensor(c[:, n:n + w], tt_[:, 0, :w], tt_[:, 1, :w], ALU.add))
                    tch.on(G.tensor_scalar(tt_[:, 0, :w], a0, E[1], None, ALU.mult))
                    done(pool, tch, G.tensor_scalar(tt_[:, 1, :w], a1, E[0], None, ALU.mult))
                    last = G.tensor_tensor(sn[:, n:n + w], tt_[:, 0, :w], tt_[:, 1, :w], ALU.add)
                    if n + w < TOK:
                        done(pool, tch, last)
                    else:
                        tb.on(last)
                    n, j = n + w, j + 1

        @block.tensor
        def _(pe):
            def readout(un):
                f = (un % 8) // 4
                first, last_ = un == 4 * f, un == 8 + 4 * f + 3
                pe.wait_ge(hd.sem, 2 * (un + 1))
                d = un // 8
                for c in range(2):
                    col = {0: (CTX, SEQ, 0, CTX), 1: (0, SEQ, SEQ, CTX)}[d]
                    nc.tensor.matmul(read[f][1][:, :], lc[:, un, c, :], hh[:, un % 2, c, col[0]:col[0] + SEQ],
                                     start=first and c == 0, stop=last_ and c == 1)
                    last = nc.tensor.matmul(read[f][0][:, CTX:2 * CTX], lc[:, un, c, :],
                                            hh[:, un % 2, c, col[2]:col[2] + CTX],
                                            start=first and c == 0, stop=last_ and c == 1)
                ym.on(last)

            pe.wait_ge(rv.sem, 2)
            for un in range(UNITS):
                d, f = un // 8, (un % 8) // 4
                if un >= 1:
                    pe.wait_ge(be.sem, un)
                for c in range(2):
                    cx_, lt = (u[:, f, SEQ:TOK], u[:, f, 0:SEQ]) if d == 0 else (ur[:, f, 0:CTX], ur[:, f, CTX:TOK])
                    nc.tensor.matmul(drive[2 * c][:, CTX:2 * CTX], lb[:, un, c, :], cx_, start=True, stop=True)
                    last = nc.tensor.matmul(drive[2 * c + 1][:, :], lb[:, un, c, :], lt, start=True, stop=True)
                bm.on(last)
                if un >= 1:
                    readout(un - 1)
            readout(UNITS - 1)
            pe.wait_ge(ge.sem, 2)
            pe.wait_ge(loads.sem, loads.n)
            for i, t in enumerate(tiles):
                if i >= 2:
                    pe.wait_ge(go.sem, i - 1)
                for f in range(2):
                    last = nc.tensor.matmul(m.bank[i % 2][:, 0:GW], bu[:, f, t * P:(t + 1) * P], gl[:, f, :],
                                            start=(f == 0), stop=(f == 1))
                gm.on(last)
                for f in range(2):
                    last = nc.tensor.transpose(m.bank[2 + i % 2][:, f * P:(f + 1) * P], bu[:, f, t * P:(t + 1) * P],
                                               m.ident[:, :])
                gt.on(last)

        @block.scalar
        def _(act):
            for un in range(UNITS):
                act.wait_ge(bm.sem, un + 1)
                if un >= 1:
                    act.wait_ge(ch.sem, 8 * un - 4)
                for c in range(2):
                    act.activation(bu[:, c, 0:CTX], drive[2 * c][:, CTX:2 * CTX], ACT.Copy)
                    last = act.activation(bu[:, c, CTX:TOK], drive[2 * c + 1][:, :], ACT.Copy)
                be.on(last)
            for f in range(2):
                act.wait_ge(sk.sem, 2 * (f + 1))
                ge.on(nc.scalar.activation(bu[:, f, :], wr[:, f, :], ACT.Gelu_apprx_tanh))
            for i, t in enumerate(tiles):
                act.wait_ge(gm.sem, i + 1)
                if i >= 2:
                    act.wait_ge(go.sem, i - 1)
                si.on(nc.scalar.activation(sg[:, i % 2, :], m.bank[i % 2][:, 0:GW], ACT.Sigmoid))

        @block.vector
        def _(dve):
            V = nc.vector
            for f in range(2):
                rv.on(V.tensor_copy(ur[:, f, :], reversed_columns(u, f, TOK)))
            for un in range(UNITS):
                c, sn = tab[:, un % 2, 0, :], tab[:, un % 2, 1, :]
                dve.wait_ge(be.sem, un + 1)
                dve.wait_ge(tb.sem, un + 1)
                if un:
                    dve.wait_ge(hd.sem, 2 * un)
                ch.on(V.tensor_tensor(wr[:, 0, :], bu[:, 0, :], c, ALU.mult))
                ch.on(V.tensor_tensor(t_[:, 0, :], bu[:, 1, :], sn, ALU.mult))
                ch.on(V.tensor_tensor(wr[:, 1, :], bu[:, 1, :], c, ALU.mult))
                done(dve, ch, V.tensor_tensor(t_[:, 1, :], bu[:, 0, :], sn, ALU.mult))
                ch.on(V.tensor_tensor(wr[:, 0, :], wr[:, 0, :], t_[:, 0, :], ALU.add))
                done(dve, ch, V.tensor_tensor(wr[:, 1, :], wr[:, 1, :], t_[:, 1, :], ALU.subtract))
                r = bcast(radius[:, un:un + 1], [P, TOK])
                for q in range(2):
                    ch.on(V.tensor_tensor_scan(out=t_[:, q, :], data0=r, data1=wr[:, q, :], initial=0.0,
                                               op0=ALU.mult, op1=ALU.add))
                dve.wait_ge(ch.sem, ch.n)
                if un >= 2:
                    dve.wait_ge(ym.sem, un - 1)
                out = [hh[:, un % 2, q, :] for q in range(2)]
                if un >= 8:
                    out = [reversed_columns(hh[:, un % 2, :, :], q, TOK) for q in range(2)]
                rt.on(V.tensor_tensor(wr[:, 0, :], t_[:, 0, :], c, ALU.mult))
                rt.on(V.tensor_tensor(bu2[:, 0, :], t_[:, 1, :], sn, ALU.mult))
                rt.on(V.tensor_tensor(wr[:, 1, :], t_[:, 0, :], sn, ALU.mult))
                done(dve, rt, V.tensor_tensor(bu2[:, 1, :], t_[:, 1, :], c, ALU.mult))
                hd.on(V.tensor_tensor(out[0], wr[:, 0, :], bu2[:, 0, :], ALU.subtract))
                hd.on(V.tensor_tensor(out[1], wr[:, 1, :], bu2[:, 1, :], ALU.add))
            dve.wait_ge(ym.sem, UNITS)
            dve.wait_ge(hd.sem, hd.n)
            dve.wait_ge(loads.sem, loads.n)
            for f in range(2):
                sk.on(V.scalar_tensor_tensor(out=wr[:, f, 0:SEQ], in0=u[:, f, 0:SEQ], scalar=dsk[:, f:f + 1],
                                             in1=read[f][1][:, :], op0=ALU.mult, op1=ALU.add))
                sk.on(V.scalar_tensor_tensor(out=wr[:, f, SEQ:TOK], in0=u[:, f, SEQ:TOK], scalar=dsk[:, f:f + 1],
                                             in1=read[f][0][:, CTX:2 * CTX], op0=ALU.mult, op1=ALU.add))
            for i, t in enumerate(tiles):
                dve.wait_ge(si.sem, i + 1)
                dve.wait_ge(gt.sem, i + 1)
                go.on(V.tensor_tensor(y[:, t, 3 * GW:4 * GW], m.bank[2 + i % 2][:, 0:GW], sg[:, i % 2, :], ALU.mult))


def stage_merge(m, a, l, rows, y, yt, tiles):
    nc = m.nc
    n = len(tiles)
    with Stage(m) as s:
        w = m.part(0, "k d", k=KC, d=D)
        gg = s.sb("group_gains", [P, D])
        junk, ssq = s.sb("g_squares", [P, GW]), s.sb("g_ssq", [P, NT, 4])
        prod = s.sb("gated", [P, D])
        w_in, g_in = s.sem("w_out_loaded"), s.sem("gains_loaded")
        sq, ms, rt, yn, tp, ev, mm, add = (s.sem(x) for x in ("g_squares_done", "g_mean", "g_root", "y_normed",
                                                              "y_transposed", "y_copied", "out_mm", "x_added"))
        block = s.block()

        @block.sync
        def _(sp):
            g_in.on(sp.dma_start(gg[:, :], a["grp_g"][l:l + 1, :].broadcast_to([P, D])), 16)
            w_in.on(sp.dma_start(w[:, :, :], a["w_out"][l].rearrange("(k p) n -> p k n", p=P)), 16)

        @block.scalar
        def _(act):
            for t in tiles:
                for g in range(4):
                    done(act, sq, nc.scalar.activation(junk[:, :], y[:, t, g * GW:(g + 1) * GW], ACT.Square,
                                                       accum_out=ssq[:, t, g:g + 1]))
            act.wait_ge(ms.sem, 2)
            rt.on(nc.scalar.activation(ssq[:, :n, :], ssq[:, :n, :], ACT.Sqrt))
            for i, t in enumerate(tiles):
                for c in range(2):
                    act.wait_ge(tp.sem, 2 * i + c + 1)
                    ev.on(nc.scalar.activation(yt[:, 4 * c:4 * c + 4, t * P:(t + 1) * P],
                                               m.bank[(2 * i + c) % 4][:, :].rearrange("p (k n) -> p k n", k=4),
                                               ACT.Copy))

        @block.vector
        def _(dve):
            V = nc.vector
            dve.wait_ge(sq.sem, 4 * n)
            done(dve, ms, V.tensor_scalar(ssq[:, :n, :], ssq[:, :n, :], 1.0 / GW, EPS, ALU.mult, ALU.add))
            ms.on(V.reciprocal(ssq[:, :n, :], ssq[:, :n, :]))
            dve.wait_ge(rt.sem, 1)
            dve.wait_ge(g_in.sem, 16)
            for t in tiles:
                for g in range(4):
                    c = slice(g * GW, (g + 1) * GW)
                    yn.on(V.scalar_tensor_tensor(out=y[:, t, c], in0=y[:, t, c], scalar=ssq[:, t, g:g + 1],
                                                 in1=gg[:, c], op0=ALU.mult, op1=ALU.mult))
            for i, t in enumerate(tiles):
                for c in range(2):
                    dve.wait_ge(mm.sem, 2 * i + c + 1)
                    cols = slice(512 * c, 512 * c + 512)
                    done(dve, add, V.tensor_tensor(prod[:, cols], m.bank[4 + (2 * i + c) % 4][:, :],
                                                   rows[:, t // NTL, G1, cols], ALU.mult))
                    add.on(V.tensor_tensor(m.x[:, t, cols], m.x[:, t, cols], prod[:, cols], ALU.add))

        @block.tensor
        def _(pe):
            for i, t in enumerate(tiles):
                pe.wait_ge(yn.sem, 4 * (i + 1))
                for c in range(2):
                    u = 2 * i + c
                    if u >= 4:
                        pe.wait_ge(ev.sem, u - 3)
                    for k in range(4):
                        last = nc.tensor.transpose(m.bank[u % 4][:, k * P:(k + 1) * P],
                                                   y[:, t, (4 * c + k) * P:(4 * c + k + 1) * P], m.ident[:, :])
                    tp.on(last)
            pe.wait_ge(w_in.sem, 16)
            for i, t in enumerate(tiles):
                pe.wait_ge(ev.sem, 2 * (i + 1))
                for c in range(2):
                    u = 2 * i + c
                    if u >= 4:
                        pe.wait_ge(add.sem, 2 * (u - 3))
                    for k in range(KC):
                        last = nc.tensor.matmul(m.bank[4 + u % 4][:, :], yt[:, k, t * P:(t + 1) * P],
                                                w[:, k, 512 * c:512 * c + 512], start=(k == 0), stop=(k == KC - 1))
                    mm.on(last)


PAIRS = SLOTS // 2
PRIME = 5


def stage_peer(m, a, l, qt, tiles):
    nc = m.nc
    uv = a[f"peer_uv{l}"]
    with Stage(m) as s:
        ring = s.sb("expert_rows", [P, RING, 2 * D])
        keys = s.sb("keys_T", [P, HALVES, PK])
        qs = s.sb("q_stage", [P, 2, 2, P])
        idx, idx_next = s.sb("idx", [P, SLOTS], U32), s.sb("idx_next", [P, SLOTS], U32)
        gate, gate_next = s.sb("gate", [P, SLOTS]), s.sb("gate_next", [P, PH, TOPK])
        top = s.sb("top_scores", [P, PH, TOPK])
        best = s.sb("best", [P, 2, TOPK])
        bi = s.sb("best_idx", [P, 2, TOPK], U32)
        bif = s.sb("best_idx_f", [P, 2, TOPK])
        work = s.sb("topk_work", [P, PK])
        cand = s.sb("cand", [P, TOPK * TOPK])
        cwork = s.sb("cand_work", [P, TOPK * TOPK])
        pos, split = s.sb("cand_pos", [P, TOPK], U32), s.sb("pos_split", [P, 2, TOPK], U32)
        splitf = s.sb("pos_split_f", [P, 2, TOPK])
        hot = s.sb("one_hot", [P, 2, TOPK, TOPK])
        half = s.sb("half_idx", [P, 2, TOPK])
        red = s.sb("gate_sums", [P, PH, 2])
        junk = s.sb("dot_products", [P, 2, D], mybir.dt.bfloat16)
        dot, act_ = s.sb("dots", [P, 2, 2]), s.sb("gelu_dots", [P, 2, 2])
        diag = s.sb("diag_w", [P, 2, 2, P])
        prod = s.sb("gated_experts", [P, D])
        hcur = s.sb("h_cur", [P, D])
        k_in = s.sem("keys_loaded")
        gathered, before = m.gathered, m.gathered[0].n
        ready, dots, gel, dg, used = (s.sem(x) for x in ("idx_ready", "dots_done", "gelu_done", "diag_done", "pair_used"))
        ch, issued, begun, acc_free = s.sem("topk_chain"), s.sem("pairs_begun"), s.sem("topk_begun"), s.sem("acc_free")
        qc, sc, tk = s.sem("q_staged"), s.sem("scores_done"), s.sem("scores_read")
        ex, exi = s.sem("gates_exp"), s.sem("gates_shifted")
        acc = [m.bank[0], m.bank[1]]
        n = len(tiles)
        V = nc.vector
        block = s.block()

        class chain:

            def __init__(self, dve):
                self.dve, self.n = dve, 0
                dve.sem_clear(ch.sem)

            def __call__(self, ins):
                ins.then_inc(ch.sem, 1)
                self.n += 1
                self.dve.wait_ge(ch.sem, self.n)

        def topk_half(dve, t, h, z):
            c = chain(dve)
            if z == 0:
                dve.wait_ge(sc.sem, t * PH + (h + 1))
                dve.sem_inc(begun.sem, 1)
            sv = m.bank[2 + h % 2][:, z * PK:(z + 1) * PK]
            lo, hi = best[:, z, 0:8], best[:, z, 8:16]
            c(V.max(lo, sv))
            c(V.match_replace(work[:, :], lo, sv, -3.0e38))
            c(V.max(hi, work[:, :]))
            c(V.max_index(bi[:, z, 0:8], lo, sv))
            c(V.max_index(bi[:, z, 8:16], hi, work[:, :]))
            if z == 1:
                tk.on(V.tensor_copy(bif[:, :, :], bi[:, :, :]))

        def topk_cross(dve, t, h):
            c = chain(dve)
            c(V.tensor_tensor(cand[:, :].rearrange("p (i j) -> p i j", i=TOPK),
                              bcast(best[:, 0, :].unsqueeze(2), [P, TOPK, TOPK]),
                              bcast(best[:, 1, :].unsqueeze(1), [P, TOPK, TOPK]), ALU.add))
            lo, hi = top[:, h, 0:8], top[:, h, 8:16]
            c(V.max(lo, cand[:, :]))
            c(V.match_replace(cwork[:, :], lo, cand[:, :], -3.0e38))
            c(V.max(hi, cwork[:, :]))
            c(V.max_index(pos[:, 0:8], lo, cand[:, :]))
            c(V.max_index(pos[:, 8:16], hi, cwork[:, :]))

        def topk_index(dve, t, h):
            c = chain(dve)
            c(V.tensor_scalar(split[:, 0, :], pos[:, :], 4, None, ALU.logical_shift_right))
            c(V.tensor_scalar(split[:, 1, :], pos[:, :], 15, None, ALU.bitwise_and))
            c(V.tensor_copy(splitf[:, :, :], split[:, :, :]))
            for z in range(2):
                c(V.tensor_tensor(hot[:, z, :, :], bcast(splitf[:, z, :].unsqueeze(2), [P, TOPK, TOPK]),
                                  bcast(m.iota[:, :].unsqueeze(1), [P, TOPK, TOPK]), ALU.is_equal))
                c(V.tensor_tensor(hot[:, z, :, :], hot[:, z, :, :],
                                  bcast(bif[:, z, :].unsqueeze(1), [P, TOPK, TOPK]), ALU.mult))
                c(V.tensor_reduce(out=half[:, z, :], in_=hot[:, z, :, :], axis=AX.X, op=ALU.add))
            c(V.scalar_tensor_tensor(out=idx_next[:, h * TOPK:(h + 1) * TOPK], in0=half[:, 0, :], scalar=float(PK),
                                     in1=half[:, 1, :], op0=ALU.mult, op1=ALU.add))

        def topk_part(dve, t, part):
            h, k = divmod(part, 4)
            if k < 2:
                topk_half(dve, t, h, k)
            elif k == 2:
                topk_cross(dve, t, h)
            else:
                topk_index(dve, t, h)

        def gates_shift(dve, t):
            exi.on(V.tensor_tensor(gate_next[:, :, :], top[:, :, :], bcast(top[:, :, 0:1], [P, PH, TOPK]),
                                   ALU.subtract))

        def gates_norm(dve, t):
            c = chain(dve)
            dve.wait_ge(ex.sem, t + 1)
            c(V.tensor_reduce(out=red[:, :, 0:1], in_=gate_next[:, :, :], axis=AX.X, op=ALU.add))
            c(V.reciprocal(red[:, :, 1:2], red[:, :, 0:1]))
            c(V.tensor_tensor(gate_next[:, :, :], gate_next[:, :, :], bcast(red[:, :, 1:2], [P, PH, TOPK]), ALU.mult))

        HALF = SLOTS // 2

        def publish(eng, part):
            c = slice(part * HALF, (part + 1) * HALF)
            ready.on(V.tensor_copy(idx[:, c], idx_next[:, c]))

        def pool_tile(pool, t):
            for p in range(PAIRS):
                if p in (0, PAIRS // 2):
                    pool.wait_ge(ready.sem, t * 2 + (1 + (p > 0)))
                pool.wait_ge(used.sem, t * PAIRS + (PRIME + p - RING // 2 + 1))
                pool.sem_inc(issued.sem, 1)
                for j in range(2):
                    sl = 2 * p + j
                    nc.gpsimd.indirect_dma_start(ring[:, sl % RING, :], None, uv,
                                                 bass.IndirectOffsetOnAxis(ap=idx[:, sl:sl + 1], axis=0)) \
                      .then_inc(gathered[sl % RING].sem, 16)

        def vector_tile(dve, t, stream, with_next):
            publish(dve, 1)
            done_c = chain(dve)
            done_c(V.tensor_copy(gate[:, :], gate_next[:, :, :].rearrange("p h k -> p (h k)")))
            done_c(V.tensor_copy(hcur[:, :], m.h[:, bass.ds(t, 1), :].rearrange("p a d -> p (a d)")))

            def spread(p):
                dve.wait_ge(gel.sem, t * PAIRS + (p + 1))
                dve.wait_ge(used.sem, t * PAIRS + (PRIME + p - 1))
                for j in range(2):
                    last = V.tensor_scalar(diag[:, p % 2, j, :], m.ident[:, :], act_[:, p % 2, j:j + 1],
                                           gate[:, 2 * p + j:2 * p + j + 1], ALU.mult, ALU.mult)
                dg.on(last)

            for p in range(PAIRS):
                dve.wait_ge(dots.sem, t * PAIRS + (p + 1))
                for j in range(2):
                    sl = 2 * p + j
                    dve.wait_ge(gathered[sl % RING].sem, t * (16 * SLOTS // RING) + (before + 16 * (sl // RING + 1)))
                    last = V.tensor_tensor_reduce(out=junk[:, j, :], in0=ring[:, sl % RING, 0:D], in1=hcur[:, :], scale=1.0,
                                                  scalar=0.0, op0=ALU.mult, op1=ALU.add, accum_out=dot[:, p % 2, j:j + 1])
                dots.on(last)
                if p:
                    spread(p - 1)
                if with_next and 1 <= p <= 4 * PH:
                    topk_part(dve, t + 1, p - 1)
                if with_next and p == 4 * PH + 2:
                    gates_shift(dve, t + 1)
                if with_next and p == 4 * PH + 6:
                    gates_norm(dve, t + 1)
                if with_next and p == 4 * PH + 8:
                    publish(dve, 0)
            spread(PAIRS - 1)
            c = chain(dve)
            dve.wait_ge(used.sem, t * PAIRS + (PRIME + PAIRS))
            xt = m.x[:, bass.ds(t, 1), :].rearrange("p a d -> p (a d)")
            for j in range(2):
                cols = slice(512 * j, 512 * j + 512)
                c(V.tensor_tensor(prod[:, cols], acc[j][:, :], m.gate2[:, stream, cols], ALU.mult))
            acc_free.on(V.tensor_tensor(xt, xt, prod[:, :], ALU.add))

        def stage_scores_act(act, t, h):
            act.wait_ge(tk.sem, t * PH + (h + 1))
            qc.on(nc.scalar.activation(qs[:, h % 2, :, :], qt[:, 2 * h:2 * h + 2, bass.ds(t * P, P)], ACT.Copy))

        def scalar_tile(act, t, with_next):
            for p in range(PAIRS):
                if with_next and p % 4 == 0 and p < 4 * PH:
                    stage_scores_act(act, t + 1, p // 4)
                act.wait_ge(dots.sem, t * PAIRS + (p + 2))
                gel.on(nc.scalar.activation(act_[:, p % 2, :], dot[:, p % 2, :], ACT.Gelu_apprx_tanh))
                if with_next and p == 4 * PH + 3:
                    exp_gates(act, t + 1)

        def exp_gates(act, t):
            act.wait_ge(exi.sem, t + 1)
            ex.on(nc.scalar.activation(gate_next[:, :, :], gate_next[:, :, :], ACT.Exp))

        def scores(pe, t, h):
            pe.wait_ge(qc.sem, t * PH + (h + 1))
            for z in range(2):
                last = nc.tensor.matmul(m.bank[2 + h % 2][:, z * PK:(z + 1) * PK], qs[:, h % 2, z, :],
                                        keys[:, 2 * h + z, :], start=True, stop=True)
            sc.on(last)

        def tensor_tile(pe, t, with_next):
            for p in range(PAIRS):
                if with_next and p % 4 == 0 and p < 4 * PH:
                    scores(pe, t + 1, p // 4)
                pe.wait_ge(dg.sem, t * PAIRS + (p + 1))
                if p == 0:
                    pe.wait_ge(acc_free.sem, t + 1)
                for j in range(2):
                    for c in range(2):
                        last = nc.tensor.matmul(acc[c][:, :], diag[:, p % 2, j, :],
                                                ring[:, (2 * p + j) % RING, D + 512 * c:D + 512 * c + 512],
                                                start=(p == 0 and j == 0), stop=(p == PAIRS - 1 and j == 1))
                used.on(last)

        turn = min(n - 1, NTL)

        def every_tile(eng, body):
            with eng.Fori(0, turn) as t:
                body(t, 0, True)
            for t in range(turn, n):
                body(t, t // NTL, t + 1 < n)

        @block.sync
        def _(sp):
            sp.dma_start(keys[:, :, :], a["peer_keys"][l]).then_inc(k_in.sem, 16)

        @block.gpsimd
        def _(pool):
            every_tile(pool, lambda t, st, nxt: pool_tile(pool, t))
            for g in gathered:
                g.n += n * 16 * SLOTS // RING

        @block.vector
        def _(dve):
            dve.sem_inc(tk.sem, 2)
            dve.sem_inc(dots.sem, 1)
            dve.sem_inc(acc_free.sem, 1)
            for part in range(4 * PH):
                topk_part(dve, 0, part)
            gates_shift(dve, 0)
            gates_norm(dve, 0)
            publish(dve, 0)
            every_tile(dve, lambda t, st, nxt: vector_tile(dve, t, st, nxt))

        @block.scalar
        def _(act):
            for h in range(PH):
                stage_scores_act(act, 0, h)
            exp_gates(act, 0)
            every_tile(act, lambda t, st, nxt: scalar_tile(act, t, nxt))

        @block.tensor
        def _(pe):
            pe.sem_inc(used.sem, PRIME)
            pe.wait_ge(k_in.sem, 16)
            for h in range(PH):
                scores(pe, 0, h)
            every_tile(pe, lambda t, st, nxt: tensor_tile(pe, t, nxt))


def stage_final(m, a, out):
    nc = m.nc
    with Stage(m, last=True) as s:
        fg, junk, ssq = s.sb("final_gain", [P, D]), s.sb("f_squares", [P, D]), s.sb("f_ssq", [P, NTL])
        g_in, sq, ms, rt, fo, st = (s.sem(x) for x in ("final_gain_loaded", "f_squares_done", "f_mean", "f_root",
                                                       "final_done", "stored"))
        block = s.block()

        @block.sync
        def _(sp):
            sp.dma_start(fg[:, :], a["final_g"].broadcast_to([P, D])).then_inc(g_in.sem, 16)
            for t in range(NTL):
                sp.wait_ge(fo.sem, t + 1)
                sp.dma_start(out[t * P:(t + 1) * P, :], m.h[:, t, :]).then_inc(st.sem, 16)
            sp.wait_ge(st.sem, 16 * NTL)

        @block.scalar
        def _(act):
            for t in range(NTL):
                done(act, sq, nc.scalar.activation(junk[:, :], m.x[:, t, :], ACT.Square, accum_out=ssq[:, t:t + 1]))
            act.wait_ge(ms.sem, 2)
            rt.on(nc.scalar.activation(ssq[:, :], ssq[:, :], ACT.Sqrt))

        @block.vector
        def _(dve):
            dve.wait_ge(sq.sem, NTL)
            done(dve, ms, nc.vector.tensor_scalar(ssq[:, :], ssq[:, :], 1.0 / D, EPS, ALU.mult, ALU.add))
            ms.on(nc.vector.reciprocal(ssq[:, :], ssq[:, :]))
            dve.wait_ge(rt.sem, 1)
            dve.wait_ge(g_in.sem, 16)
            for t in range(NTL):
                fo.on(nc.vector.scalar_tensor_tensor(out=m.h[:, t, :], in0=m.x[:, t, :], scalar=ssq[:, t:t + 1],
                                                     in1=fg[:, :], op0=ALU.mult, op1=ALU.mult))


def build(nc, a, out, until=None):
    count = [0]

    def go(stage, *args):
        count[0] += 1
        if until is None or count[0] <= until:
            stage(*args)

    with ExitStack() as ctx:
        m = Machine(nc, ctx)
        go(stage_load, m, a)
        every = list(range(NT))
        spans = [(0, SEQ), (SEQ, CTX)]
        for l in range(DEPTH):
            tiles = every if l < DEPTH - 1 else every[:NTL]
            out_spans = spans[:2 if l < DEPTH - 1 else 1]
            view = lambda w: w[l].rearrange("(k p) n -> p k n", p=P)
            with nc.sbuf_tensor(f"h_feat{l}", [P, KC, TOK], F32) as ht:
                with nc.sbuf_tensor(f"mod_rows{l}", [P, 2, N_MOD - 1, D], F32) as rows:
                    go(stage_modulation, m, a, l, rows, ht)
                    go(stage_norm, m, rows, SC1, SH1, ht, every)
                    q, k, cb, cc, cx, su = (m.part(i * 2 * TOK, "f t", f=2, t=TOK) for i in (0, 1, 2, 3, 4, 7))
                    v, fz = (m.part(i * 2 * TOK, "t n", t=NT, n=GW) for i in (5, 6))
                    go(stage_project, m, view(a["w_in"]),
                       [(7, su, True, spans), (0, q, True, out_spans), (1, k, True, spans), (2, v, False, every),
                        (3, cb, True, out_spans), (4, cc, True, out_spans), (5, cx, True, out_spans),
                        (6, fz, False, tiles)], ht)
                    y = m.h
                    go(stage_attention, m, a, l, q, k, v, y, tiles, ht)
                    go(stage_conv, m, a, l, cb, cc, cx, y, tiles)
                    go(stage_fourier, m, a, fz, y, tiles)
                    lb, lc = (m.part(i * UNITS * 2 * P, "u c n", u=UNITS, c=2, n=P) for i in (0, 1))
                    gl, sg = (m.part(2 * UNITS * 2 * P + i * 2 * GW, "f n", f=2, n=GW) for i in (0, 1))
                    tmp = m.part(2 * UNITS * 2 * P + 4 * GW, "i u", i=16, u=UNITS)
                    seeds = m.part(2 * UNITS * 2 * P + 4 * GW + 16 * UNITS, "j c u", j=NS, c=3, u=UNITS)
                    go(stage_s5_weights, m, a, l, seeds, tmp, lb, lc)
                    go(stage_s5, m, a, l, su, y, tiles, seeds, tmp[:, 5, :], lb, lc, ht, gl, sg)
                    go(stage_merge, m, a, l, rows, y, ht, tiles)
                    go(stage_norm, m, rows, SC2, SH2, ht, tiles)
                qt = m.part(0, "b t", b=HALVES, t=TOK)
                go(stage_project, m, view(a["peer_wq"]),
                   [(g, qt[:, 2 * g:2 * g + 2, :], True, out_spans) for g in range(PH)], ht)
            go(stage_peer, m, a, l, qt, tiles)
            if l < DEPTH - 1:
                go(stage_clear, m)
        if until is None:
            stage_final(m, a, out)


def constants():
    i = np.arange(TOPK)
    col = np.arange(GRID_W)
    start = np.clip(col - 8, 0, GRID_W - 16)
    ok = (col[None, :] >= start[:, None]) & (col[None, :] < start[:, None] + 16)
    mask = np.where(ok, 0.0, -1e30).astype(np.float32)

    def dft(n, scale):
        w = 2 * np.pi * (np.outer(np.arange(n), np.arange(n)) % n) / n
        return np.cos(w) * scale, np.sin(w) * scale

    def positions(n):
        t = np.stack(dft(n, 1 / math.sqrt(n * DH)), 1).astype(np.float32)
        return np.ascontiguousarray(t.reshape(n // P, P, 2, n).transpose(1, 0, 2, 3))

    chan = np.zeros((P, 2, P), np.float32)
    c, sn = dft(DH, 1.0)
    for b in range(2):
        r = slice(b * DH, (b + 1) * DH)
        chan[r, 0, r], chan[r, 1, r] = c, -sn
    pick = np.zeros((2, 2, P), np.float32)
    pick[0, 0], pick[1, 1] = 1, 1
    turn = np.zeros((P, P), np.float32)
    for b in range(2):
        turn[b * GRID_W:(b + 1) * GRID_W, b * GRID_W:(b + 1) * GRID_W] = np.eye(GRID_W)[::-1]
    return {
        "ident": np.eye(P, dtype=np.float32), "pick": pick, "flip": turn,
        "iota": np.tile(i.astype(np.float32), (P, 1)),
        "col_mask": np.concatenate([mask, mask]),
        "dft_lat": positions(SEQ), "dft_ctx": positions(CTX), "dft_chan": chan,
    }


def layouts(x, c, ctx, c_ctx, ada_w, ada_b, norm1_g, norm2_g, w_in, na_rpb, conv_w, s5_a_re, s5_a_im, s5_b_re,
            s5_b_im, s5_c_re, s5_c_im, s5_log_dt, s5_d, s5_w_glu, grp_g, w_out, peer_wq, peer_keys, peer_u, peer_v,
            final_g):
    L = DEPTH

    def states(t):
        t = t.reshape(L, 2, 8, P, *t.shape[4:])
        return np.moveaxis(t, 3, 1).reshape(L, P, UNITS, *t.shape[4:])

    log_dt = np.repeat(s5_log_dt[..., None], DH, axis=-1)
    rpb = np.zeros((L, NH, 17, 2 * GRID_W - 1), np.float32)
    rpb[:, :, 1:16, 48:79] = na_rpb
    return {
        "x": x[0], "ctx": ctx[0],
        "cond": np.stack([c[0], c_ctx]).reshape(2, KC, P).transpose(2, 1, 0),
        "ada_w": ada_w, "ada_b": ada_b, "norm1_g": norm1_g, "norm2_g": norm2_g, "w_in": w_in,
        "rpb": rpb, "conv_w": conv_w.reshape(L, 3, 2, P).transpose(0, 3, 2, 1),
        "s5_params": np.stack([states(s5_a_re), states(s5_a_im), states(log_dt)], 2),
        "s5_b": np.stack([states(s5_b_re), states(s5_b_im)], 2),
        "s5_c": np.stack([states(t.transpose(0, 1, 2, 4, 3)) for t in (s5_c_re, s5_c_im)], 2),
        "s5_d": s5_d.reshape(L, 2, P).transpose(0, 2, 1), "s5_w_glu": s5_w_glu,
        "grp_g": grp_g.reshape(L, D), "w_out": w_out, "peer_wq": peer_wq,
        "peer_keys": peer_keys.reshape(L, HALVES, PK, P).transpose(0, 3, 1, 2),
        **{f"peer_uv{l}": np.concatenate([peer_u[l], peer_v[l]], axis=-1) for l in range(L)},
        "final_g": final_g[None, :],
    }


def kernel(**inputs):
    import concourse.bacc as bacc
    from concourse.bass_utils import run_bass_kernel_spmd

    arrays = layouts(**{n: np.asarray(v) for n, v in inputs.items()})
    arrays.update(constants())
    arrays = {n: np.ascontiguousarray(v) for n, v in arrays.items()}
    nc = bacc.Bacc("TRN2", target_bir_lowering=False, num_devices=1)
    aps = {n: nc.dram_tensor(f"in_{n}", v.shape, F32, kind="ExternalInput").ap() for n, v in arrays.items()}
    out = nc.dram_tensor("out", (SEQ, D), F32, kind="ExternalOutput").ap()
    build(nc, aps, out)
    r = run_bass_kernel_spmd(nc, [{f"in_{n}": v for n, v in arrays.items()}], core_ids=[0])
    return r.results[0]["out"].reshape(1, SEQ, D)
```

```python
import math
from contextlib import ExitStack

import numpy as np

import concourse.bass as bass
from concourse import mybir

F32 = mybir.dt.float32
U32 = mybir.dt.uint32
ALU = mybir.AluOpType
ACT = mybir.ActivationFunctionType
AX = mybir.AxisListType

P = 128
D = 1024
KC = D // P
SEQ, CTX = 512, 256
TOK = SEQ + CTX
NT, NTL = TOK // P, SEQ // P
DEPTH = 2
N_MOD = 6
GW = 256
NH, DH = 4, 64
GRID_W, ROWS = 64, SEQ // 64
BASE = 64
NS = 10
UNITS = 16
EPS = 1e-6
PH, PK, TOPK = 8, 128, 16
HALVES = 2 * PH
SLOTS = PH * TOPK
RING = 8
SH1, SC1, G1, SH2, SC2, G2 = range(N_MOD)


class Signal:

    def __init__(self, sem):
        self.sem, self.n = sem, 0

    def on(self, ins, by=1):
        ins.then_inc(self.sem, by)
        self.n += by
        return self.n


def done(eng, signal, ins):
    eng.wait_ge(signal.sem, signal.on(ins))


class Machine:

    def __init__(self, nc, ctx):
        self.nc = nc
        self.stages = 0
        self.gathered = [Signal(ctx.enter_context(nc.semaphore(f"gathered{j}"))) for j in range(RING)]
        self.spent = []
        self.x = ctx.enter_context(nc.sbuf_tensor("x_stream", [P, NT, D], F32))
        self.ident = ctx.enter_context(nc.sbuf_tensor("ident", [P, P], F32))
        self.cond = ctx.enter_context(nc.sbuf_tensor("cond_silu", [P, KC, 2], F32))
        self.pick = ctx.enter_context(nc.sbuf_tensor("pick_stream", [2, 2, P], F32))
        self.iota = ctx.enter_context(nc.sbuf_tensor("iota16", [P, TOPK], F32))
        self.gate2 = ctx.enter_context(nc.sbuf_tensor("gate2_rows", [P, 2, D], F32))
        self.h = ctx.enter_context(nc.sbuf_tensor("h_tok", [P, NT, D], F32))
        self.ring = ctx.enter_context(nc.sbuf_tensor("ring", [P, RING * 2 * D], F32))
        self.seeds = ctx.enter_context(nc.sbuf_tensor("s5_seeds", [P, NS, 3, UNITS], F32))
        self.tmp = ctx.enter_context(nc.sbuf_tensor("s5_tmp", [P, 16, UNITS], F32))
        self.big = ctx.enter_context(nc.sbuf_tensor("big", [P, HALVES * TOK], F32))
        self.bank = [ctx.enter_context(nc.psum_tensor(f"bank{i}", [P, 512], F32)) for i in range(8)]


    def part(self, first, pattern, **sizes):
        n = math.prod(sizes.values())
        names = " ".join(sizes)
        return self.big[:, first:first + n].rearrange(f"p ({names}) -> p {pattern}", **sizes)


class Stage:

    def __init__(self, m, last=False):
        self.m, self.nc, self.stack, self.last = m, m.nc, ExitStack(), last
        m.stages += 1

    def __enter__(self):
        return self

    def __exit__(self, *e):
        return self.stack.__exit__(*e)

    def sem(self, name):
        sem = self.stack.enter_context(self.nc.semaphore(name))
        self.m.spent.append(sem.num)
        return Signal(sem)

    def sb(self, name, shape, dtype=F32):
        return self.stack.enter_context(self.nc.sbuf_tensor(f"{name}_{self.m.stages}", shape, dtype))

    def block(self):
        return self.stack.enter_context(self.nc.Block(no_gpsimd_drain=not self.last))


def bcast(ap, shape):
    return ap.broadcast_to(shape)


def stage_clear(m):
    with m.nc.Block(no_gpsimd_drain=True) as block:

        @block.gpsimd
        def _(pool):
            pool.sem_clear(range(min(m.spent), max(m.spent) + 1))

    m.spent.clear()


def stage_load(m, a):
    nc = m.nc
    with Stage(m) as s:
        loads, c_in, c_out = s.sem("loads_done"), s.sem("cond_loaded"), s.sem("silu_done")
        raw = s.sb("cond_raw", [P, KC, 2])
        block = s.block()

        @block.sync
        def _(sp):
            c_in.on(sp.dma_start(raw[:, :, :], a["cond"]), 16)
            loads.on(sp.dma_start(m.x[:, :NTL, :], a["x"].rearrange("(t p) d -> p t d", p=P)), 16)
            loads.on(sp.dma_start(m.x[:, NTL:, :], a["ctx"].rearrange("(t p) d -> p t d", p=P)), 16)
            loads.on(sp.dma_start(m.ident[:, :], a["ident"]), 16)
            loads.on(sp.dma_start(m.pick[:, :, :], a["pick"]), 16)
            loads.on(sp.dma_start(m.iota[:, :], a["iota"]), 16)
            sp.wait_ge(loads.sem, loads.n)

        @block.scalar
        def _(act):
            act.wait_ge(c_in.sem, 16)
            c_out.on(nc.scalar.activation(m.cond[:, :, :], raw[:, :, :], ACT.Silu))


def stage_modulation(m, a, l, rows, ht):
    nc = m.nc
    NB = N_MOD * D // 512
    W = 3
    with Stage(m) as s:
        ring = m.part(0, "w k n", w=W, k=KC, n=512)
        mod = s.sb("mod", [2, N_MOD, D])
        bias = m.h[0:2, :, :]
        gains = ht[0:2, 0:4, :].rearrange("a k t -> a (k t)")[:, 0:2 * D].rearrange("a (g d) -> a g d", g=2)
        w_in = [s.sem(f"ada_w_loaded{j}") for j in range(W)]
        small = s.sem("bias_loaded")
        mm, ev, chain, bc, cp = (s.sem(n) for n in ("mod_mm", "mod_evac", "mod_rows", "row_mm", "row_copied"))
        w = a["ada_w"][l].rearrange("(k p) n -> p k n", p=P)
        modv = mod[:, :, :].rearrange("a j d -> a (j d)")
        biasv = bias[:, :, :].rearrange("a j d -> a (j d)")
        rowv = rows[:, :, :, :].rearrange("p s j d -> p s (j d)")
        block = s.block()

        @block.sync
        def _(sp):
            for r in range(2):
                small.on(sp.dma_start(bias[r:r + 1, :, :].rearrange("a j d -> a (j d)"), a["ada_b"][l:l + 1, :]), 16)
                small.on(sp.dma_start(gains[r:r + 1, 0, :], a["norm1_g"][l:l + 1, :]), 16)
                small.on(sp.dma_start(gains[r:r + 1, 1, :], a["norm2_g"][l:l + 1, :]), 16)
            for j in range(W):
                sp.dma_start(ring[:, j, :, :], w[:, :, 512 * j:512 * (j + 1)]).then_inc(w_in[j].sem, 16)
            with sp.Fori(0, NB // W - 1) as i:
                for j in range(W):
                    sp.wait_ge(mm.sem, i * W + (j + 1))
                    sp.dma_start(ring[:, j, :, :], w[:, :, bass.ds((i + 1) * (W * 512) + 512 * j, 512)]) \
                      .then_inc(w_in[j].sem, 16)

        @block.tensor
        def _(pe):
            for b in range(NB):
                pe.wait_ge(w_in[b % W].sem, 16 * (b // W + 1))
                if b >= 4:
                    pe.wait_ge(ev.sem, b - 3)
                for k in range(KC):
                    last = nc.tensor.matmul(m.bank[b % 4][0:2, :], m.cond[:, k, :], ring[:, b % W, k, :],
                                            start=(k == 0), stop=(k == KC - 1))
                mm.on(last)
            pe.wait_ge(chain.sem, 2)
            for st in range(2):
                for b in range(NB):
                    n = st * NB + b
                    if n >= 4:
                        pe.wait_ge(cp.sem, n - 3)
                    bc.on(nc.tensor.matmul(m.bank[4 + n % 4][:, :], m.pick[:, st, :], modv[:, 512 * b:512 * b + 512],
                                           start=True, stop=True))

        @block.vector
        def _(dve):
            dve.wait_ge(small.sem, small.n)
            for b in range(NB):
                dve.wait_ge(mm.sem, b + 1)
                ev.on(nc.vector.tensor_tensor(modv[:, 512 * b:512 * b + 512], m.bank[b % 4][0:2, :],
                                              biasv[:, 512 * b:512 * b + 512], ALU.add))
            dve.wait_ge(ev.sem, NB)
            for j, g in ((SC1, 0), (SC2, 1)):
                chain.on(nc.vector.scalar_tensor_tensor(out=mod[:, j, :], in0=mod[:, j, :], scalar=1.0,
                                                        in1=gains[:, g, :], op0=ALU.add, op1=ALU.mult))

        @block.scalar
        def _(act):
            for n in range(2 * NB):
                st, b = divmod(n, NB)
                act.wait_ge(bc.sem, n + 1)
                dst = rowv[:, st, 512 * b:512 * b + 512] if b < 10 else m.gate2[:, st, 512 * (b - 10):512 * (b - 9)]
                cp.on(nc.scalar.activation(dst, m.bank[4 + n % 4][:, :], ACT.Copy))


class Norm:

    def __init__(self, s, m, rows, sc, sh, ht, tiles, banks, junk=None):
        self.m, self.rows, self.sc, self.sh, self.ht, self.tiles, self.banks = m, rows, sc, sh, ht, tiles, banks
        self.junk, self.ssq = junk or s.sb("squares", [P, D]), s.sb("ssq", [P, NT])
        self.squared, self.mean, self.root, self.h_done, self.turned, self.copied, self.scaled = (
            s.sem(n) for n in ("squares_done", "mean_done", "root_done", "h_done", "h_transposed", "hT_copied", "h_scaled"))

    def scalar(self, act):
        m, n, ssq = self.m, len(self.tiles), self.ssq
        for t in self.tiles:
            done(act, self.squared, m.nc.scalar.activation(self.junk[:, :], m.x[:, t, :], ACT.Square,
                                                           accum_out=ssq[:, t:t + 1]))
        act.wait_ge(self.mean.sem, 2)
        self.root.on(m.nc.scalar.activation(ssq[:, :n], ssq[:, :n], ACT.Sqrt))
        for i, t in enumerate(self.tiles):
            for c in range(2):
                act.wait_ge(self.turned.sem, 2 * i + c + 1)
                bank = m.bank[self.banks[(2 * i + c) % len(self.banks)]]
                self.copied.on(m.nc.scalar.activation(self.ht[:, 4 * c:4 * c + 4, t * P:(t + 1) * P],
                                                      bank[:, :].rearrange("p (k n) -> p k n", k=4), ACT.Copy))

    def vector(self, dve):
        m, n, ssq, V = self.m, len(self.tiles), self.ssq, self.m.nc.vector
        dve.wait_ge(self.squared.sem, n)
        done(dve, self.mean, V.tensor_scalar(ssq[:, :n], ssq[:, :n], 1.0 / D, EPS, ALU.mult, ALU.add))
        self.mean.on(V.reciprocal(ssq[:, :n], ssq[:, :n]))
        dve.wait_ge(self.root.sem, 1)
        for t in self.tiles:
            st = t // NTL
            done(dve, self.scaled, V.scalar_tensor_tensor(out=m.h[:, t, :], in0=m.x[:, t, :], scalar=ssq[:, t:t + 1],
                                                          in1=self.rows[:, st, self.sc, :], op0=ALU.mult, op1=ALU.mult))
            self.h_done.on(V.tensor_tensor(m.h[:, t, :], m.h[:, t, :], self.rows[:, st, self.sh, :], ALU.add))
        dve.wait_ge(self.h_done.sem, n)

    def tensor(self, pe):
        m, banks = self.m, self.banks
        for i, t in enumerate(self.tiles):
            pe.wait_ge(self.h_done.sem, i + 1)
            for c in range(2):
                u = 2 * i + c
                if u >= len(banks):
                    pe.wait_ge(self.copied.sem, u - len(banks) + 1)
                for k in range(4):
                    last = m.nc.tensor.transpose(m.bank[banks[u % len(banks)]][:, k * P:(k + 1) * P],
                                                 m.h[:, t, (4 * c + k) * P:(4 * c + k + 1) * P], m.ident[:, :])
                self.turned.on(last)
        pe.wait_ge(self.copied.sem, 2 * len(self.tiles))


class Project:

    def __init__(self, s, m, w_view, groups, ht, places, banks):
        self.m, self.w, self.groups, self.ht, self.places, self.banks = m, w_view, groups, ht, places, banks
        self.loaded = [s.sem(f"w_loaded{j}") for j in range(len(places))]
        self.used, self.multiplied, self.copied = s.sem("w_used"), s.sem("product_done"), s.sem("product_copied")
        self.u_pe = self.u_act = 0

    def outs(self, g):
        _col, dst, feat, spans = self.groups[g]
        if feat:
            return [(dst[:, b, t0:t0 + n], b, t0, n) for b in range(2) for t0, n in spans]
        return [(dst[:, t, :], None, t * P, GW) for t in spans]

    def sync(self, sp):
        W = len(self.places)
        for g, (col, *_r) in enumerate(self.groups):
            if g >= W:
                sp.wait_ge(self.used.sem, g - W + 1)
            self.loaded[g % W].on(sp.dma_start(self.places[g % W], self.w[:, :, GW * col:GW * (col + 1)]), 16)

    def tensor_group(self, pe, g):
        nc, W, NB = self.m.nc, len(self.places), len(self.banks)
        w = self.places[g % W]
        pe.wait_ge(self.loaded[g % W].sem, 16 * (g // W + 1))
        for _dst, b, t0, n in self.outs(g):
            if self.u_pe >= NB:
                pe.wait_ge(self.copied.sem, self.u_pe - NB + 1)
            bank = self.m.bank[self.banks[self.u_pe % NB]]
            for k in range(KC):
                lhs, rhs = (self.ht[:, k, t0:t0 + P], w[:, k, :]) if b is None \
                    else (w[:, k, b * P:(b + 1) * P], self.ht[:, k, t0:t0 + n])
                last = nc.tensor.matmul(bank[:, :n], lhs, rhs, start=(k == 0), stop=(k == KC - 1))
            self.multiplied.on(last)
            self.u_pe += 1
        pe.wait_ge(self.multiplied.sem, self.u_pe)
        self.used.on(pe.nop())

    def scalar_group(self, act, g):
        for dst, _b, _t0, n in self.outs(g):
            act.wait_ge(self.multiplied.sem, self.u_act + 1)
            bank = self.m.bank[self.banks[self.u_act % len(self.banks)]]
            self.copied.on(self.m.nc.scalar.activation(dst, bank[:, :n], ACT.Copy))
            self.u_act += 1


def stage_inputs(m, a, l, rows, groups, w_view, ht, seeds, tmp, wide, lc, base):
    nc = m.nc
    with Stage(m) as s:
        norm = Norm(s, m, rows, SC1, SH1, ht, list(range(NT)), (0, 1, 2, 3))
        w = s.sb("w_ring", [P, 2, KC, GW])
        proj = Project(s, m, w_view, groups, ht, [w[:, j, :, :] for j in range(2)], (4, 5, 6, 7))
        s5 = S5Weights(s, m, a, l, seeds, tmp, wide, lc, base)
        block = s.block()

        @block.sync
        def _(sp):
            s5.sync(sp)
            proj.sync(sp)

        @block.scalar
        def _(act):
            norm.scalar(act)
            for g in range(len(groups)):
                proj.scalar_group(act, g)

        @block.vector
        def _(dve):
            norm.vector(dve)
            s5.vector(dve)

        @block.tensor
        def _(pe):
            norm.tensor(pe)
            for g in range(len(groups)):
                proj.tensor_group(pe, g)


def stage_attention(m, a, l, qt, kt, v, y, tiles, ht):
    nc = m.nc
    scale = DH ** -0.5
    with Stage(m) as s:
        bias = s.sb("pos_bias", [P, NH, 16, GRID_W])
        falling = ht[:, 0:6, :].rearrange("p k t -> p (k t)")[:, 0:NH * 16 * GRID_W] \
            .rearrange("p (h j c) -> p h j c", h=NH, j=16)
        flip = s.sb("flip", [P, P])
        mask = s.sb("col_mask", [P, GRID_W])
        sc = s.sb("scores", [P, 2, TOK])
        pt = s.sb("probs_T", [P, 2, TOK])
        st = s.sb("softmax_stats", [P, 2, 4])
        loads, biased, turned = s.sem("bias_loaded"), s.sem("bias_masked"), s.sem("bias_turned")
        sm, tp, om = s.sem("scores_mm"), s.sem("probs_transposed"), s.sem("out_mm")
        sb_, mx, od = s.sem("scores_biased"), s.sem("max_done"), s.sem("out_done")
        ex, pc = s.sem("exp_done"), s.sem("probsT_copied")
        todo = [(t, h) for t in tiles for h in range(NH)]
        pad, rows = 2 * GRID_W - 1, 17
        block = s.block()

        def keys(t):
            return (0, TOK) if t < NTL else (SEQ, CTX)

        @block.sync
        def _(sp):
            loads.on(sp.dma_start(mask[:, :], a["col_mask"]), 16)
            loads.on(sp.dma_start(flip[:, :], a["flip"]), 16)
            for h in range(NH):
                for half in range(2):
                    src = bass.AP(tensor=a["rpb"].tensor,
                                  offset=((l * NH + h) * rows + 1 - half) * pad,
                                  ap=[[1, GRID_W], [pad, 16], [1, GRID_W]])
                    loads.on(sp.dma_start(falling[64 * half:64 * half + 64, h, :, :], src), 16)

        @block.vector
        def _(dve):
            dve.wait_ge(loads.sem, loads.n)
            for b in range(2 * NH):
                h, j = b // 2, 8 * (b % 2)
                dve.wait_ge(turned.sem, b + 1)
                biased.on(nc.vector.tensor_tensor(bias[:, h, j:j + 8, :],
                                                  m.bank[b][:, :].rearrange("p (j c) -> p j c", j=8),
                                                  bcast(mask[:, :].unsqueeze(1), [P, 8, GRID_W]), ALU.add))
            dve.wait_ge(biased.sem, 2 * NH)

            def finish(i):
                t, h = todo[i]
                dve.wait_ge(om.sem, i + 1)
                done(dve, od, nc.vector.reciprocal(st[:, i % 2, 2:3], st[:, i % 2, 1:2]))
                od.on(nc.vector.tensor_scalar(y[:, t, h * DH:(h + 1) * DH], m.bank[6 + i % 2][:, 0:DH],
                                              st[:, i % 2, 2:3], None, ALU.mult))

            for i, (t, h) in enumerate(todo):
                dve.wait_ge(sm.sem, i + 1)
                if i >= 2:
                    finish(i - 2)
                k0, n = keys(t)
                if t < NTL:
                    j0 = 7 - 2 * t
                    sb_.on(nc.vector.scalar_tensor_tensor(
                        out=sc[:, i % 2, 0:SEQ], in0=m.bank[i % 2][:, :], scalar=scale,
                        in1=bias[:, h, :, :].rearrange("p j c -> p (j c)")[:, (j0) * GRID_W:(j0 + 8) * GRID_W],
                        op0=ALU.mult, op1=ALU.add))
                sb_.on(nc.vector.tensor_scalar(sc[:, i % 2, SEQ:TOK], m.bank[2 + i % 2][:, 0:CTX], scale, None, ALU.mult))
                dve.wait_ge(sb_.sem, sb_.n)
                mx.on(nc.vector.tensor_reduce(out=st[:, i % 2, 0:1], in_=sc[:, i % 2, k0:TOK], axis=AX.X,
                                              op=ALU.max, negate=True))
            for i in (len(todo) - 2, len(todo) - 1):
                finish(i)

        @block.scalar
        def _(act):
            def copy_t(i):
                t, _h = todo[i]
                act.wait_ge(tp.sem, i + 1)
                if t < NTL:
                    nc.scalar.activation(pt[:, i % 2, 0:SEQ], m.bank[4][:, :], ACT.Copy)
                pc.on(nc.scalar.activation(pt[:, i % 2, SEQ:TOK], m.bank[5][:, 0:CTX], ACT.Copy))

            for i, (t, h) in enumerate(todo):
                k0, n = keys(t)
                act.wait_ge(mx.sem, i + 1)
                if i >= 2:
                    act.wait_ge(od.sem, 2 * (i - 1))
                ex.on(nc.scalar.activation(sc[:, i % 2, k0:TOK], sc[:, i % 2, k0:TOK], ACT.Exp,
                                           bias=st[:, i % 2, 0:1], accum_out=st[:, i % 2, 1:2]))
                if i >= 1:
                    copy_t(i - 1)
            copy_t(len(todo) - 1)

        @block.tensor
        def _(pe):
            def scores(i):
                t, h = todo[i]
                r = slice(DH * (h % 2), DH * (h % 2) + DH)
                if i >= 2:
                    pe.wait_ge(mx.sem, i - 1)
                q = qt[r, h // 2, t * P:(t + 1) * P]
                if t < NTL:
                    nc.tensor.matmul(m.bank[i % 2][:, :], q, kt[r, h // 2, 0:SEQ], start=True, stop=True)
                sm.on(nc.tensor.matmul(m.bank[2 + i % 2][:, 0:CTX], q, kt[r, h // 2, SEQ:TOK], start=True, stop=True))

            def weighted(i):
                t, h = todo[i]
                tiles_k = range(NT) if t < NTL else range(NTL, NT)
                pe.wait_ge(pc.sem, i + 1)
                if i >= 2:
                    pe.wait_ge(od.sem, 2 * (i - 1))
                for n, kt_ in enumerate(tiles_k):
                    last = nc.tensor.matmul(m.bank[6 + i % 2][:, 0:DH], pt[:, i % 2, kt_ * P:(kt_ + 1) * P],
                                            v[:, kt_, h * DH:(h + 1) * DH], start=(n == 0), stop=(n == len(tiles_k) - 1))
                om.on(last)

            pe.wait_ge(loads.sem, loads.n)
            for b in range(2 * NH):
                h, j = b // 2, 8 * (b % 2)
                turned.on(nc.tensor.matmul(m.bank[b][:, :], flip[:, :],
                                           falling[:, h, j:j + 8, :].rearrange("p j c -> p (j c)"),
                                           start=True, stop=True))
            pe.wait_ge(biased.sem, 2 * NH)
            scores(0)
            for i, (t, h) in enumerate(todo):
                if i + 1 < len(todo):
                    scores(i + 1)
                pe.wait_ge(ex.sem, i + 1)
                if i >= 1:
                    pe.wait_ge(pc.sem, i)
                for kt_ in range(0 if t < NTL else NTL, NT):
                    dst = m.bank[4][:, kt_ * P:(kt_ + 1) * P] if kt_ < NTL else m.bank[5][:, (kt_ - NTL) * P:(kt_ - NTL + 1) * P]
                    last = nc.tensor.transpose(dst, sc[:, i % 2, kt_ * P:(kt_ + 1) * P], m.ident[:, :])
                tp.on(last)
                if i >= 1:
                    weighted(i - 1)
            weighted(len(todo) - 1)


def spans_of(tiles):
    return [(0, 0, SEQ)] + ([(1, SEQ, CTX)] if len(tiles) > NTL else [])


def stage_conv(m, a, l, cb, cc, cx, y, tiles):
    nc = m.nc
    with Stage(m) as s:
        z = s.sb("conv_z", [P, 2, TOK + 4])
        w = s.sb("conv_w", [P, 2, 3])
        loads, ch, fin = s.sem("conv_w_loaded"), s.sem("conv_chain"), s.sem("conv_done")
        tp, cp = s.sem("conv_transposed"), s.sem("conv_copied")
        spans = spans_of(tiles)
        block = s.block()

        @block.sync
        def _(sp):
            loads.on(sp.dma_start(w[:, :, :], a["conv_w"][l]), 16)

        @block.vector
        def _(dve):
            for n in range(2):
                ch.on(nc.vector.memset(z[:, n, :], 0.0))
            dve.wait_ge(ch.sem, ch.n)
            dve.wait_ge(loads.sem, 16)
            for f in range(2):
                for st, t0, n in spans:
                    z0 = t0 + 1 + 2 * st
                    t = slice(t0, t0 + n)
                    done(dve, ch, nc.vector.tensor_tensor(z[:, f, z0:z0 + n], cc[:, f, t], cx[:, f, t], ALU.mult))
                    done(dve, ch, nc.vector.tensor_scalar(cx[:, f, t], z[:, f, z0 - 1:z0 - 1 + n], w[:, f, 0:1], None, ALU.mult))
                    for j in (1, 2):
                        done(dve, ch, nc.vector.scalar_tensor_tensor(out=cx[:, f, t], in0=z[:, f, z0 - 1 + j:z0 - 1 + j + n],
                                                                     scalar=w[:, f, j:j + 1], in1=cx[:, f, t],
                                                                     op0=ALU.mult, op1=ALU.add))
                    fin.on(nc.vector.tensor_tensor(cx[:, f, t], cx[:, f, t], cb[:, f, t], ALU.mult))

        @block.tensor
        def _(pe):
            pe.wait_ge(fin.sem, 2 * len(spans))
            for i, t in enumerate(tiles):
                for f in range(2):
                    last = nc.tensor.transpose(m.bank[i][:, f * P:(f + 1) * P], cx[:, f, t * P:(t + 1) * P], m.ident[:, :])
                tp.on(last)

        @block.scalar
        def _(act):
            for i, t in enumerate(tiles):
                act.wait_ge(tp.sem, i + 1)
                cp.on(nc.scalar.activation(y[:, t, GW:2 * GW], m.bank[i][:, 0:GW], ACT.Copy))


def stage_fourier(m, a, fz, y, tiles):
    nc = m.nc
    with Stage(m) as s:
        tab = [s.sb("dft_lat", [P, NTL, 2, SEQ]), s.sb("dft_ctx", [P, NT - NTL, 2, CTX])]
        ch = s.sb("dft_channels", [P, 2, P])
        pf = s.sb("dft_positions", [P, 2, 2, TOK])
        loads, mm, cp, om, oc = (s.sem(n) for n in ("dft_loaded", "pos_mm", "pos_copied", "chan_mm", "four_copied"))
        spans = spans_of(tiles)
        block = s.block()
        first = [(st, t0, n, f, c) for st, t0, n in spans for f in range(2) for c in range(2)]

        @block.sync
        def _(sp):
            loads.on(sp.dma_start(ch[:, :, :], a["dft_chan"]), 16)
            loads.on(sp.dma_start(tab[0][:, :, :, :], a["dft_lat"]), 16)
            if len(spans) > 1:
                loads.on(sp.dma_start(tab[1][:, :, :, :], a["dft_ctx"]), 16)

        @block.tensor
        def _(pe):
            pe.wait_ge(loads.sem, loads.n)
            for i, (st, t0, n, f, c) in enumerate(first):
                if i >= 4:
                    pe.wait_ge(cp.sem, i - 3)
                for lt in range(n // P):
                    last = nc.tensor.matmul(m.bank[i % 4][:, :n], fz[:, t0 // P + lt, f * P:(f + 1) * P],
                                            tab[st][:, lt, c, :], start=(lt == 0), stop=(lt == n // P - 1))
                mm.on(last)
            pe.wait_ge(cp.sem, len(first))
            for i, t in enumerate(tiles):
                if i >= 4:
                    pe.wait_ge(oc.sem, i - 3)
                for f in range(2):
                    for c in range(2):
                        last = nc.tensor.matmul(m.bank[4 + i % 4][:, f * P:(f + 1) * P], pf[:, f, c, t * P:(t + 1) * P],
                                                ch[:, c, :], start=(c == 0), stop=(c == 1))
                om.on(last)

        @block.scalar
        def _(act):
            for i, (st, t0, n, f, c) in enumerate(first):
                act.wait_ge(mm.sem, i + 1)
                cp.on(nc.scalar.activation(pf[:, f, c, t0:t0 + n], m.bank[i % 4][:, :n], ACT.Copy))
            for i, t in enumerate(tiles):
                act.wait_ge(om.sem, i + 1)
                oc.on(nc.scalar.activation(y[:, t, 2 * GW:3 * GW], m.bank[4 + i % 4][:, 0:GW], ACT.Copy))


def reversed_columns(ap3, f, n):
    v = ap3[:, f, n - 1:n]
    return bass.AP(tensor=v.tensor, offset=v.offset, ap=[v.ap[0], [-1, n]])


class S5Weights:

    def __init__(self, s, m, a, l, seeds, tmp, wide, lc, base):
        self.m, self.a, self.l = m, a, l
        self.seeds, self.tmp, self.wide, self.lc, self.base = seeds, tmp, wide, lc, base
        self.pr = s.sb("s5_params", [P, 3, UNITS])
        self.bw = s.sb("s5_b", [P, 2, UNITS, 16])
        self.cw = s.sb("s5_c", [P, 2, UNITS, 16])
        self.bb = s.sb("s5_b_bar", [P, 3, UNITS, 16])
        self.bt = s.sb("base_tmp", [P, 2, UNITS, BASE // 2])
        self.loads, self.chain, self.placed = s.sem("s5_loaded"), s.sem("s5_chain"), s.sem("s5_placed")

    def sync(self, sp):
        a, l = self.a, self.l
        self.loads.on(sp.dma_start(self.pr[:, :, :], a["s5_params"][l]), 16)
        self.loads.on(sp.dma_start(self.bw[:, :, :, :], a["s5_b"][l]), 16)
        self.loads.on(sp.dma_start(self.cw[:, :, :, :], a["s5_c"][l]), 16)

    def vector(self, dve):
        V = self.m.nc.vector
        ch, wd, loads, K = self.chain, self.placed, self.loads, 10
        pr, bw, cw, bb, tmp, seeds, wide, lc, base, bt = (self.pr, self.bw, self.cw, self.bb, self.tmp, self.seeds,
                                                        self.wide, self.lc, self.base, self.bt)
        T = lambda i: tmp[:, i, :]

        def tt(o, x, z, op):
            done(dve, ch, V.tensor_tensor(o, x, z, op))

        def ts(o, x, s1, op0, s2=None, op1=None):
            done(dve, ch, V.tensor_scalar(o, x, s1, s2, op0, op1) if op1 else V.tensor_scalar(o, x, s1, None, op0))

        def stt(o, x, c, z, op0, op1):
            done(dve, ch, V.scalar_tensor_tensor(out=o, in0=x, scalar=c, in1=z, op0=op0, op1=op1))

        def real_expm1(o, x):
            ts(x, x, 2.0 ** -K, ALU.mult)
            ts(o, x, 1.0 / 4, ALU.mult, 1.0, ALU.add)
            for c in (3, 2):
                tt(o, o, x, ALU.mult)
                ts(o, o, 1.0 / c, ALU.mult, 1.0, ALU.add)
            tt(o, o, x, ALU.mult)
            for _ in range(K):
                stt(o, o, 2.0, o, ALU.add, ALU.mult)

        ch.on(V.memset(wide, 0.0))
        ch.on(V.memset(lc, 0.0))
        dve.wait_ge(loads.sem, loads.n)
        dve.wait_ge(ch.sem, ch.n)
        a_re, a_im, log_dt = pr[:, 0, :], pr[:, 1, :], pr[:, 2, :]
        dt, x, th, mr, mi, er, w2 = (T(i) for i in range(7))
        ts(x, log_dt, -1.0, ALU.mult)
        real_expm1(dt, x)
        ts(dt, dt, 1.0, ALU.add)
        done(dve, ch, V.reciprocal(dt, dt))
        tt(x, a_re, dt, ALU.mult)
        real_expm1(er, x)
        tt(th, a_im, dt, ALU.mult)
        ts(th, th, 2.0 ** -K, ALU.mult)
        tt(w2, th, th, ALU.mult)
        ts(mr, w2, -1.0 / 30, ALU.mult, 1.0, ALU.add)
        tt(mr, mr, w2, ALU.mult)
        ts(mr, mr, -1.0 / 12, ALU.mult, 1.0, ALU.add)
        tt(mr, mr, w2, ALU.mult)
        ts(mr, mr, -0.5, ALU.mult)
        ts(mi, w2, -1.0 / 20, ALU.mult, 1.0, ALU.add)
        tt(mi, mi, w2, ALU.mult)
        ts(mi, mi, -1.0 / 6, ALU.mult, 1.0, ALU.add)
        tt(mi, mi, th, ALU.mult)
        for _ in range(K):
            tt(w2, mi, mi, ALU.mult)
            stt(mi, mr, 1.0, mi, ALU.add, ALU.mult)
            ts(mi, mi, 2.0, ALU.mult)
            stt(mr, mr, 2.0, mr, ALU.add, ALU.mult)
            tt(mr, mr, w2, ALU.subtract)
        nr, ni, den, fr, fi, t1 = (T(i) for i in range(7, 13))
        stt(nr, er, 1.0, mr, ALU.add, ALU.mult)
        tt(nr, nr, er, ALU.add)
        stt(ni, er, 1.0, mi, ALU.add, ALU.mult)
        tt(den, a_re, a_re, ALU.mult)
        tt(t1, a_im, a_im, ALU.mult)
        tt(den, den, t1, ALU.add)
        done(dve, ch, V.reciprocal(den, den))
        tt(fr, nr, a_re, ALU.mult)
        tt(t1, ni, a_im, ALU.mult)
        tt(fr, fr, t1, ALU.add)
        tt(fr, fr, den, ALU.mult)
        tt(fi, ni, a_re, ALU.mult)
        tt(t1, nr, a_im, ALU.mult)
        tt(fi, fi, t1, ALU.subtract)
        tt(fi, fi, den, ALU.mult)
        wide_f = lambda f: bcast(f.unsqueeze(2), [P, UNITS, 16])
        for o, f0, f1, op in ((0, fr, fi, ALU.subtract), (1, fi, fr, ALU.add)):
            tt(bb[:, o, :, :], bw[:, 0, :, :], wide_f(f0), ALU.mult)
            tt(bb[:, 2, :, :], bw[:, 1, :, :], wide_f(f1), ALU.mult)
            tt(bb[:, o, :, :], bb[:, o, :, :], bb[:, 2, :, :], op)
        for un in range(UNITS):
            d, f, j = un // 8, (un % 8) // 4, un % 4
            for half in range(2):
                r, c0 = slice(64 * half, 64 * half + 64), 16 * half
                wd.on(V.tensor_copy(wide[r, d, f, :, j, c0:c0 + 16], bb[r, 0:2, un, :]))
                wd.on(V.tensor_copy(lc[r, 0, un, c0:c0 + 16], cw[r, 0, un, :]))
                wd.on(V.tensor_scalar(lc[r, 1, un, c0:c0 + 16], cw[r, 1, un, :], -1.0, None, ALU.mult))
        ts(seeds[:, 0, 0, :], mr, 1.0, ALU.add)
        ts(seeds[:, 0, 1, :], mi, 1.0, ALU.mult)
        for j in range(NS):
            cr, ci = seeds[:, j, 0, :], seeds[:, j, 1, :]
            if j:
                pr_, pi_ = seeds[:, j - 1, 0, :], seeds[:, j - 1, 1, :]
                tt(cr, pr_, pr_, ALU.mult)
                tt(t1, pi_, pi_, ALU.mult)
                tt(cr, cr, t1, ALU.subtract)
                stt(ci, pr_, 2.0, pi_, ALU.mult, ALU.mult)
            tt(x, cr, cr, ALU.mult)
            tt(t1, ci, ci, ALU.mult)
            tt(x, x, t1, ALU.add)
            ts(x, x, -0.5, ALU.mult, 1.5, ALU.add)
            tt(cr, cr, x, ALU.mult)
            tt(ci, ci, x, ALU.mult)
            ts(seeds[:, j, 2, :], ci, -1.0, ALU.mult)
        ts(er, er, 1.0, ALU.add)
        done(dve, ch, V.memset(base[:, 0, :, 0:1], 1.0))
        done(dve, ch, V.memset(base[:, 1, :, 0:1], 0.0))
        n, j = 1, 0
        while n < BASE:
            c0, s0 = base[:, 0, :, 0:n], base[:, 1, :, 0:n]
            E = [bcast(seeds[:, j, q, :].unsqueeze(2), [P, UNITS, n]) for q in range(2)]
            t0, t1 = bt[:, 0, :, 0:n], bt[:, 1, :, 0:n]
            for o, e0, e1, op in ((0, 0, 1, ALU.subtract), (1, 1, 0, ALU.add)):
                tt(t0, c0, E[e0], ALU.mult)
                tt(t1, s0, E[e1], ALU.mult)
                tt(base[:, o, :, n:2 * n], t0, t1, op)
            n, j = 2 * n, j + 1


def stage_s5(m, a, l, u, y, tiles, seeds, radius, wide, lc, base, ht):
    nc = m.nc
    order = [d * 8 + 4 * f + j for f in range(2) for d in range(2) for j in range(4)]
    with Stage(m) as s:
        tab = ht[:, 0:4, :].rearrange("p (a c) t -> p a c t", a=2)
        bu = ht[:, 4:8, :].rearrange("p (a c) t -> p a c t", a=2)
        wr, g_, pr = (m.part(i, "q t", q=q, t=TOK) for i, q in ((0, 2), (2 * TOK, 2), (4 * TOK, 4)))
        yf = m.part(8 * TOK, "f t", f=2, t=TOK)
        gl, sg = (m.part(10 * TOK + i * 2 * GW, "f n", f=2, n=GW) for i in (0, 1))
        lb = s.sb("s5_b_lhsT", [P, 8, P])
        dsk = s.sb("s5_d", [P, 2])
        tt_ = s.sb("table_tmp", [P, 2, 256])
        loads, tp, lbc, tb, bm, be, ch, pd, ym, tch = (s.sem(n) for n in (
            "s5w_loaded", "b_transposed", "b_copied", "table_done", "drive_mm", "drive_copied", "scan_chain",
            "products_done", "readout_done", "table_chain"))
        sk, ge, gm, gt, si, go = (s.sem(n) for n in ("skip_added", "gelu_done", "glu_mm", "gelu_T", "sigmoid_done",
                                                     "glu_done"))
        drive = [[m.bank[3 * i + j] for j in range(3)] for i in range(2)]
        read_lat, read_ctx = m.bank[6], m.bank[7]
        block = s.block()

        @block.sync
        def _(sp):
            loads.on(sp.dma_start(dsk[:, :], a["s5_d"][l]), 16)
            loads.on(sp.dma_start(gl, a["s5_w_glu"][l].rearrange("(f p) n -> p f n", p=P)), 16)

        @block.gpsimd
        def _(pool):
            G = nc.gpsimd
            for i, un in enumerate(order):
                c, sn = tab[:, i % 2, 0, :], tab[:, i % 2, 1, :]
                if i >= 2:
                    pool.wait_ge(pd.sem, 4 * (i - 1))
                tch.on(G.tensor_copy(c[:, 0:BASE], base[:, 0, un, :]))
                done(pool, tch, G.tensor_copy(sn[:, 0:BASE], base[:, 1, un, :]))
                n, j = BASE, BASE.bit_length() - 1
                while n < TOK:
                    w = min(n, TOK - n)
                    E = [seeds[:, j, q, un:un + 1] for q in range(3)]
                    for out, a0, e0, a1, e1 in ((c, c, 0, sn, 2), (sn, c, 1, sn, 0)):
                        tch.on(G.tensor_scalar(tt_[:, 0, :w], a0[:, 0:w], E[e0], 1.0, ALU.mult, ALU.mult))
                        done(pool, tch, G.tensor_scalar(tt_[:, 1, :w], a1[:, 0:w], E[e1], 1.0, ALU.mult, ALU.mult))
                        last = G.tensor_tensor(out[:, n:n + w], tt_[:, 0, :w], tt_[:, 1, :w], ALU.add)
                        if n + w < TOK or out is c:
                            done(pool, tch, last)
                    n, j = n + w, j + 1
                tb.on(last)

        @block.tensor
        def _(pe):
            for d in range(2):
                for f in range(2):
                    for c in range(2):
                        k = 4 * d + 2 * f + c
                        last = nc.tensor.transpose(m.bank[k // 4][:, (k % 4) * P:(k % 4 + 1) * P],
                                                   wide[:, d, f, c, :, :].rearrange("p j h -> p (j h)"), m.ident[:, :])
                tp.on(last)
            pe.wait_ge(lbc.sem, 2)

            def drives(i):
                un = order[i]
                d, f, j = un // 8, (un % 8) // 4, un % 4
                q = slice(32 * j, 32 * j + 32)
                if i >= 2:
                    pe.wait_ge(be.sem, i - 1)
                if d == 0:
                    cx_, lt = u[q, f, SEQ:TOK], u[q, f, 0:SEQ]
                else:
                    cx_ = bass.AP(tensor=u.tensor, offset=u[q, f, TOK - 1:TOK].offset, ap=[u[q, f, 0:1].ap[0], [-1, CTX]])
                    lt = bass.AP(tensor=u.tensor, offset=u[q, f, SEQ - 1:SEQ].offset, ap=[u[q, f, 0:1].ap[0], [-1, SEQ]])
                D_ = drive[i % 2]
                for c in range(2):
                    lhs = lb[q, 4 * d + 2 * f + c, :]
                    nc.tensor.matmul(D_[2][:, c * CTX:(c + 1) * CTX], lhs, cx_, start=True, stop=True)
                    last = nc.tensor.matmul(D_[c][:, :], lhs, lt, start=True, stop=True)
                bm.on(last)

            def readout(i):
                un = order[i]
                d, j = un // 8, un % 4
                o = slice(32 * j, 32 * j + 32)
                lat, cx_ = ((CTX, 0), (0, SEQ))[d]
                if i == 8:
                    pe.wait_ge(sk.sem, 2)
                for q in range(4):
                    pe.wait_ge(pd.sem, 4 * i + q + 1)
                    lhs = lc[:, 0 if q < 2 else 1, un, :]
                    first, last_ = d == 0 and q == 0, d == 1 and q == 3
                    nc.tensor.matmul(read_lat[o, :], lhs, pr[:, q, lat:lat + SEQ], start=first, stop=last_)
                    last = nc.tensor.matmul(read_ctx[o, 0:CTX], lhs, pr[:, q, cx_:cx_ + CTX], start=first, stop=last_)
                ym.on(last)

            drives(0)
            for i in range(UNITS):
                if i + 1 < UNITS:
                    drives(i + 1)
                readout(i)
            pe.wait_ge(ge.sem, 2)
            pe.wait_ge(loads.sem, loads.n)
            for i, t in enumerate(tiles):
                if i >= 2:
                    pe.wait_ge(go.sem, i - 1)
                for f in range(2):
                    last = nc.tensor.matmul(m.bank[i % 2][:, 0:GW], pr[:, f, t * P:(t + 1) * P], gl[:, f, :],
                                            start=(f == 0), stop=(f == 1))
                gm.on(last)
                for f in range(2):
                    last = nc.tensor.transpose(m.bank[2 + i % 2][:, f * P:(f + 1) * P], pr[:, f, t * P:(t + 1) * P],
                                               m.ident[:, :])
                gt.on(last)

        @block.scalar
        def _(act):
            for k in range(2):
                act.wait_ge(tp.sem, k + 1)
                lbc.on(act.activation(lb[:, 4 * k:4 * k + 4, :], m.bank[k][:, :].rearrange("p (b n) -> p b n", b=4), ACT.Copy))
            for i in range(UNITS):
                act.wait_ge(bm.sem, i + 1)
                if i >= 2:
                    act.wait_ge(ch.sem, 8 * (i - 2) + 4)
                for c in range(2):
                    act.activation(bu[:, i % 2, c, 0:CTX], drive[i % 2][2][:, c * CTX:(c + 1) * CTX], ACT.Copy)
                    last = act.activation(bu[:, i % 2, c, CTX:TOK], drive[i % 2][c][:, :], ACT.Copy)
                be.on(last)
            act.wait_ge(ym.sem, UNITS)
            for f in range(2):
                act.wait_ge(sk.sem, 2 * (f + 1))
                ge.on(nc.scalar.activation(pr[:, f, :], yf[:, f, :], ACT.Gelu_apprx_tanh))
            for i, t in enumerate(tiles):
                act.wait_ge(gm.sem, i + 1)
                if i >= 2:
                    act.wait_ge(go.sem, i - 1)
                si.on(nc.scalar.activation(sg[:, i % 2, :], m.bank[i % 2][:, 0:GW], ACT.Sigmoid))

        @block.vector
        def _(dve):
            V = nc.vector
            dve.wait_ge(loads.sem, loads.n)
            for i, un in enumerate(order):
                c, sn = tab[:, i % 2, 0, :], tab[:, i % 2, 1, :]
                b = bu[:, i % 2, :, :]
                dve.wait_ge(be.sem, i + 1)
                dve.wait_ge(tb.sem, i + 1)
                if i:
                    dve.wait_ge(pd.sem, 4 * i)
                ch.on(V.tensor_tensor(wr[:, 0, :], b[:, 0, :], c, ALU.mult))
                ch.on(V.tensor_tensor(g_[:, 0, :], b[:, 1, :], sn, ALU.mult))
                ch.on(V.tensor_tensor(wr[:, 1, :], b[:, 1, :], c, ALU.mult))
                done(dve, ch, V.tensor_tensor(g_[:, 1, :], b[:, 0, :], sn, ALU.mult))
                ch.on(V.tensor_tensor(wr[:, 0, :], wr[:, 0, :], g_[:, 0, :], ALU.add))
                done(dve, ch, V.tensor_tensor(wr[:, 1, :], wr[:, 1, :], g_[:, 1, :], ALU.subtract))
                r = bcast(radius[:, un:un + 1], [P, TOK])
                for q in range(2):
                    ch.on(V.tensor_tensor_scan(out=g_[:, q, :], data0=r, data1=wr[:, q, :], initial=0.0,
                                               op0=ALU.mult, op1=ALU.add))
                dve.wait_ge(ch.sem, ch.n)
                if i:
                    dve.wait_ge(ym.sem, i)
                out = [pr[:, q, :] if un < 8 else reversed_columns(pr, q, TOK) for q in range(4)]
                pd.on(V.tensor_tensor(out[0], g_[:, 0, :], c, ALU.mult))
                pd.on(V.scalar_tensor_tensor(out=out[1], in0=g_[:, 1, :], scalar=-1.0, in1=sn, op0=ALU.mult, op1=ALU.mult))
                pd.on(V.tensor_tensor(out[2], g_[:, 0, :], sn, ALU.mult))
                pd.on(V.tensor_tensor(out[3], g_[:, 1, :], c, ALU.mult))
                if i in (7, 15):
                    f = i // 8
                    dve.wait_ge(ym.sem, i + 1)
                    sk.on(V.scalar_tensor_tensor(out=yf[:, f, 0:SEQ], in0=u[:, f, 0:SEQ], scalar=dsk[:, f:f + 1],
                                                 in1=read_lat[:, :], op0=ALU.mult, op1=ALU.add))
                    sk.on(V.scalar_tensor_tensor(out=yf[:, f, SEQ:TOK], in0=u[:, f, SEQ:TOK], scalar=dsk[:, f:f + 1],
                                                 in1=read_ctx[:, 0:CTX], op0=ALU.mult, op1=ALU.add))
            for i, t in enumerate(tiles):
                dve.wait_ge(si.sem, i + 1)
                dve.wait_ge(gt.sem, i + 1)
                go.on(V.tensor_tensor(y[:, t, 3 * GW:4 * GW], m.bank[2 + i % 2][:, 0:GW], sg[:, i % 2, :], ALU.mult))


def stage_merge(m, a, l, rows, y, yt, tiles):
    nc = m.nc
    n = len(tiles)
    with Stage(m) as s:
        w = m.part(0, "k d", k=KC, d=D)
        gg = s.sb("group_gains", [P, D])
        junk, ssq = s.sb("g_squares", [P, GW]), s.sb("g_ssq", [P, NT, 4])
        prod = s.sb("gated", [P, D])
        w_in, g_in = s.sem("w_out_loaded"), s.sem("gains_loaded")
        sq, ms, rt, yn, tp, ev, mm, add = (s.sem(x) for x in ("g_squares_done", "g_mean", "g_root", "y_normed",
                                                              "y_transposed", "y_copied", "out_mm", "x_added"))
        block = s.block()

        @block.sync
        def _(sp):
            g_in.on(sp.dma_start(gg[:, :], a["grp_g"][l:l + 1, :].broadcast_to([P, D])), 16)
            w_in.on(sp.dma_start(w[:, :, :], a["w_out"][l].rearrange("(k p) n -> p k n", p=P)), 16)

        @block.scalar
        def _(act):
            for t in tiles:
                for g in range(4):
                    done(act, sq, nc.scalar.activation(junk[:, :], y[:, t, g * GW:(g + 1) * GW], ACT.Square,
                                                       accum_out=ssq[:, t, g:g + 1]))
            act.wait_ge(ms.sem, 2)
            rt.on(nc.scalar.activation(ssq[:, :n, :], ssq[:, :n, :], ACT.Sqrt))
            for i, t in enumerate(tiles):
                for c in range(2):
                    act.wait_ge(tp.sem, 2 * i + c + 1)
                    ev.on(nc.scalar.activation(yt[:, 4 * c:4 * c + 4, t * P:(t + 1) * P],
                                               m.bank[(2 * i + c) % 4][:, :].rearrange("p (k n) -> p k n", k=4),
                                               ACT.Copy))

        @block.vector
        def _(dve):
            V = nc.vector
            dve.wait_ge(sq.sem, 4 * n)
            done(dve, ms, V.tensor_scalar(ssq[:, :n, :], ssq[:, :n, :], 1.0 / GW, EPS, ALU.mult, ALU.add))
            ms.on(V.reciprocal(ssq[:, :n, :], ssq[:, :n, :]))
            dve.wait_ge(rt.sem, 1)
            dve.wait_ge(g_in.sem, 16)
            for t in tiles:
                for g in range(4):
                    c = slice(g * GW, (g + 1) * GW)
                    yn.on(V.scalar_tensor_tensor(out=y[:, t, c], in0=y[:, t, c], scalar=ssq[:, t, g:g + 1],
                                                 in1=gg[:, c], op0=ALU.mult, op1=ALU.mult))
            for i, t in enumerate(tiles):
                for c in range(2):
                    dve.wait_ge(mm.sem, 2 * i + c + 1)
                    cols = slice(512 * c, 512 * c + 512)
                    done(dve, add, V.tensor_tensor(prod[:, cols], m.bank[4 + (2 * i + c) % 4][:, :],
                                                   rows[:, t // NTL, G1, cols], ALU.mult))
                    add.on(V.tensor_tensor(m.x[:, t, cols], m.x[:, t, cols], prod[:, cols], ALU.add))

        @block.tensor
        def _(pe):
            for i, t in enumerate(tiles):
                pe.wait_ge(yn.sem, 4 * (i + 1))
                for c in range(2):
                    u = 2 * i + c
                    if u >= 4:
                        pe.wait_ge(ev.sem, u - 3)
                    for k in range(4):
                        last = nc.tensor.transpose(m.bank[u % 4][:, k * P:(k + 1) * P],
                                                   y[:, t, (4 * c + k) * P:(4 * c + k + 1) * P], m.ident[:, :])
                    tp.on(last)
            pe.wait_ge(w_in.sem, 16)
            for i, t in enumerate(tiles):
                pe.wait_ge(ev.sem, 2 * (i + 1))
                for c in range(2):
                    u = 2 * i + c
                    if u >= 4:
                        pe.wait_ge(add.sem, 2 * (u - 3))
                    for k in range(KC):
                        last = nc.tensor.matmul(m.bank[4 + u % 4][:, :], yt[:, k, t * P:(t + 1) * P],
                                                w[:, k, 512 * c:512 * c + 512], start=(k == 0), stop=(k == KC - 1))
                    mm.on(last)


PAIRS = SLOTS // 2
PRIME = 5


def stage_peer(m, a, l, rows, ht, w_view, tiles):
    nc = m.nc
    uv = a[f"peer_uv{l}"]
    with Stage(m) as s:
        ring = m.ring[:, :].rearrange("p (r d) -> p r d", r=RING)
        qt = m.part(0, "b t", b=HALVES, t=TOK)
        prod = s.sb("gated_experts", [P, D])
        norm = Norm(s, m, rows, SC2, SH2, ht, tiles, (0, 1, 2, 3), junk=prod)
        spans = [(0, SEQ), (SEQ, CTX)][:1 if len(tiles) <= NTL else 2]
        proj = Project(s, m, w_view, [(h, qt[:, 2 * h:2 * h + 2, :], True, spans) for h in range(PH)], ht,
                       [rows[:, st, SH1:SC1 + 1, :].rearrange("p j (k n) -> p (j k) n", n=GW) for st in range(2)],
                       (4, 5, 6, 7))
        keys = s.sb("keys_T", [P, HALVES, PK])
        qs = s.sb("q_stage", [P, 2, 2, P])
        idx, idx_next = s.sb("idx", [P, SLOTS], U32), s.sb("idx_next", [P, SLOTS], U32)
        gate, gate_next = s.sb("gate", [P, SLOTS]), s.sb("gate_next", [P, PH, TOPK])
        top = s.sb("top_scores", [P, PH, TOPK])
        best = s.sb("best", [P, 2, TOPK])
        bi = s.sb("best_idx", [P, 2, TOPK], U32)
        bif = s.sb("best_idx_f", [P, 2, TOPK])
        work = s.sb("topk_work", [P, PK])
        cand = s.sb("cand", [P, TOPK * TOPK])
        cwork = s.sb("cand_work", [P, TOPK * TOPK])
        pos, split = s.sb("cand_pos", [P, TOPK], U32), s.sb("pos_split", [P, 2, TOPK], U32)
        splitf = s.sb("pos_split_f", [P, 2, TOPK])
        hot = s.sb("one_hot", [P, 2, TOPK, TOPK])
        half = s.sb("half_idx", [P, 2, TOPK])
        red = s.sb("gate_sums", [P, PH, 2])
        junk = s.sb("dot_products", [P, 2, D], mybir.dt.bfloat16)
        dot, act_ = s.sb("dots", [P, 2, 2]), s.sb("gelu_dots", [P, 2, 2])
        diag = s.sb("diag_w", [P, 2, 2, P])
        hcur = s.sb("h_cur", [P, D])
        k_in = s.sem("keys_loaded")
        gathered, before = m.gathered, m.gathered[0].n
        ready, dots, gel, dg, used = (s.sem(x) for x in ("idx_ready", "dots_done", "gelu_done", "diag_done", "pair_used"))
        ch, issued, begun, acc_free = s.sem("topk_chain"), s.sem("pairs_begun"), s.sem("topk_begun"), s.sem("acc_free")
        qc, sc, tk = s.sem("q_staged"), s.sem("scores_done"), s.sem("scores_read")
        ex, exi = s.sem("gates_exp"), s.sem("gates_shifted")
        acc = [m.bank[0], m.bank[1]]
        n = len(tiles)
        V = nc.vector
        block = s.block()

        class chain:

            def __init__(self, dve):
                self.dve, self.n = dve, 0
                dve.sem_clear(ch.sem)

            def __call__(self, ins):
                ins.then_inc(ch.sem, 1)
                self.n += 1
                self.dve.wait_ge(ch.sem, self.n)

        def topk_half(dve, t, h, z):
            c = chain(dve)
            if z == 0:
                dve.wait_ge(sc.sem, t * PH + (h + 1))
                dve.sem_inc(begun.sem, 1)
            sv = m.bank[2 + h % 2][:, z * PK:(z + 1) * PK]
            lo, hi = best[:, z, 0:8], best[:, z, 8:16]
            c(V.max(lo, sv))
            c(V.match_replace(work[:, :], lo, sv, -3.0e38))
            c(V.max(hi, work[:, :]))
            c(V.max_index(bi[:, z, 0:8], lo, sv))
            c(V.max_index(bi[:, z, 8:16], hi, work[:, :]))
            if z == 1:
                tk.on(V.tensor_copy(bif[:, :, :], bi[:, :, :]))

        def topk_cross(dve, t, h):
            c = chain(dve)
            c(V.tensor_tensor(cand[:, :].rearrange("p (i j) -> p i j", i=TOPK),
                              bcast(best[:, 0, :].unsqueeze(2), [P, TOPK, TOPK]),
                              bcast(best[:, 1, :].unsqueeze(1), [P, TOPK, TOPK]), ALU.add))
            lo, hi = top[:, h, 0:8], top[:, h, 8:16]
            c(V.max(lo, cand[:, :]))
            c(V.match_replace(cwork[:, :], lo, cand[:, :], -3.0e38))
            c(V.max(hi, cwork[:, :]))
            c(V.max_index(pos[:, 0:8], lo, cand[:, :]))
            c(V.max_index(pos[:, 8:16], hi, cwork[:, :]))

        def topk_index(dve, t, h):
            c = chain(dve)
            c(V.tensor_scalar(split[:, 0, :], pos[:, :], 4, None, ALU.logical_shift_right))
            c(V.tensor_scalar(split[:, 1, :], pos[:, :], 15, None, ALU.bitwise_and))
            c(V.tensor_copy(splitf[:, :, :], split[:, :, :]))
            for z in range(2):
                c(V.tensor_tensor(hot[:, z, :, :], bcast(splitf[:, z, :].unsqueeze(2), [P, TOPK, TOPK]),
                                  bcast(m.iota[:, :].unsqueeze(1), [P, TOPK, TOPK]), ALU.is_equal))
                c(V.tensor_tensor(hot[:, z, :, :], hot[:, z, :, :],
                                  bcast(bif[:, z, :].unsqueeze(1), [P, TOPK, TOPK]), ALU.mult))
                c(V.tensor_reduce(out=half[:, z, :], in_=hot[:, z, :, :], axis=AX.X, op=ALU.add))
            c(V.scalar_tensor_tensor(out=idx_next[:, h * TOPK:(h + 1) * TOPK], in0=half[:, 0, :], scalar=float(PK),
                                     in1=half[:, 1, :], op0=ALU.mult, op1=ALU.add))

        def topk_part(dve, t, part):
            h, k = divmod(part, 4)
            if k < 2:
                topk_half(dve, t, h, k)
            elif k == 2:
                topk_cross(dve, t, h)
            else:
                topk_index(dve, t, h)

        def gates_shift(dve, t):
            exi.on(V.tensor_tensor(gate_next[:, :, :], top[:, :, :], bcast(top[:, :, 0:1], [P, PH, TOPK]),
                                   ALU.subtract))

        def gates_norm(dve, t):
            c = chain(dve)
            dve.wait_ge(ex.sem, t + 1)
            c(V.tensor_reduce(out=red[:, :, 0:1], in_=gate_next[:, :, :], axis=AX.X, op=ALU.add))
            c(V.reciprocal(red[:, :, 1:2], red[:, :, 0:1]))
            c(V.tensor_tensor(gate_next[:, :, :], gate_next[:, :, :], bcast(red[:, :, 1:2], [P, PH, TOPK]), ALU.mult))

        HALF = SLOTS // 2

        def publish(eng, part):
            c = slice(part * HALF, (part + 1) * HALF)
            ready.on(V.tensor_copy(idx[:, c], idx_next[:, c]))

        def pool_tile(pool, t):
            for p in range(PAIRS):
                if p in (0, PAIRS // 2):
                    pool.wait_ge(ready.sem, t * 2 + (1 + (p > 0)))
                pool.wait_ge(used.sem, t * PAIRS + (PRIME + p - RING // 2 + 1))
                pool.sem_inc(issued.sem, 1)
                for j in range(2):
                    sl = 2 * p + j
                    nc.gpsimd.indirect_dma_start(ring[:, sl % RING, :], None, uv,
                                                 bass.IndirectOffsetOnAxis(ap=idx[:, sl:sl + 1], axis=0)) \
                      .then_inc(gathered[sl % RING].sem, 16)

        def vector_tile(dve, t, stream, with_next):
            publish(dve, 1)
            done_c = chain(dve)
            done_c(V.tensor_copy(gate[:, :], gate_next[:, :, :].rearrange("p h k -> p (h k)")))
            done_c(V.tensor_copy(hcur[:, :], m.h[:, bass.ds(t, 1), :].rearrange("p a d -> p (a d)")))

            def spread(p):
                dve.wait_ge(gel.sem, t * PAIRS + (p + 1))
                dve.wait_ge(used.sem, t * PAIRS + (PRIME + p - 1))
                for j in range(2):
                    last = V.tensor_scalar(diag[:, p % 2, j, :], m.ident[:, :], act_[:, p % 2, j:j + 1],
                                           gate[:, 2 * p + j:2 * p + j + 1], ALU.mult, ALU.mult)
                dg.on(last)

            for p in range(PAIRS):
                dve.wait_ge(dots.sem, t * PAIRS + (p + 1))
                for j in range(2):
                    sl = 2 * p + j
                    dve.wait_ge(gathered[sl % RING].sem, t * (16 * SLOTS // RING) + (before + 16 * (sl // RING + 1)))
                    last = V.tensor_tensor_reduce(out=junk[:, j, :], in0=ring[:, sl % RING, 0:D], in1=hcur[:, :], scale=1.0,
                                                  scalar=0.0, op0=ALU.mult, op1=ALU.add, accum_out=dot[:, p % 2, j:j + 1])
                dots.on(last)
                if p:
                    spread(p - 1)
                if with_next and 1 <= p <= 4 * PH:
                    topk_part(dve, t + 1, p - 1)
                if with_next and p == 4 * PH + 2:
                    gates_shift(dve, t + 1)
                if with_next and p == 4 * PH + 6:
                    gates_norm(dve, t + 1)
                if with_next and p == 4 * PH + 8:
                    publish(dve, 0)
            spread(PAIRS - 1)
            c = chain(dve)
            dve.wait_ge(used.sem, t * PAIRS + (PRIME + PAIRS))
            xt = m.x[:, bass.ds(t, 1), :].rearrange("p a d -> p (a d)")
            for j in range(2):
                cols = slice(512 * j, 512 * j + 512)
                c(V.tensor_tensor(prod[:, cols], acc[j][:, :], m.gate2[:, stream, cols], ALU.mult))
            acc_free.on(V.tensor_tensor(xt, xt, prod[:, :], ALU.add))

        def stage_scores_act(act, t, h):
            act.wait_ge(tk.sem, t * PH + (h + 1))
            qc.on(nc.scalar.activation(qs[:, h % 2, :, :], qt[:, 2 * h:2 * h + 2, bass.ds(t * P, P)], ACT.Copy))

        def scalar_tile(act, t, with_next):
            for p in range(PAIRS):
                if with_next and p % 4 == 0 and p < 4 * PH:
                    stage_scores_act(act, t + 1, p // 4)
                act.wait_ge(dots.sem, t * PAIRS + (p + 2))
                gel.on(nc.scalar.activation(act_[:, p % 2, :], dot[:, p % 2, :], ACT.Gelu_apprx_tanh))
                if with_next and p == 4 * PH + 3:
                    exp_gates(act, t + 1)

        def exp_gates(act, t):
            act.wait_ge(exi.sem, t + 1)
            ex.on(nc.scalar.activation(gate_next[:, :, :], gate_next[:, :, :], ACT.Exp))

        def scores(pe, t, h):
            pe.wait_ge(qc.sem, t * PH + (h + 1))
            for z in range(2):
                last = nc.tensor.matmul(m.bank[2 + h % 2][:, z * PK:(z + 1) * PK], qs[:, h % 2, z, :],
                                        keys[:, 2 * h + z, :], start=True, stop=True)
            sc.on(last)

        def tensor_tile(pe, t, with_next):
            for p in range(PAIRS):
                if with_next and p % 4 == 0 and p < 4 * PH:
                    scores(pe, t + 1, p // 4)
                pe.wait_ge(dg.sem, t * PAIRS + (p + 1))
                if p == 0:
                    pe.wait_ge(acc_free.sem, t + 1)
                for j in range(2):
                    for c in range(2):
                        last = nc.tensor.matmul(acc[c][:, :], diag[:, p % 2, j, :],
                                                ring[:, (2 * p + j) % RING, D + 512 * c:D + 512 * c + 512],
                                                start=(p == 0 and j == 0), stop=(p == PAIRS - 1 and j == 1))
                used.on(last)

        turn = min(n - 1, NTL)

        def every_tile(eng, body):
            with eng.Fori(0, turn) as t:
                body(t, 0, True)
            for t in range(turn, n):
                body(t, t // NTL, t + 1 < n)

        @block.sync
        def _(sp):
            sp.dma_start(keys[:, :, :], a["peer_keys"][l]).then_inc(k_in.sem, 16)
            proj.sync(sp)

        @block.gpsimd
        def _(pool):
            every_tile(pool, lambda t, st, nxt: pool_tile(pool, t))
            for g in gathered:
                g.n += n * 16 * SLOTS // RING

        @block.vector
        def _(dve):
            norm.vector(dve)
            dve.sem_inc(tk.sem, 2)
            dve.sem_inc(dots.sem, 1)
            dve.sem_inc(acc_free.sem, 1)
            for part in range(4 * PH):
                topk_part(dve, 0, part)
            gates_shift(dve, 0)
            gates_norm(dve, 0)
            publish(dve, 0)
            every_tile(dve, lambda t, st, nxt: vector_tile(dve, t, st, nxt))

        @block.scalar
        def _(act):
            norm.scalar(act)
            for h in range(PH):
                proj.scalar_group(act, h)
                act.wait_ge(proj.copied.sem, proj.u_act)
                stage_scores_act(act, 0, h)
            exp_gates(act, 0)
            every_tile(act, lambda t, st, nxt: scalar_tile(act, t, nxt))

        @block.tensor
        def _(pe):
            norm.tensor(pe)
            for h in range(PH):
                proj.tensor_group(pe, h)
                if h == 0:
                    pe.wait_ge(k_in.sem, 16)
                scores(pe, 0, h)
            pe.sem_inc(used.sem, PRIME)
            every_tile(pe, lambda t, st, nxt: tensor_tile(pe, t, nxt))


def stage_final(m, a, out):
    nc = m.nc
    with Stage(m, last=True) as s:
        fg, junk, ssq = s.sb("final_gain", [P, D]), s.sb("f_squares", [P, D]), s.sb("f_ssq", [P, NTL])
        g_in, sq, ms, rt, fo, st = (s.sem(x) for x in ("final_gain_loaded", "f_squares_done", "f_mean", "f_root",
                                                       "final_done", "stored"))
        block = s.block()

        @block.sync
        def _(sp):
            sp.dma_start(fg[:, :], a["final_g"].broadcast_to([P, D])).then_inc(g_in.sem, 16)
            for t in range(NTL):
                sp.wait_ge(fo.sem, t + 1)
                sp.dma_start(out[t * P:(t + 1) * P, :], m.h[:, t, :]).then_inc(st.sem, 16)
            sp.wait_ge(st.sem, 16 * NTL)

        @block.scalar
        def _(act):
            for t in range(NTL):
                done(act, sq, nc.scalar.activation(junk[:, :], m.x[:, t, :], ACT.Square, accum_out=ssq[:, t:t + 1]))
            act.wait_ge(ms.sem, 2)
            rt.on(nc.scalar.activation(ssq[:, :], ssq[:, :], ACT.Sqrt))

        @block.vector
        def _(dve):
            dve.wait_ge(sq.sem, NTL)
            done(dve, ms, nc.vector.tensor_scalar(ssq[:, :], ssq[:, :], 1.0 / D, EPS, ALU.mult, ALU.add))
            ms.on(nc.vector.reciprocal(ssq[:, :], ssq[:, :]))
            dve.wait_ge(rt.sem, 1)
            dve.wait_ge(g_in.sem, 16)
            for t in range(NTL):
                fo.on(nc.vector.scalar_tensor_tensor(out=m.h[:, t, :], in0=m.x[:, t, :], scalar=ssq[:, t:t + 1],
                                                     in1=fg[:, :], op0=ALU.mult, op1=ALU.mult))


def build(nc, a, out, until=None):
    count = [0]

    def go(stage, *args):
        count[0] += 1
        if until is None or count[0] <= until:
            stage(*args)

    with ExitStack() as ctx:
        m = Machine(nc, ctx)
        go(stage_load, m, a)
        every = list(range(NT))
        spans = [(0, SEQ), (SEQ, CTX)]
        for l in range(DEPTH):
            tiles = every if l < DEPTH - 1 else every[:NTL]
            out_spans = spans[:2 if l < DEPTH - 1 else 1]
            view = lambda w: w[l].rearrange("(k p) n -> p k n", p=P)
            ht = m.ring[:, 0:KC * TOK].rearrange("p (k t) -> p k t", k=KC)
            rows = m.ring[:, KC * TOK:].rearrange("p (s j d) -> p s j d", s=2, j=N_MOD - 1)
            go(stage_modulation, m, a, l, rows, ht)
            base = rows[:, 0, 0:2, :].rearrange("p c (u n) -> p c u n", u=UNITS)
            wide = rows[:, 1, 0, :].rearrange("p (d f c j h) -> p d f c j h", d=2, f=2, c=2, j=4)
            lc = rows[:, 1, 1, :].rearrange("p (c u h) -> p c u h", c=2, u=UNITS)
            q, k, cb, cc, cx, su = (m.part(i * 2 * TOK, "f t", f=2, t=TOK) for i in (0, 1, 2, 3, 4, 7))
            v, fz = (m.part(i * 2 * TOK, "t n", t=NT, n=GW) for i in (5, 6))
            go(stage_inputs, m, a, l, rows,
               [(7, su, True, spans), (0, q, True, out_spans), (1, k, True, spans), (2, v, False, every),
                (3, cb, True, out_spans), (4, cc, True, out_spans), (5, cx, True, out_spans),
                (6, fz, False, tiles)], view(a["w_in"]), ht, m.seeds, m.tmp, wide, lc, base)
            y = m.h
            go(stage_attention, m, a, l, q, k, v, y, tiles, ht)
            go(stage_conv, m, a, l, cb, cc, cx, y, tiles)
            go(stage_fourier, m, a, fz, y, tiles)
            go(stage_s5, m, a, l, su, y, tiles, m.seeds, m.tmp[:, 5, :], wide, lc, base, ht)
            go(stage_merge, m, a, l, rows, y, ht, tiles)
            go(stage_peer, m, a, l, rows, ht, view(a["peer_wq"]), tiles)
            if l < DEPTH - 1:
                go(stage_clear, m)
        if until is None:
            stage_final(m, a, out)


def constants():
    i = np.arange(TOPK)
    col = np.arange(GRID_W)
    start = np.clip(col - 8, 0, GRID_W - 16)
    ok = (col[None, :] >= start[:, None]) & (col[None, :] < start[:, None] + 16)
    mask = np.where(ok, 0.0, -1e30).astype(np.float32)

    def dft(n, scale):
        w = 2 * np.pi * (np.outer(np.arange(n), np.arange(n)) % n) / n
        return np.cos(w) * scale, np.sin(w) * scale

    def positions(n):
        t = np.stack(dft(n, 1 / math.sqrt(n * DH)), 1).astype(np.float32)
        return np.ascontiguousarray(t.reshape(n // P, P, 2, n).transpose(1, 0, 2, 3))

    chan = np.zeros((P, 2, P), np.float32)
    c, sn = dft(DH, 1.0)
    for b in range(2):
        r = slice(b * DH, (b + 1) * DH)
        chan[r, 0, r], chan[r, 1, r] = c, -sn
    pick = np.zeros((2, 2, P), np.float32)
    pick[0, 0], pick[1, 1] = 1, 1
    turn = np.zeros((P, P), np.float32)
    for b in range(2):
        turn[b * GRID_W:(b + 1) * GRID_W, b * GRID_W:(b + 1) * GRID_W] = np.eye(GRID_W)[::-1]
    return {
        "ident": np.eye(P, dtype=np.float32), "pick": pick, "flip": turn,
        "iota": np.tile(i.astype(np.float32), (P, 1)),
        "col_mask": np.concatenate([mask, mask]),
        "dft_lat": positions(SEQ), "dft_ctx": positions(CTX), "dft_chan": chan,
    }


def layouts(x, c, ctx, c_ctx, ada_w, ada_b, norm1_g, norm2_g, w_in, na_rpb, conv_w, s5_a_re, s5_a_im, s5_b_re,
            s5_b_im, s5_c_re, s5_c_im, s5_log_dt, s5_d, s5_w_glu, grp_g, w_out, peer_wq, peer_keys, peer_u, peer_v,
            final_g):
    L = DEPTH

    def states(t):
        t = t.reshape(L, 2, 8, P, *t.shape[4:])
        return np.moveaxis(t, 3, 1).reshape(L, P, UNITS, *t.shape[4:])

    log_dt = np.repeat(s5_log_dt[..., None], DH, axis=-1)
    rpb = np.zeros((L, NH, 17, 2 * GRID_W - 1), np.float32)
    rpb[:, :, 1:16, 48:79] = na_rpb
    return {
        "x": x[0], "ctx": ctx[0],
        "cond": np.stack([c[0], c_ctx]).reshape(2, KC, P).transpose(2, 1, 0),
        "ada_w": ada_w, "ada_b": ada_b, "norm1_g": norm1_g, "norm2_g": norm2_g, "w_in": w_in,
        "rpb": rpb, "conv_w": conv_w.reshape(L, 3, 2, P).transpose(0, 3, 2, 1),
        "s5_params": np.stack([states(s5_a_re), states(s5_a_im), states(log_dt)], 2),
        "s5_b": np.stack([states(s5_b_re), states(s5_b_im)], 2),
        "s5_c": np.stack([states(t.transpose(0, 1, 2, 4, 3)) for t in (s5_c_re, s5_c_im)], 2),
        "s5_d": s5_d.reshape(L, 2, P).transpose(0, 2, 1), "s5_w_glu": s5_w_glu,
        "grp_g": grp_g.reshape(L, D), "w_out": w_out, "peer_wq": peer_wq,
        "peer_keys": peer_keys.reshape(L, HALVES, PK, P).transpose(0, 3, 1, 2),
        **{f"peer_uv{l}": np.concatenate([peer_u[l], peer_v[l]], axis=-1) for l in range(L)},
        "final_g": final_g[None, :],
    }


def kernel(**inputs):
    import concourse.bacc as bacc
    from concourse.bass_utils import run_bass_kernel_spmd

    arrays = layouts(**{n: np.asarray(v) for n, v in inputs.items()})
    arrays.update(constants())
    arrays = {n: np.ascontiguousarray(v) for n, v in arrays.items()}
    nc = bacc.Bacc("TRN2", target_bir_lowering=False, num_devices=1)
    aps = {n: nc.dram_tensor(f"in_{n}", v.shape, F32, kind="ExternalInput").ap() for n, v in arrays.items()}
    out = nc.dram_tensor("out", (SEQ, D), F32, kind="ExternalOutput").ap()
    build(nc, aps, out)
    r = run_bass_kernel_spmd(nc, [{f"in_{n}": v for n, v in arrays.items()}], core_ids=[0])
    return r.results[0]["out"].reshape(1, SEQ, D)
```

```python
import math
from contextlib import ExitStack

import numpy as np

import concourse.bass as bass
from concourse import mybir

F32 = mybir.dt.float32
U32 = mybir.dt.uint32
ALU = mybir.AluOpType
ACT = mybir.ActivationFunctionType
AX = mybir.AxisListType

P = 128
D = 1024
KC = D // P
SEQ, CTX = 512, 256
TOK = SEQ + CTX
NT, NTL = TOK // P, SEQ // P
DEPTH = 2
N_MOD = 6
GW = 256
NH, DH = 4, 64
GRID_W, ROWS = 64, SEQ // 64
BASE = 64
NS = 10
UNITS = 16
EPS = 1e-6
PH, PK, TOPK = 8, 128, 16
HALVES = 2 * PH
SLOTS = PH * TOPK
RING = 8
SH1, SC1, G1, SH2, SC2, G2 = range(N_MOD)


class Signal:

    def __init__(self, sem):
        self.sem, self.n = sem, 0

    def on(self, ins, by=1):
        ins.then_inc(self.sem, by)
        self.n += by
        return self.n


def done(eng, signal, ins):
    eng.wait_ge(signal.sem, signal.on(ins))


class Machine:

    def __init__(self, nc, ctx):
        self.nc = nc
        self.stages = 0
        self.gathered = [Signal(ctx.enter_context(nc.semaphore(f"gathered{j}"))) for j in range(RING)]
        self.rows_in = Signal(ctx.enter_context(nc.semaphore("rows_loaded")))
        self.h_out = nc.dram_tensor("h_rows", (TOK, D), F32).ap()
        self.mod = [nc.dram_tensor(f"mod_rows{l}", (2, N_MOD * D), F32).ap() for l in range(DEPTH)]
        self.spent = []
        self.x = ctx.enter_context(nc.sbuf_tensor("x_stream", [P, NT, D], F32))
        self.ident = ctx.enter_context(nc.sbuf_tensor("ident", [P, P], F32))
        self.cond = ctx.enter_context(nc.sbuf_tensor("cond_silu", [P, KC, 32], F32))
        self.ssq = ctx.enter_context(nc.sbuf_tensor("x_squares", [P, NT], F32))
        self.gsq = ctx.enter_context(nc.sbuf_tensor("group_squares", [P, NT, 4], F32))
        self.iota = ctx.enter_context(nc.sbuf_tensor("iota16", [P, TOPK], F32))
        self.gate2 = ctx.enter_context(nc.sbuf_tensor("gate2_rows", [P, 2, D], F32))
        self.h = ctx.enter_context(nc.sbuf_tensor("h_tok", [P, NT, D], F32))
        self.ring = ctx.enter_context(nc.sbuf_tensor("ring", [P, RING * 2 * D], F32))
        self.seeds = ctx.enter_context(nc.sbuf_tensor("s5_seeds", [P, NS, 3, UNITS], F32))
        self.tmp = ctx.enter_context(nc.sbuf_tensor("s5_tmp", [P, 16, UNITS], F32))
        self.big = ctx.enter_context(nc.sbuf_tensor("big", [P, HALVES * TOK], F32))
        self.bank = [ctx.enter_context(nc.psum_tensor(f"bank{i}", [P, 512], F32)) for i in range(8)]

    def part(self, first, pattern, **sizes):
        n = math.prod(sizes.values())
        names = " ".join(sizes)
        return self.big[:, first:first + n].rearrange(f"p ({names}) -> p {pattern}", **sizes)


class Stage:

    def __init__(self, m, last=False):
        self.m, self.nc, self.stack, self.last = m, m.nc, ExitStack(), last
        m.stages += 1

    def __enter__(self):
        return self

    def __exit__(self, *e):
        return self.stack.__exit__(*e)

    def sem(self, name):
        sem = self.stack.enter_context(self.nc.semaphore(name))
        self.m.spent.append(sem.num)
        return Signal(sem)

    def sb(self, name, shape, dtype=F32):
        return self.stack.enter_context(self.nc.sbuf_tensor(f"{name}_{self.m.stages}", shape, dtype))

    def block(self):
        return self.stack.enter_context(self.nc.Block(no_gpsimd_drain=not self.last))


def bcast(ap, shape):
    return ap.broadcast_to(shape)


def stage_clear(m):
    with m.nc.Block(no_gpsimd_drain=True) as block:

        @block.gpsimd
        def _(pool):
            pool.sem_clear(range(min(m.spent), max(m.spent) + 1))

    m.spent.clear()


class Modulation:
    GROUPS = N_MOD * D // 512
    PER = D // 512

    def __init__(self, s, m, a, l, slots, sub, banks):
        self.m, self.a, self.l, self.slots, self.sub, self.banks = m, a, l, slots, sub, banks
        self.n = 512 // (4 * sub)
        self.acc = s.sb("mod", [P, self.GROUPS, 128])
        self.bias, self.gains = s.sb("mod_bias", [P, self.GROUPS, 128]), s.sb("mod_gains", [P, 2, self.PER, 128])
        self.w_in = [s.sem(f"ada_w_loaded{j}") for j in range(len(slots))]
        self.zeroed, self.small, self.mm, self.ev, self.vec, self.wr = (
            s.sem(n) for n in ("bias_zeroed", "bias_loaded", "mod_mm", "mod_evac", "vector_done", "mod_written"))

    def spread(self, dram):
        return dram.rearrange("o (b j c) -> (o j) b c", j=4, c=self.n)

    def blocks(self, t, r):
        return t[r:P:32, :, :].rearrange("p g (s c) -> p (g s) c", s=self.sub)

    def sync_small(self, sp):
        a, l = self.a, self.l
        sp.wait_ge(self.zeroed.sem, 2)
        for r in range(2):
            self.small.on(sp.dma_start(self.blocks(self.bias, r), self.spread(a["ada_b"][l:l + 1, :])), 16)
            for g, name in enumerate(("norm1_g", "norm2_g")):
                self.small.on(sp.dma_start(self.blocks(self.gains[:, g, :, :], r), self.spread(a[name][l:l + 1, :])), 16)

    def sync_group(self, sp, g):
        w = self.a["ada_w"][self.l].rearrange("(k p) n -> p k n", p=P)
        W, width = len(self.slots), 4 * self.n
        for b in range(self.sub * g, self.sub * (g + 1)):
            if b >= W:
                sp.wait_ge(self.mm.sem, (b - W) // self.sub + 1)
            self.w_in[b % W].on(sp.dma_start(self.slots[b % W], w[:, :, width * b:width * (b + 1)]), 16)

    def tensor_group(self, pe, g):
        m, n, W = self.m, self.n, len(self.slots)
        bank = m.bank[self.banks[g % len(self.banks)]]
        if g >= len(self.banks):
            pe.wait_ge(self.ev.sem, g - len(self.banks) + 1)
        for b in range(self.sub * g, self.sub * (g + 1)):
            pe.wait_ge(self.w_in[b % W].sem, 16 * (b // W + 1))
            c0 = n * (b % self.sub)
            for k in range(KC):
                for j in range(4):
                    last = m.nc.tensor.matmul(bank[32 * j:32 * j + 32, c0:c0 + n], m.cond[:, k, :],
                                              self.slots[b % W][:, k, n * j:n * j + n], start=(k == 0), stop=(k == KC - 1))
        self.mm.on(last)

    def vector_start(self, dve):
        self.zeroed.on(self.m.nc.vector.memset(self.bias[:, :, :], 0.0))
        self.zeroed.on(self.m.nc.vector.memset(self.gains[:, :, :, :], 0.0))
        dve.wait_ge(self.zeroed.sem, 2)

    def vector_group(self, dve, g):
        V, bank, (j, last) = self.m.nc.vector, self.m.bank[self.banks[g % len(self.banks)]], divmod(g, self.PER)
        if g == 0:
            dve.wait_ge(self.small.sem, self.small.n)
        dve.wait_ge(self.mm.sem, g + 1)
        self.ev.on(V.tensor_tensor(self.acc[:, g, :], bank[:, 0:128], self.bias[:, g, :], ALU.add))
        if last == self.PER - 1:
            dve.wait_ge(self.ev.sem, g + 1)
            vec = self.acc[:, g - last:g + 1, :]
            if j in (SC1, SC2):
                self.vec.on(V.scalar_tensor_tensor(out=vec, in0=vec, scalar=1.0, in1=self.gains[:, j // SC2, :, :],
                                                   op0=ALU.add, op1=ALU.mult))
            else:
                self.vec.on(dve.nop())

    def store(self, eng, j0, j1):
        eng.wait_ge(self.vec.sem, j1)
        for r in range(2):
            self.wr.on(eng.dma_start(self.spread(self.m.mod[self.l][r:r + 1, j0 * D:j1 * D]),
                                     self.blocks(self.acc[:, self.PER * j0:self.PER * j1, :], r)), 16)
        eng.wait_ge(self.wr.sem, self.wr.n)


def load_rows(eng, m, l, rows, vectors, signal, streams=range(2)):
    for j in vectors:
        for st in streams:
            dst = rows[:, st, j, :] if j < G2 else m.gate2[:, st, :]
            signal.on(eng.dma_start(dst, m.mod[l][st:st + 1, j * D:(j + 1) * D].broadcast_to([P, D])), 16)


NORM_VECTOR, NORM_TENSOR = 8, 10


def stage_modulation(m, a, rows, ht):
    nc = m.nc
    with Stage(m) as s:
        W = 3
        ring = m.part(0, "w k n", w=W, k=KC, n=512)
        raw, junk = s.sb("cond_raw", [P, KC, 2]), s.sb("squares", [P, D])
        ada = Modulation(s, m, a, 0, [ring[:, j, :, :] for j in range(W)], 1, (0, 1, 2, 3))
        norm = Norm(s, m, rows, SC1, SH1, ht, list(range(NT)), (4, 5, 6, 7))
        c_in, c_zero, c_out, x_in, sq, norm_in = (s.sem(n) for n in (
            "cond_loaded", "cond_zeroed", "silu_done", "x_loaded", "squares_done", "norm1_rows_loaded"))
        block = s.block()

        @block.sync
        def _(sp):
            c_in.on(sp.dma_start(raw[:, :, :], a["cond"]), 16)
            for g in range(W):
                ada.sync_group(sp, g)
            ada.sync_small(sp)
            x_in.on(sp.dma_start(m.x[:, :NTL, :], a["x"].rearrange("(t p) d -> p t d", p=P)), 16)
            x_in.on(sp.dma_start(m.x[:, NTL:, :], a["ctx"].rearrange("(t p) d -> p t d", p=P)), 16)
            x_in.on(sp.dma_start(m.ident[:, :], a["ident"]), 16)
            x_in.on(sp.dma_start(m.iota[:, :], a["iota"]), 16)
            for g in range(W, ada.GROUPS):
                ada.sync_group(sp, g)

        @block.tensor
        def _(pe):
            pe.wait_ge(c_out.sem, 1)
            for g in range(ada.GROUPS):
                if g == NORM_TENSOR:
                    norm.tensor(pe)
                ada.tensor_group(pe, g)

        @block.vector
        def _(dve):
            c_zero.on(nc.vector.memset(m.cond[:, :, :], 0.0))
            ada.vector_start(dve)
            for g in range(ada.GROUPS):
                if g == NORM_VECTOR:
                    dve.wait_ge(sq.sem, NT)
                    dve.wait_ge(norm_in.sem, 4 * 16)
                    norm.vector(dve)
                ada.vector_group(dve, g)

        @block.scalar
        def _(act):
            act.wait_ge(c_in.sem, 16)
            act.wait_ge(c_zero.sem, 1)
            c_out.on(nc.scalar.activation(m.cond[:, :, 0:2], raw[:, :, :], ACT.Silu))
            act.wait_ge(x_in.sem, x_in.n)
            for t in range(NT):
                done(act, sq, nc.scalar.activation(junk[:, :], m.x[:, t, :], ACT.Square, accum_out=m.ssq[:, t:t + 1]))
            for j in range(N_MOD):
                ada.store(act, j, j + 1)
                if j != G2:
                    load_rows(act, m, 0, rows, (j,), norm_in if j <= SC1 else m.rows_in)
                if j == SC1 + 1:
                    norm.scalar(act)


class Norm:

    def __init__(self, s, m, rows, sc, sh, ht, tiles, banks):
        self.m, self.rows, self.sc, self.sh, self.ht, self.tiles, self.banks = m, rows, sc, sh, ht, tiles, banks
        self.ssq = m.ssq
        self.mean, self.root, self.h_done, self.turned, self.copied, self.scaled = (
            s.sem(n) for n in ("mean_done", "root_done", "h_done", "h_transposed", "hT_copied", "h_scaled"))

    def scalar(self, act, i0=0, i1=None):
        m, n, ssq = self.m, len(self.tiles), self.ssq
        if i0 == 0:
            act.wait_ge(self.mean.sem, 2)
            self.root.on(m.nc.scalar.activation(ssq[:, :n], ssq[:, :n], ACT.Sqrt))
        for i in range(i0, n if i1 is None else i1):
            t = self.tiles[i]
            for c in range(2):
                act.wait_ge(self.turned.sem, 2 * i + c + 1)
                bank = m.bank[self.banks[(2 * i + c) % len(self.banks)]]
                self.copied.on(m.nc.scalar.activation(self.ht[:, 4 * c:4 * c + 4, t * P:(t + 1) * P],
                                                      bank[:, :].rearrange("p (k n) -> p k n", k=4), ACT.Copy))

    def vector(self, dve):
        m, n, ssq, V = self.m, len(self.tiles), self.ssq, self.m.nc.vector
        done(dve, self.mean, V.tensor_scalar(ssq[:, :n], ssq[:, :n], 1.0 / D, EPS, ALU.mult, ALU.add))
        self.mean.on(V.reciprocal(ssq[:, :n], ssq[:, :n]))
        dve.wait_ge(self.root.sem, 1)
        for t in self.tiles:
            st = t // NTL
            done(dve, self.scaled, V.scalar_tensor_tensor(out=m.h[:, t, :], in0=m.x[:, t, :], scalar=ssq[:, t:t + 1],
                                                          in1=self.rows[:, st, self.sc, :], op0=ALU.mult, op1=ALU.mult))
            self.h_done.on(V.tensor_tensor(m.h[:, t, :], m.h[:, t, :], self.rows[:, st, self.sh, :], ALU.add))
        dve.wait_ge(self.h_done.sem, n)

    def tensor(self, pe, i0=0, i1=None):
        m, banks = self.m, self.banks
        i1 = len(self.tiles) if i1 is None else i1
        for i in range(i0, i1):
            t = self.tiles[i]
            pe.wait_ge(self.h_done.sem, i + 1)
            for c in range(2):
                u = 2 * i + c
                if u >= len(banks):
                    pe.wait_ge(self.copied.sem, u - len(banks) + 1)
                for k in range(4):
                    last = m.nc.tensor.transpose(m.bank[banks[u % len(banks)]][:, k * P:(k + 1) * P],
                                                 m.h[:, t, (4 * c + k) * P:(4 * c + k + 1) * P], m.ident[:, :])
                self.turned.on(last)
        pe.wait_ge(self.copied.sem, 2 * i1)


class Project:

    def __init__(self, s, m, w_view, groups, ht, places, banks):
        self.m, self.w, self.groups, self.ht, self.places, self.banks = m, w_view, groups, ht, places, banks
        self.loaded = [s.sem(f"w_loaded{j}") for j in range(len(places))]
        self.used, self.multiplied, self.copied = s.sem("w_used"), s.sem("product_done"), s.sem("product_copied")
        self.u_pe = self.u_act = 0

    def outs(self, g):
        _col, dst, feat, spans = self.groups[g]
        if feat:
            return [(dst[:, b, t0:t0 + n], b, t0, n) for b in range(2) for t0, n in spans]
        return [(dst[:, t, :], None, t * P, GW) for t in spans]

    def sync(self, sp):
        self.sync_groups(sp, 0, len(self.groups))

    def sync_groups(self, sp, g0, g1):
        W = len(self.places)
        for g in range(g0, g1):
            col = self.groups[g][0]
            if g >= W:
                sp.wait_ge(self.used.sem, g - W + 1)
            self.loaded[g % W].on(sp.dma_start(self.places[g % W], self.w[:, :, GW * col:GW * (col + 1)]), 16)

    def tensor_group(self, pe, g):
        nc, W, NB = self.m.nc, len(self.places), len(self.banks)
        w = self.places[g % W]
        pe.wait_ge(self.loaded[g % W].sem, 16 * (g // W + 1))
        for _dst, b, t0, n in self.outs(g):
            if self.u_pe >= NB:
                pe.wait_ge(self.copied.sem, self.u_pe - NB + 1)
            bank = self.m.bank[self.banks[self.u_pe % NB]]
            for k in range(KC):
                lhs, rhs = (self.ht[:, k, t0:t0 + P], w[:, k, :]) if b is None \
                    else (w[:, k, b * P:(b + 1) * P], self.ht[:, k, t0:t0 + n])
                last = nc.tensor.matmul(bank[:, :n], lhs, rhs, start=(k == 0), stop=(k == KC - 1))
            self.multiplied.on(last)
            self.u_pe += 1
        pe.wait_ge(self.multiplied.sem, self.u_pe)
        self.used.on(pe.nop())

    def scalar_group(self, act, g):
        for dst, _b, _t0, n in self.outs(g):
            act.wait_ge(self.multiplied.sem, self.u_act + 1)
            bank = self.m.bank[self.banks[self.u_act % len(self.banks)]]
            self.copied.on(self.m.nc.scalar.activation(dst, bank[:, :n], ACT.Copy))
            self.u_act += 1


def stage_inputs(m, a, l, rows, groups, w_view, ht, seeds, tmp, wide, lc, base):
    with Stage(m) as s:
        norm = Norm(s, m, rows, SC1, SH1, ht, list(range(NT)), (0, 1, 2, 3)) if l else None
        w = s.sb("w_ring", [P, 2, KC, GW])
        proj = Project(s, m, w_view, groups, ht, [w[:, j, :, :] for j in range(2)], (4, 5, 6, 7))
        s5 = S5Weights(s, m, a, l, seeds, tmp, wide, lc, base)
        norm_in = s.sem("norm1_rows_loaded")
        block = s.block()

        @block.sync
        def _(sp):
            if l:
                load_rows(sp, m, l, rows, (SC1, SH1), norm_in)
            proj.sync_groups(sp, 0, 2)
            s5.sync(sp)
            load_rows(sp, m, l, rows, (G1, SH2, SC2, G2) if l else (G2,), m.rows_in,
                      range(1 if l == DEPTH - 1 else 2))
            proj.sync_groups(sp, 2, len(groups))
            sp.wait_ge(m.rows_in.sem, m.rows_in.n)

        @block.scalar
        def _(act):
            if l:
                norm.scalar(act)
            for g in range(len(groups)):
                proj.scalar_group(act, g)

        @block.vector
        def _(dve):
            if l:
                dve.wait_ge(norm_in.sem, norm_in.n)
                norm.vector(dve)
            s5.vector(dve)

        @block.tensor
        def _(pe):
            if l:
                norm.tensor(pe)
            for g in range(len(groups)):
                proj.tensor_group(pe, g)


SCORE_BUFS = 3


def stage_attention(m, a, l, qt, kt, v, y, tiles, ht, tables):
    nc = m.nc
    scale = DH ** -0.5
    with Stage(m) as s:
        bias = s.sb("pos_bias", [P, NH, 16, GRID_W])
        falling = ht[:, 0:6, :].rearrange("p k t -> p (k t)")[:, 0:NH * 16 * GRID_W] \
            .rearrange("p (h j c) -> p h j c", h=NH, j=16)
        flip = s.sb("flip", [P, P])
        mask = s.sb("col_mask", [P, GRID_W])
        sc = s.sb("scores", [P, SCORE_BUFS, TOK])
        pt = s.sb("probs_T", [P, 2, TOK])
        st = s.sb("softmax_stats", [P, 4, 4])
        loads, biased, turned = s.sem("bias_loaded"), s.sem("bias_masked"), s.sem("bias_turned")
        sm, tp, om = s.sem("scores_mm"), s.sem("probs_transposed"), s.sem("out_mm")
        sb_, mx, rc, od = s.sem("scores_biased"), s.sem("max_done"), s.sem("sum_inverted"), s.sem("out_done")
        ex, pc = s.sem("exp_done"), s.sem("probsT_copied")
        tables_in = s.sem("dft_loaded")
        context = [(t, h) for t in tiles[NTL:] for h in range(NH)]
        todo = context + [(t, h) for t in tiles[:NTL] for h in range(NH)]
        n_ctx, N = len(context), len(todo)
        pad, rows = 2 * GRID_W - 1, 17
        block = s.block()

        scaled = [sum(1 + (t < NTL) for t, _h in todo[:i + 1]) for i in range(N)]

        def turned_bank(i, part):
            return m.bank[4 + (2 * i + part) % 3]

        @block.sync
        def _(sp):
            loads.on(sp.dma_start(mask[:, :], a["col_mask"]), 16)
            loads.on(sp.dma_start(flip[:, :], a["flip"]), 16)
            for h in range(NH):
                for half in range(2):
                    src = bass.AP(tensor=a["rpb"].tensor,
                                  offset=((l * NH + h) * rows + 1 - half) * pad,
                                  ap=[[1, GRID_W], [pad, 16], [1, GRID_W]])
                    loads.on(sp.dma_start(falling[64 * half:64 * half + 64, h, :, :], src), 16)
            sp.wait_ge(turned.sem, 2 * NH)
            for name, dst in tables[:2 if n_ctx else 1] + tables[2:]:
                tables_in.on(sp.dma_start(dst, a[name]), 16)
            sp.wait_ge(tables_in.sem, tables_in.n)

        @block.vector
        def _(dve):
            def mask_bias():
                dve.wait_ge(loads.sem, loads.n)
                for b in range(2 * NH):
                    h, j = b // 2, 8 * (b % 2)
                    dve.wait_ge(turned.sem, b + 1)
                    biased.on(nc.vector.tensor_tensor(bias[:, h, j:j + 8, :],
                                                      m.bank[4 + b % 3][:, :].rearrange("p (j c) -> p j c", j=8),
                                                      bcast(mask[:, :].unsqueeze(1), [P, 8, GRID_W]), ALU.add))
                dve.wait_ge(biased.sem, 2 * NH)

            def finish(i):
                t, h = todo[i]
                dve.wait_ge(ex.sem, i + 1)
                rc.on(nc.vector.reciprocal(st[:, i % 4, 2:3], st[:, i % 4, 1:2]))
                dve.wait_ge(om.sem, i + 1)
                dve.wait_ge(rc.sem, rc.n)
                od.on(nc.vector.tensor_scalar(y[:, t, h * DH:(h + 1) * DH], m.bank[7][:, 0:DH], st[:, i % 4, 2:3], None,
                                              ALU.mult))

            for i, (t, h) in enumerate(todo):
                if i == n_ctx:
                    mask_bias()
                dve.wait_ge(sm.sem, i + 1)
                if i >= SCORE_BUFS:
                    dve.wait_ge(tp.sem, i - SCORE_BUFS + 1)
                k = i % SCORE_BUFS
                if t < NTL:
                    j0 = 7 - 2 * t
                    sb_.on(nc.vector.scalar_tensor_tensor(
                        out=sc[:, k, 0:SEQ], in0=m.bank[i % 2][:, :], scalar=scale,
                        in1=bias[:, h, :, :].rearrange("p j c -> p (j c)")[:, j0 * GRID_W:(j0 + 8) * GRID_W],
                        op0=ALU.mult, op1=ALU.add))
                sb_.on(nc.vector.tensor_scalar(sc[:, k, SEQ:TOK], m.bank[2 + i % 2][:, 0:CTX], scale, None, ALU.mult))
                dve.wait_ge(sb_.sem, sb_.n)
                if i >= 4:
                    dve.wait_ge(od.sem, i - 3)
                mx.on(nc.vector.tensor_reduce(out=st[:, i % 4, 0:1], in_=sc[:, k, (0 if t < NTL else SEQ):TOK],
                                              axis=AX.X, op=ALU.max, negate=True))
                if i >= 2:
                    finish(i - 2)
            for i in range(N - 2, N):
                finish(i)

        @block.scalar
        def _(act):
            def copy_t(i):
                t, _h = todo[i]
                act.wait_ge(tp.sem, i + 1)
                if i >= 2:
                    act.wait_ge(om.sem, i - 1)
                if t < NTL:
                    pc.on(nc.scalar.activation(pt[:, i % 2, 0:SEQ], turned_bank(i, 0)[:, :], ACT.Copy))
                else:
                    pc.on(act.nop())
                pc.on(nc.scalar.activation(pt[:, i % 2, SEQ:TOK], turned_bank(i, 1)[:, 0:CTX], ACT.Copy))

            for i, (t, h) in enumerate(todo):
                if i >= 2:
                    copy_t(i - 2)
                k0 = 0 if t < NTL else SEQ
                act.wait_ge(mx.sem, i + 1)
                ex.on(nc.scalar.activation(sc[:, i % SCORE_BUFS, k0:TOK], sc[:, i % SCORE_BUFS, k0:TOK], ACT.Exp,
                                           bias=st[:, i % 4, 0:1], accum_out=st[:, i % 4, 1:2]))
            copy_t(N - 2)
            copy_t(N - 1)

        @block.tensor
        def _(pe):
            def turn_bias():
                pe.wait_ge(loads.sem, loads.n)
                for b in range(2 * NH):
                    h, j = b // 2, 8 * (b % 2)
                    if b >= 3:
                        pe.wait_ge(biased.sem, b - 2)
                    turned.on(nc.tensor.matmul(m.bank[4 + b % 3][:, :], flip[:, :],
                                               falling[:, h, j:j + 8, :].rearrange("p j c -> p (j c)"),
                                               start=True, stop=True))
                pe.wait_ge(biased.sem, 2 * NH)

            def scores(i):
                t, h = todo[i]
                r = slice(DH * (h % 2), DH * (h % 2) + DH)
                if i >= 2:
                    pe.wait_ge(sb_.sem, scaled[i - 2])
                q = qt[r, h // 2, t * P:(t + 1) * P]
                if t < NTL:
                    nc.tensor.matmul(m.bank[i % 2][:, :], q, kt[r, h // 2, 0:SEQ], start=True, stop=True)
                sm.on(nc.tensor.matmul(m.bank[2 + i % 2][:, 0:CTX], q, kt[r, h // 2, SEQ:TOK], start=True, stop=True))

            def transpose(i):
                t, _h = todo[i]
                pe.wait_ge(ex.sem, i + 1)
                if i >= 1:
                    pe.wait_ge(pc.sem, 2 * i - 1)
                for n in range(0 if t < NTL else NTL, NT):
                    dst = turned_bank(i, n // NTL)[:, (n % NTL) * P:(n % NTL + 1) * P]
                    last = nc.tensor.transpose(dst, sc[:, i % SCORE_BUFS, n * P:(n + 1) * P], m.ident[:, :])
                tp.on(last)

            def weighted(i):
                t, h = todo[i]
                tiles_k = range(NT) if t < NTL else range(NTL, NT)
                pe.wait_ge(pc.sem, 2 * (i + 1))
                if i >= 1:
                    pe.wait_ge(od.sem, i)
                for n, kt_ in enumerate(tiles_k):
                    last = nc.tensor.matmul(m.bank[7][:, 0:DH], pt[:, i % 2, kt_ * P:(kt_ + 1) * P],
                                            v[:, kt_, h * DH:(h + 1) * DH], start=(n == 0), stop=(n == len(tiles_k) - 1))
                om.on(last)

            if not n_ctx:
                turn_bias()
            scores(0)
            scores(1)
            for i in range(N):
                if i + 2 < N:
                    scores(i + 2)
                if i >= 1:
                    weighted(i - 1)
                transpose(i)
                if i == n_ctx - 2:
                    pe.wait_ge(pc.sem, 2 * (i + 1))
                    turn_bias()
            weighted(N - 1)


def spans_of(tiles):
    return [(0, 0, SEQ)] + ([(1, SEQ, CTX)] if len(tiles) > NTL else [])


def stage_conv_fourier(m, a, l, cb, cc, cx, fz, y, tiles, tables):
    nc = m.nc
    with Stage(m) as s:
        z = s.sb("conv_z", [P, 2, TOK + 4])
        w = s.sb("conv_w", [P, 2, 3])
        pf = s.sb("dft_positions", [P, 2, 2, TOK])
        tab, ch_ = [dst for _name, dst in tables[:2]], tables[2][1]
        loads, ch, fin = s.sem("conv_w_loaded"), s.sem("conv_chain"), s.sem("conv_done")
        tp, cv = s.sem("conv_transposed"), s.sem("conv_copied")
        mm, cp, om, oc = (s.sem(n) for n in ("pos_mm", "pos_copied", "chan_mm", "four_copied"))
        spans = spans_of(tiles)
        block = s.block()
        first = [(st, t0, n, f, c) for st, t0, n in spans for f in range(2) for c in range(2)]

        @block.sync
        def _(sp):
            loads.on(sp.dma_start(w[:, :, :], a["conv_w"][l]), 16)

        @block.vector
        def _(dve):
            for n in range(2):
                ch.on(nc.vector.memset(z[:, n, :], 0.0))
            dve.wait_ge(ch.sem, ch.n)
            dve.wait_ge(loads.sem, 16)
            for f in range(2):
                for st, t0, n in spans:
                    z0 = t0 + 1 + 2 * st
                    t = slice(t0, t0 + n)
                    done(dve, ch, nc.vector.tensor_tensor(z[:, f, z0:z0 + n], cc[:, f, t], cx[:, f, t], ALU.mult))
                    done(dve, ch, nc.vector.tensor_scalar(cx[:, f, t], z[:, f, z0 - 1:z0 - 1 + n], w[:, f, 0:1], None, ALU.mult))
                    for j in (1, 2):
                        done(dve, ch, nc.vector.scalar_tensor_tensor(out=cx[:, f, t], in0=z[:, f, z0 - 1 + j:z0 - 1 + j + n],
                                                                     scalar=w[:, f, j:j + 1], in1=cx[:, f, t],
                                                                     op0=ALU.mult, op1=ALU.add))
                    fin.on(nc.vector.tensor_tensor(cx[:, f, t], cx[:, f, t], cb[:, f, t], ALU.mult))

        @block.tensor
        def _(pe):
            for i, (st, t0, n, f, c) in enumerate(first):
                if i >= 4:
                    pe.wait_ge(cp.sem, i - 3)
                for lt in range(n // P):
                    last = nc.tensor.matmul(m.bank[i % 4][:, :n], fz[:, t0 // P + lt, f * P:(f + 1) * P],
                                            tab[st][:, lt, c, :], start=(lt == 0), stop=(lt == n // P - 1))
                mm.on(last)
            pe.wait_ge(cp.sem, len(first))
            for i, t in enumerate(tiles):
                if i >= 4:
                    pe.wait_ge(oc.sem, i - 3)
                for f in range(2):
                    for c in range(2):
                        last = nc.tensor.matmul(m.bank[4 + i % 4][:, f * P:(f + 1) * P], pf[:, f, c, t * P:(t + 1) * P],
                                                ch_[:, c, :], start=(c == 0), stop=(c == 1))
                om.on(last)
            pe.wait_ge(fin.sem, 2 * len(spans))
            for i, t in enumerate(tiles):
                if i >= 4:
                    pe.wait_ge(cv.sem, i - 3)
                for f in range(2):
                    last = nc.tensor.transpose(m.bank[i % 4][:, f * P:(f + 1) * P], cx[:, f, t * P:(t + 1) * P], m.ident[:, :])
                tp.on(last)

        @block.scalar
        def _(act):
            for i, (st, t0, n, f, c) in enumerate(first):
                act.wait_ge(mm.sem, i + 1)
                cp.on(nc.scalar.activation(pf[:, f, c, t0:t0 + n], m.bank[i % 4][:, :n], ACT.Copy))
            for i, t in enumerate(tiles):
                act.wait_ge(om.sem, i + 1)
                oc.on(nc.scalar.activation(y[:, t, 2 * GW:3 * GW], m.bank[4 + i % 4][:, 0:GW], ACT.Copy))
            for i, t in enumerate(tiles):
                act.wait_ge(tp.sem, i + 1)
                cv.on(nc.scalar.activation(y[:, t, GW:2 * GW], m.bank[i % 4][:, 0:GW], ACT.Copy))


def reversed_columns(ap3, f, n):
    v = ap3[:, f, n - 1:n]
    return bass.AP(tensor=v.tensor, offset=v.offset, ap=[v.ap[0], [-1, n]])


class S5Weights:

    def __init__(self, s, m, a, l, seeds, tmp, wide, lc, base):
        self.m, self.a, self.l = m, a, l
        self.seeds, self.tmp, self.wide, self.lc, self.base = seeds, tmp, wide, lc, base
        self.pr = s.sb("s5_params", [P, 3, UNITS])
        self.bw = s.sb("s5_b", [P, 2, UNITS, 16])
        self.cw = s.sb("s5_c", [P, 2, UNITS, 16])
        self.bb = s.sb("s5_b_bar", [P, 3, UNITS, 16])
        self.bt = s.sb("base_tmp", [P, 2, UNITS, BASE // 2])
        self.loads, self.chain, self.placed = s.sem("s5_loaded"), s.sem("s5_chain"), s.sem("s5_placed")

    def sync(self, sp):
        a, l = self.a, self.l
        self.loads.on(sp.dma_start(self.pr[:, :, :], a["s5_params"][l]), 16)
        self.loads.on(sp.dma_start(self.bw[:, :, :, :], a["s5_b"][l]), 16)
        self.loads.on(sp.dma_start(self.cw[:, :, :, :], a["s5_c"][l]), 16)

    def vector(self, dve):
        V = self.m.nc.vector
        ch, wd, loads, K = self.chain, self.placed, self.loads, 10
        pr, bw, cw, bb, tmp, seeds, wide, lc, base, bt = (self.pr, self.bw, self.cw, self.bb, self.tmp, self.seeds,
                                                        self.wide, self.lc, self.base, self.bt)
        T = lambda i: tmp[:, i, :]

        def tt(o, x, z, op):
            done(dve, ch, V.tensor_tensor(o, x, z, op))

        def ts(o, x, s1, op0, s2=None, op1=None):
            done(dve, ch, V.tensor_scalar(o, x, s1, s2, op0, op1) if op1 else V.tensor_scalar(o, x, s1, None, op0))

        def stt(o, x, c, z, op0, op1):
            done(dve, ch, V.scalar_tensor_tensor(out=o, in0=x, scalar=c, in1=z, op0=op0, op1=op1))

        def real_expm1(o, x):
            ts(x, x, 2.0 ** -K, ALU.mult)
            ts(o, x, 1.0 / 4, ALU.mult, 1.0, ALU.add)
            for c in (3, 2):
                tt(o, o, x, ALU.mult)
                ts(o, o, 1.0 / c, ALU.mult, 1.0, ALU.add)
            tt(o, o, x, ALU.mult)
            for _ in range(K):
                stt(o, o, 2.0, o, ALU.add, ALU.mult)

        ch.on(V.memset(wide, 0.0))
        ch.on(V.memset(lc, 0.0))
        dve.wait_ge(loads.sem, loads.n)
        dve.wait_ge(ch.sem, ch.n)
        a_re, a_im, log_dt = pr[:, 0, :], pr[:, 1, :], pr[:, 2, :]
        dt, x, th, mr, mi, er, w2 = (T(i) for i in range(7))
        ts(x, log_dt, -1.0, ALU.mult)
        real_expm1(dt, x)
        ts(dt, dt, 1.0, ALU.add)
        done(dve, ch, V.reciprocal(dt, dt))
        tt(x, a_re, dt, ALU.mult)
        real_expm1(er, x)
        tt(th, a_im, dt, ALU.mult)
        ts(th, th, 2.0 ** -K, ALU.mult)
        tt(w2, th, th, ALU.mult)
        ts(mr, w2, -1.0 / 30, ALU.mult, 1.0, ALU.add)
        tt(mr, mr, w2, ALU.mult)
        ts(mr, mr, -1.0 / 12, ALU.mult, 1.0, ALU.add)
        tt(mr, mr, w2, ALU.mult)
        ts(mr, mr, -0.5, ALU.mult)
        ts(mi, w2, -1.0 / 20, ALU.mult, 1.0, ALU.add)
        tt(mi, mi, w2, ALU.mult)
        ts(mi, mi, -1.0 / 6, ALU.mult, 1.0, ALU.add)
        tt(mi, mi, th, ALU.mult)
        for _ in range(K):
            tt(w2, mi, mi, ALU.mult)
            stt(mi, mr, 1.0, mi, ALU.add, ALU.mult)
            ts(mi, mi, 2.0, ALU.mult)
            stt(mr, mr, 2.0, mr, ALU.add, ALU.mult)
            tt(mr, mr, w2, ALU.subtract)
        nr, ni, den, fr, fi, t1 = (T(i) for i in range(7, 13))
        stt(nr, er, 1.0, mr, ALU.add, ALU.mult)
        tt(nr, nr, er, ALU.add)
        stt(ni, er, 1.0, mi, ALU.add, ALU.mult)
        tt(den, a_re, a_re, ALU.mult)
        tt(t1, a_im, a_im, ALU.mult)
        tt(den, den, t1, ALU.add)
        done(dve, ch, V.reciprocal(den, den))
        tt(fr, nr, a_re, ALU.mult)
        tt(t1, ni, a_im, ALU.mult)
        tt(fr, fr, t1, ALU.add)
        tt(fr, fr, den, ALU.mult)
        tt(fi, ni, a_re, ALU.mult)
        tt(t1, nr, a_im, ALU.mult)
        tt(fi, fi, t1, ALU.subtract)
        tt(fi, fi, den, ALU.mult)
        wide_f = lambda f: bcast(f.unsqueeze(2), [P, UNITS, 16])
        for o, f0, f1, op in ((0, fr, fi, ALU.subtract), (1, fi, fr, ALU.add)):
            tt(bb[:, o, :, :], bw[:, 0, :, :], wide_f(f0), ALU.mult)
            tt(bb[:, 2, :, :], bw[:, 1, :, :], wide_f(f1), ALU.mult)
            tt(bb[:, o, :, :], bb[:, o, :, :], bb[:, 2, :, :], op)
        for un in range(UNITS):
            d, f, j = un // 8, (un % 8) // 4, un % 4
            for half in range(2):
                r, c0 = slice(64 * half, 64 * half + 64), 16 * half
                wd.on(V.tensor_copy(wide[r, d, f, :, j, c0:c0 + 16], bb[r, 0:2, un, :]))
                wd.on(V.tensor_copy(lc[r, 0, un, c0:c0 + 16], cw[r, 0, un, :]))
                wd.on(V.tensor_scalar(lc[r, 1, un, c0:c0 + 16], cw[r, 1, un, :], -1.0, None, ALU.mult))
        ts(seeds[:, 0, 0, :], mr, 1.0, ALU.add)
        ts(seeds[:, 0, 1, :], mi, 1.0, ALU.mult)
        for j in range(NS):
            cr, ci = seeds[:, j, 0, :], seeds[:, j, 1, :]
            if j:
                pr_, pi_ = seeds[:, j - 1, 0, :], seeds[:, j - 1, 1, :]
                tt(cr, pr_, pr_, ALU.mult)
                tt(t1, pi_, pi_, ALU.mult)
                tt(cr, cr, t1, ALU.subtract)
                stt(ci, pr_, 2.0, pi_, ALU.mult, ALU.mult)
            tt(x, cr, cr, ALU.mult)
            tt(t1, ci, ci, ALU.mult)
            tt(x, x, t1, ALU.add)
            ts(x, x, -0.5, ALU.mult, 1.5, ALU.add)
            tt(cr, cr, x, ALU.mult)
            tt(ci, ci, x, ALU.mult)
            ts(seeds[:, j, 2, :], ci, -1.0, ALU.mult)
        ts(er, er, 1.0, ALU.add)
        done(dve, ch, V.memset(base[:, 0, :, 0:1], 1.0))
        done(dve, ch, V.memset(base[:, 1, :, 0:1], 0.0))
        n, j = 1, 0
        while n < BASE:
            c0, s0 = base[:, 0, :, 0:n], base[:, 1, :, 0:n]
            E = [bcast(seeds[:, j, q, :].unsqueeze(2), [P, UNITS, n]) for q in range(2)]
            t0, t1 = bt[:, 0, :, 0:n], bt[:, 1, :, 0:n]
            for o, e0, e1, op in ((0, 0, 1, ALU.subtract), (1, 1, 0, ALU.add)):
                tt(t0, c0, E[e0], ALU.mult)
                tt(t1, s0, E[e1], ALU.mult)
                tt(base[:, o, :, n:2 * n], t0, t1, op)
            n, j = 2 * n, j + 1


def stage_s5(m, a, l, u, y, tiles, seeds, radius, wide, lc, base, ht):
    nc = m.nc
    order = [d * 8 + 4 * f + j for f in range(2) for d in range(2) for j in range(4)]
    with Stage(m) as s:
        tab = ht[:, 0:4, :].rearrange("p (a c) t -> p a c t", a=2)
        bu = ht[:, 4:8, :].rearrange("p (a c) t -> p a c t", a=2)
        wr, g_, pr = (m.part(i, "q t", q=q, t=TOK) for i, q in ((0, 2), (2 * TOK, 2), (4 * TOK, 4)))
        yf = m.part(8 * TOK, "f t", f=2, t=TOK)
        gl, sg = (m.part(10 * TOK + i * 2 * GW, "f n", f=2, n=GW) for i in (0, 1))
        lb = s.sb("s5_b_lhsT", [P, 8, P])
        dsk = s.sb("s5_d", [P, 2])
        tt_ = s.sb("table_tmp", [P, 2, 2, 256])
        junk, sq = s.sb("group_squares_junk", [P, GW]), s.sem("group_squares")
        finished = [(t, g) for t in tiles for g in range(3)]
        loads, tp, lbc, tb, bm, be, ch, pd, ym, tch = (s.sem(n) for n in (
            "s5w_loaded", "b_transposed", "b_copied", "table_done", "drive_mm", "drive_copied", "scan_chain",
            "products_done", "readout_done", "table_chain"))
        ta, tsum = s.sem("table_part_done"), s.sem("table_step_done")
        steps, n_ = [], BASE
        while n_ < TOK:
            steps.append((n_, min(n_, TOK - n_), n_.bit_length() - 1))
            n_ += steps[-1][1]
        S = len(steps) + 1
        sk, ge, gm, gt, si, go = (s.sem(n) for n in ("skip_added", "gelu_done", "glu_mm", "gelu_T", "sigmoid_done",
                                                     "glu_done"))
        ada = None
        if l + 1 < DEPTH:
            slots = [m.part(8 * TOK + 2 * TOK + 4 * GW, "k n", k=KC, n=256), s.sb("ada_w", [P, KC, 256])[:, :, :]]
            ada = Modulation(s, m, a, l + 1, slots, 2, (5,))
        drive = [[m.bank[2 * i], m.bank[2 * i + 1], m.bank[4]] for i in range(2)]
        read_lat, read_ctx = m.bank[6], m.bank[7]
        block = s.block()

        @block.sync
        def _(sp):
            loads.on(sp.dma_start(dsk[:, :], a["s5_d"][l]), 16)
            loads.on(sp.dma_start(gl, a["s5_w_glu"][l].rearrange("(f p) n -> p f n", p=P)), 16)
            if ada:
                ada.sync_group(sp, 0)
                ada.sync_small(sp)
                for g in range(1, ada.GROUPS):
                    ada.sync_group(sp, g)
                ada.store(sp, 0, N_MOD)

        @block.gpsimd
        def _(pool):
            G = nc.gpsimd
            for i, un in enumerate(order):
                c, sn = tab[:, i % 2, 0, :], tab[:, i % 2, 1, :]
                if i >= 2:
                    pool.wait_ge(pd.sem, 4 * (i - 1))
                tch.on(G.tensor_copy(c[:, 0:BASE], base[:, 0, un, :]))
                last = G.tensor_copy(sn[:, 0:BASE], base[:, 1, un, :])
                tch.on(last)
                pool.wait_ge(tch.sem, tch.n)
                tsum.on(pool.nop())
                for k, (n, w, j) in enumerate(steps):
                    for o in range(2):
                        tch.on(G.tensor_scalar(tt_[:, o, 0, :w], c[:, 0:w], seeds[:, j, o, un:un + 1], 1.0,
                                               ALU.mult, ALU.mult))
                    pool.wait_ge(ta.sem, 2 * (len(steps) * i + k + 1))
                    pool.wait_ge(tch.sem, tch.n)
                    tch.on(G.tensor_tensor(c[:, n:n + w], tt_[:, 0, 0, :w], tt_[:, 0, 1, :w], ALU.add))
                    tch.on(G.tensor_tensor(sn[:, n:n + w], tt_[:, 1, 0, :w], tt_[:, 1, 1, :w], ALU.add))
                    pool.wait_ge(tch.sem, tch.n)
                    tsum.on(pool.nop())
                tb.on(pool.nop())

        @block.tensor
        def _(pe):
            for d in range(2):
                for f in range(2):
                    for c in range(2):
                        k = 4 * d + 2 * f + c
                        last = nc.tensor.transpose(m.bank[k // 4][:, (k % 4) * P:(k % 4 + 1) * P],
                                                   wide[:, d, f, c, :, :].rearrange("p j h -> p (j h)"), m.ident[:, :])
                tp.on(last)
            pe.wait_ge(lbc.sem, 2)

            def drives(i):
                un = order[i]
                d, f, j = un // 8, (un % 8) // 4, un % 4
                q = slice(32 * j, 32 * j + 32)
                if i >= 1:
                    pe.wait_ge(be.sem, i)
                if d == 0:
                    cx_, lt = u[q, f, SEQ:TOK], u[q, f, 0:SEQ]
                else:
                    cx_ = bass.AP(tensor=u.tensor, offset=u[q, f, TOK - 1:TOK].offset, ap=[u[q, f, 0:1].ap[0], [-1, CTX]])
                    lt = bass.AP(tensor=u.tensor, offset=u[q, f, SEQ - 1:SEQ].offset, ap=[u[q, f, 0:1].ap[0], [-1, SEQ]])
                D_ = drive[i % 2]
                for c in range(2):
                    lhs = lb[q, 4 * d + 2 * f + c, :]
                    nc.tensor.matmul(D_[2][:, c * CTX:(c + 1) * CTX], lhs, cx_, start=True, stop=True)
                    last = nc.tensor.matmul(D_[c][:, :], lhs, lt, start=True, stop=True)
                bm.on(last)

            def readout(i):
                un = order[i]
                d, j = un // 8, un % 4
                o = slice(32 * j, 32 * j + 32)
                lat, cx_ = ((CTX, 0), (0, SEQ))[d]
                if i == 8:
                    pe.wait_ge(sk.sem, 2)
                for q in range(4):
                    pe.wait_ge(pd.sem, 4 * i + q + 1)
                    lhs = lc[:, q % 2, un, :]
                    first, last_ = d == 0 and q == 0, d == 1 and q == 3
                    nc.tensor.matmul(read_lat[o, :], lhs, pr[:, q, lat:lat + SEQ], start=first, stop=last_)
                    last = nc.tensor.matmul(read_ctx[o, 0:CTX], lhs, pr[:, q, cx_:cx_ + CTX], start=first, stop=last_)
                ym.on(last)

            drives(0)
            drives(1)
            for i in range(UNITS):
                if i + 2 < UNITS:
                    drives(i + 2)
                if ada and i < ada.GROUPS:
                    ada.tensor_group(pe, i)
                readout(i)
            pe.wait_ge(ge.sem, 2)
            pe.wait_ge(loads.sem, loads.n)
            for i, t in enumerate(tiles):
                if i >= 2:
                    pe.wait_ge(go.sem, i - 1)
                for f in range(2):
                    last = nc.tensor.matmul(m.bank[i % 2][:, 0:GW], yf[:, f, t * P:(t + 1) * P], gl[:, f, :],
                                            start=(f == 0), stop=(f == 1))
                gm.on(last)
                for f in range(2):
                    last = nc.tensor.transpose(m.bank[2 + i % 2][:, f * P:(f + 1) * P], yf[:, f, t * P:(t + 1) * P],
                                               m.ident[:, :])
                gt.on(last)

        @block.scalar
        def _(act):
            for k in range(2):
                act.wait_ge(tp.sem, k + 1)
                lbc.on(act.activation(lb[:, 4 * k:4 * k + 4, :], m.bank[k][:, :].rearrange("p (b n) -> p b n", b=4), ACT.Copy))
            for i in range(UNITS):
                act.wait_ge(bm.sem, i + 1)
                if i >= 2:
                    act.wait_ge(ch.sem, 8 * (i - 2) + 5)
                for c in range(2):
                    act.activation(bu[:, i % 2, c, 0:CTX], drive[i % 2][2][:, c * CTX:(c + 1) * CTX], ACT.Copy)
                    last = act.activation(bu[:, i % 2, c, CTX:TOK], drive[i % 2][c][:, :], ACT.Copy)
                be.on(last)
                for k, (n, w, j) in enumerate(steps):
                    act.wait_ge(tsum.sem, S * i + k + 1)
                    for o, q in ((0, 2), (1, 0)):
                        ta.on(act.activation(tt_[:, o, 1, :w], tab[:, i % 2, 1, 0:w], ACT.Copy,
                                             scale=seeds[:, j, q, order[i]:order[i] + 1]))
                for t, g in finished[len(finished) * i // UNITS:len(finished) * (i + 1) // UNITS]:
                    done(act, sq, nc.scalar.activation(junk[:, :], y[:, t, g * GW:(g + 1) * GW], ACT.Square,
                                                       accum_out=m.gsq[:, t, g:g + 1]))
            for f in range(2):
                act.wait_ge(sk.sem, 2 * (f + 1))
                ge.on(nc.scalar.activation(yf[:, f, :], yf[:, f, :], ACT.Gelu_apprx_tanh))
            for i, t in enumerate(tiles):
                act.wait_ge(gm.sem, i + 1)
                if i >= 2:
                    act.wait_ge(go.sem, i - 1)
                si.on(nc.scalar.activation(sg[:, i % 2, :], m.bank[i % 2][:, 0:GW], ACT.Sigmoid))

        @block.vector
        def _(dve):
            V = nc.vector
            if ada:
                ada.vector_start(dve)
            dve.wait_ge(loads.sem, loads.n)
            for i, un in enumerate(order):
                c, sn = tab[:, i % 2, 0, :], tab[:, i % 2, 1, :]
                if ada and 1 <= i <= ada.GROUPS:
                    ada.vector_group(dve, i - 1)
                b = bu[:, i % 2, :, :]
                dve.wait_ge(be.sem, i + 1)
                dve.wait_ge(tb.sem, i + 1)
                if i:
                    dve.wait_ge(pd.sem, 4 * i)
                out = [pr[:, q, :] if un < 8 else reversed_columns(pr, q, TOK) for q in range(4)]
                r = bcast(radius[:, un:un + 1], [P, TOK])
                before = ch.n

                def after(k):
                    dve.wait_ge(ch.sem, before + k)

                ch.on(V.tensor_tensor(wr[:, 0, :], b[:, 0, :], c, ALU.mult))
                ch.on(V.tensor_tensor(g_[:, 0, :], b[:, 1, :], sn, ALU.mult))
                ch.on(V.tensor_tensor(wr[:, 1, :], b[:, 1, :], c, ALU.mult))
                after(2)
                ch.on(V.tensor_tensor(wr[:, 0, :], wr[:, 0, :], g_[:, 0, :], ALU.add))
                ch.on(V.tensor_tensor(g_[:, 1, :], b[:, 0, :], sn, ALU.mult))
                after(4)
                ch.on(V.tensor_tensor_scan(out=g_[:, 0, :], data0=r, data1=wr[:, 0, :], initial=0.0,
                                           op0=ALU.mult, op1=ALU.add))
                after(5)
                ch.on(V.tensor_tensor(wr[:, 1, :], wr[:, 1, :], g_[:, 1, :], ALU.subtract))
                after(6)
                if i:
                    dve.wait_ge(ym.sem, i)
                pd.on(V.tensor_tensor(out[0], g_[:, 0, :], c, ALU.mult))
                after(7)
                ch.on(V.tensor_tensor_scan(out=g_[:, 1, :], data0=r, data1=wr[:, 1, :], initial=0.0,
                                           op0=ALU.mult, op1=ALU.add))
                pd.on(V.tensor_tensor(out[1], g_[:, 0, :], sn, ALU.mult))
                after(8)
                pd.on(V.scalar_tensor_tensor(out=out[2], in0=g_[:, 1, :], scalar=-1.0, in1=sn, op0=ALU.mult, op1=ALU.mult))
                pd.on(V.tensor_tensor(out[3], g_[:, 1, :], c, ALU.mult))
                if i in (7, 15):
                    f = i // 8
                    dve.wait_ge(ym.sem, i + 1)
                    sk.on(V.scalar_tensor_tensor(out=yf[:, f, 0:SEQ], in0=u[:, f, 0:SEQ], scalar=dsk[:, f:f + 1],
                                                 in1=read_lat[:, :], op0=ALU.mult, op1=ALU.add))
                    sk.on(V.scalar_tensor_tensor(out=yf[:, f, SEQ:TOK], in0=u[:, f, SEQ:TOK], scalar=dsk[:, f:f + 1],
                                                 in1=read_ctx[:, 0:CTX], op0=ALU.mult, op1=ALU.add))
            for i, t in enumerate(tiles):
                dve.wait_ge(si.sem, i + 1)
                dve.wait_ge(gt.sem, i + 1)
                go.on(V.tensor_tensor(y[:, t, 3 * GW:4 * GW], m.bank[2 + i % 2][:, 0:GW], sg[:, i % 2, :], ALU.mult))


def stage_merge(m, a, l, rows, y, yt, tiles):
    nc = m.nc
    n = len(tiles)
    with Stage(m) as s:
        w = m.part(0, "k d", k=KC, d=D)
        gg = s.sb("group_gains", [P, D])
        junk, ssq = s.sb("squares", [P, D]), m.gsq
        prod = s.sb("gated", [P, D])
        w_in, g_in = s.sem("w_out_loaded"), s.sem("gains_loaded")
        sq, xsq, ms, rt, yn, tp, ev, mm, add = (s.sem(x) for x in ("g_squares_done", "x_squares_done", "g_mean", "g_root", "y_normed",
                                                              "y_transposed", "y_copied", "out_mm", "x_added"))
        block = s.block()

        @block.sync
        def _(sp):
            g_in.on(sp.dma_start(gg[:, :], a["grp_g"][l:l + 1, :].broadcast_to([P, D])), 16)
            w_in.on(sp.dma_start(w[:, :, :], a["w_out"][l].rearrange("(k p) n -> p k n", p=P)), 16)

        @block.scalar
        def _(act):
            for t in tiles:
                done(act, sq, nc.scalar.activation(junk[:, 0:GW], y[:, t, 3 * GW:4 * GW], ACT.Square,
                                                   accum_out=ssq[:, t, 3:4]))
            act.wait_ge(ms.sem, 2)
            rt.on(nc.scalar.activation(ssq[:, :n, :], ssq[:, :n, :], ACT.Sqrt))
            for i, t in enumerate(tiles):
                for c in range(2):
                    act.wait_ge(tp.sem, 2 * i + c + 1)
                    ev.on(nc.scalar.activation(yt[:, 4 * c:4 * c + 4, t * P:(t + 1) * P],
                                               m.bank[(2 * i + c) % 4][:, :].rearrange("p (k n) -> p k n", k=4),
                                               ACT.Copy))
            for i, t in enumerate(tiles):
                act.wait_ge(add.sem, 4 * (i + 1))
                done(act, xsq, nc.scalar.activation(junk[:, :], m.x[:, t, :], ACT.Square, accum_out=m.ssq[:, t:t + 1]))

        @block.vector
        def _(dve):
            V = nc.vector
            dve.wait_ge(sq.sem, n)
            done(dve, ms, V.tensor_scalar(ssq[:, :n, :], ssq[:, :n, :], 1.0 / GW, EPS, ALU.mult, ALU.add))
            ms.on(V.reciprocal(ssq[:, :n, :], ssq[:, :n, :]))
            dve.wait_ge(rt.sem, 1)
            dve.wait_ge(g_in.sem, 16)
            for t in tiles:
                for g in range(4):
                    c = slice(g * GW, (g + 1) * GW)
                    yn.on(V.scalar_tensor_tensor(out=y[:, t, c], in0=y[:, t, c], scalar=ssq[:, t, g:g + 1],
                                                 in1=gg[:, c], op0=ALU.mult, op1=ALU.mult))
            for i, t in enumerate(tiles):
                for c in range(2):
                    dve.wait_ge(mm.sem, 2 * i + c + 1)
                    cols = slice(512 * c, 512 * c + 512)
                    done(dve, add, V.tensor_tensor(prod[:, cols], m.bank[4 + (2 * i + c) % 4][:, :],
                                                   rows[:, t // NTL, G1, cols], ALU.mult))
                    add.on(V.tensor_tensor(m.x[:, t, cols], m.x[:, t, cols], prod[:, cols], ALU.add))

        @block.tensor
        def _(pe):
            for i, t in enumerate(tiles):
                pe.wait_ge(yn.sem, 4 * (i + 1))
                for c in range(2):
                    u = 2 * i + c
                    if u >= 4:
                        pe.wait_ge(ev.sem, u - 3)
                    for k in range(4):
                        last = nc.tensor.transpose(m.bank[u % 4][:, k * P:(k + 1) * P],
                                                   y[:, t, (4 * c + k) * P:(4 * c + k + 1) * P], m.ident[:, :])
                    tp.on(last)
            pe.wait_ge(w_in.sem, 16)
            for i, t in enumerate(tiles):
                pe.wait_ge(ev.sem, 2 * (i + 1))
                for c in range(2):
                    u = 2 * i + c
                    if u >= 4:
                        pe.wait_ge(add.sem, 2 * (u - 3))
                    for k in range(KC):
                        last = nc.tensor.matmul(m.bank[4 + u % 4][:, :], yt[:, k, t * P:(t + 1) * P],
                                                w[:, k, 512 * c:512 * c + 512], start=(k == 0), stop=(k == KC - 1))
                    mm.on(last)


PAIRS = SLOTS // 2
RING0 = 6
WINDOW = PAIRS // PH
PRIME = 5


def stage_peer(m, a, l, rows, ht, w_view, tiles):
    nc = m.nc
    uv = a[f"peer_uv{l}"]
    with Stage(m) as s:
        n = len(tiles)
        rowf, hf = rows.rearrange("p s j d -> p (s j d)"), m.h[:, :, :].rearrange("p t d -> p (t d)")
        htf = ht.rearrange("p k t -> p (k t)")
        place = [buf[:, 2 * D * i:2 * D * (i + 1)] for buf, i in (
            (rowf, 1), (rowf, 4), (hf, 0), (hf, 1), (rowf, 2), (rowf, 3), (htf, 0), (htf, 1))]
        spare, late = rowf[:, 0:2 * D], hf[:, 4 * D:6 * D]
        turn_of = [6, 7, 2, 3, 4, 5, 0, 1]
        first_uses = [len(range(j, SLOTS, RING0)) if j < RING0 else 0 for j in range(RING)]
        qt = m.part(0, "b t", b=HALVES, t=TOK)
        prod = s.sb("gated_experts", [P, D])
        norm = Norm(s, m, rows, SC2, SH2, ht, tiles, (0, 1, 4, 5))
        wq = [w.rearrange("p (k n) -> p k n", n=GW) for w in (spare, late)]
        parts = [(P, min(SEQ, n * P - P))] + ([(P + SEQ, n * P - P - SEQ)] if n * P - P > SEQ else [])

        def products_of(w):
            rest = [[("rest", w + 1, z, k, c) for k in range(KC) for c in range(len(parts))] for z in range(2)]
            first = [("first", w + 2, z, k, 0) for z in range(2) for k in range(KC)] if w + 2 < PH else []
            todo = rest[0] + first + rest[1] if w + 1 < PH else []
            cost = [P if what[0] == "first" else parts[what[4]][1] for what in todo]
            shares = [[] for _ in range(WINDOW)]
            for i, what in enumerate(todo):
                shares[WINDOW * sum(cost[:i]) // sum(cost)].append(what)
            return shares

        shares = [share for w in range(PH) for share in products_of(w)]
        keys = s.sb("keys_T", [P, HALVES, PK])
        qs = s.sb("q_stage", [P, 2, 2, P])
        idx, idx_next = s.sb("idx", [P, SLOTS], U32), s.sb("idx_next", [P, SLOTS], U32)
        gate, gate_next = s.sb("gate", [P, SLOTS]), s.sb("gate_next", [P, PH, TOPK])
        top = s.sb("top_scores", [P, PH, TOPK])
        best = s.sb("best", [P, 2, TOPK])
        bi = s.sb("best_idx", [P, 2, TOPK], U32)
        bif = s.sb("best_idx_f", [P, 2, TOPK])
        work = s.sb("topk_work", [P, 2, PK])
        cand = s.sb("cand", [P, TOPK * TOPK])
        cwork = s.sb("cand_work", [P, TOPK * TOPK])
        pos, split = s.sb("cand_pos", [P, TOPK], U32), s.sb("pos_split", [P, 2, TOPK], U32)
        splitf = s.sb("pos_split_f", [P, 2, TOPK])
        hot = s.sb("one_hot", [P, 2, TOPK, TOPK])
        half = s.sb("half_idx", [P, 2, TOPK])
        red = s.sb("gate_sums", [P, PH, 2])
        junk = s.sb("dot_products", [P, 2, D], mybir.dt.bfloat16)
        dot, act_ = s.sb("dots", [P, 2, 2]), s.sb("gelu_dots", [P, 2, 2])
        diag = s.sb("diag_w", [P, 2, 2, P])
        hcur = s.sb("h_cur", [P, D])
        k_in = s.sem("keys_loaded")
        gathered, before = m.gathered, [g.n for g in m.gathered]
        ready, dots, gel, dg, used = (s.sem(x) for x in ("idx_ready", "dots_done", "gelu_done", "diag_done", "pair_used"))
        ch, issued, begun, acc_free = s.sem("topk_chain"), s.sem("pairs_begun"), s.sem("topk_begun"), s.sem("acc_free")
        qc, sc, tk = s.sem("q_staged"), s.sem("scores_done"), s.sem("scores_read")
        ex, exi, sq = s.sem("gates_exp"), s.sem("gates_shifted"), s.sem("x_squares_done")
        h_first = s.sem("h_first_taken")
        h_out, h_in, h_taken = s.sem("h_stored"), s.sem("h_next_loaded"), s.sem("h_next_taken")
        w_in, rest_mm, rest_cp = [s.sem(f"wq_loaded{j}") for j in range(2)], s.sem("rest_mm"), s.sem("rest_copied")
        ready0, mm0, cp0, sc0, tk0, exi0, ex0 = (s.sem(x) for x in (
            "idx0_ready", "first_mm", "first_staged", "scores0_done", "scores0_read", "gates0_shifted", "gates0_exp"))
        top0, red0 = s.sb("top_scores0", [P, TOPK]), s.sb("gate_sums0", [P, 2])
        acc = [m.bank[0], m.bank[1]]
        V = nc.vector
        block = s.block()

        def is_first(t):
            return type(t) is int and t == 0

        def scores_of(t, h):
            bank, c0 = (m.bank[2], 2 * PK) if is_first(t) else (m.bank[3] if is_next(t) else m.bank[2 + h % 2], 0)
            return [bank[:, c0 + z * PK:c0 + (z + 1) * PK] for z in range(2)]

        def is_next(t):
            return type(t) is int and t == 1

        class chain:

            def __init__(self, dve):
                self.dve, self.n = dve, 0
                dve.sem_clear(ch.sem)

            def __call__(self, ins):
                ins.then_inc(ch.sem, 1)
                self.n += 1
                self.dve.wait_ge(ch.sem, self.n)

            def beside(self, ins):
                ins.then_inc(ch.sem, 1)
                self.n += 1
                if self.n > 1:
                    self.dve.wait_ge(ch.sem, self.n - 1)

        def topk_halves(dve, t, h):
            c = chain(dve)
            if is_first(t):
                dve.wait_ge(sc0.sem, h + 1)
            else:
                dve.wait_ge(sc.sem, t * PH + (h + 1 - PH))
            dve.sem_inc(begun.sem, 1)
            sv = scores_of(t, h)
            lo, hi = [best[:, z, 0:8] for z in range(2)], [best[:, z, 8:16] for z in range(2)]
            for z in range(2):
                c.beside(V.max(lo[z], sv[z]))
            for z in range(2):
                c.beside(V.match_replace(work[:, z, :], lo[z], sv[z], -3.0e38))
            for z in range(2):
                c.beside(V.max(hi[z], work[:, z, :]))
            for z in range(2):
                c.beside(V.max_index(bi[:, z, 0:8], lo[z], sv[z]))
            for z in range(2):
                last = V.max_index(bi[:, z, 8:16], hi[z], work[:, z, :])
                if z == 0:
                    c.beside(last)
            c(last)
            (tk0 if is_first(t) else tk).on(V.tensor_copy(bif[:, :, :], bi[:, :, :]))

        def topk_cross(dve, t, h):
            c = chain(dve)
            c(V.tensor_tensor(cand[:, :].rearrange("p (i j) -> p i j", i=TOPK),
                              bcast(best[:, 0, :].unsqueeze(2), [P, TOPK, TOPK]),
                              bcast(best[:, 1, :].unsqueeze(1), [P, TOPK, TOPK]), ALU.add))
            best_sums = top0[:, :] if is_first(t) else top[:, h, :]
            lo, hi = best_sums[:, 0:8], best_sums[:, 8:16]
            c(V.max(lo, cand[:, :]))
            c.beside(V.match_replace(cwork[:, :], lo, cand[:, :], -3.0e38))
            c.beside(V.max_index(pos[:, 0:8], lo, cand[:, :]))
            c(V.max(hi, cwork[:, :]))
            c(V.max_index(pos[:, 8:16], hi, cwork[:, :]))

        def topk_index(dve, t, h):
            c = chain(dve)
            c.beside(V.tensor_scalar(split[:, 0, :], pos[:, :], 4, None, ALU.logical_shift_right))
            c(V.tensor_scalar(split[:, 1, :], pos[:, :], 15, None, ALU.bitwise_and))
            c(V.tensor_copy(splitf[:, :, :], split[:, :, :]))
            for z in range(2):
                c.beside(V.tensor_tensor(hot[:, z, :, :], bcast(splitf[:, z, :].unsqueeze(2), [P, TOPK, TOPK]),
                                         bcast(m.iota[:, :].unsqueeze(1), [P, TOPK, TOPK]), ALU.is_equal))
            for z in range(2):
                c.beside(V.tensor_tensor(hot[:, z, :, :], hot[:, z, :, :],
                                         bcast(bif[:, z, :].unsqueeze(1), [P, TOPK, TOPK]), ALU.mult))
            c.beside(V.tensor_reduce(out=half[:, 0, :], in_=hot[:, 0, :, :], axis=AX.X, op=ALU.add))
            c(V.tensor_reduce(out=half[:, 1, :], in_=hot[:, 1, :, :], axis=AX.X, op=ALU.add))
            last = V.scalar_tensor_tensor(out=(idx if is_first(t) else idx_next)[:, h * TOPK:(h + 1) * TOPK],
                                          in0=half[:, 0, :], scalar=float(PK), in1=half[:, 1, :],
                                          op0=ALU.mult, op1=ALU.add)
            if is_first(t):
                done(dve, ready0, last)
                exi0.on(V.tensor_scalar(gate[:, h * TOPK:(h + 1) * TOPK], top0[:, :], top0[:, 0:1], None, ALU.subtract))
            else:
                c(last)

        def gate0_norm(dve, h):
            c = chain(dve)
            g = gate[:, h * TOPK:(h + 1) * TOPK]
            dve.wait_ge(ex0.sem, h + 1)
            c(V.tensor_reduce(out=red0[:, 0:1], in_=g, axis=AX.X, op=ALU.add))
            c(V.reciprocal(red0[:, 1:2], red0[:, 0:1]))
            c(V.tensor_scalar(g, g, red0[:, 1:2], None, ALU.mult))

        TOPK_PARTS = 3

        def topk_part(dve, t, part):
            h, k = divmod(part, TOPK_PARTS)
            (topk_halves, topk_cross, topk_index)[k](dve, t, h)

        def gates_shift(dve, t):
            exi.on(V.tensor_tensor(gate_next[:, :, :], top[:, :, :], bcast(top[:, :, 0:1], [P, PH, TOPK]),
                                   ALU.subtract))

        def gates_norm(dve, t):
            c = chain(dve)
            dve.wait_ge(ex.sem, t * 1)
            c(V.tensor_reduce(out=red[:, :, 0:1], in_=gate_next[:, :, :], axis=AX.X, op=ALU.add))
            c(V.reciprocal(red[:, :, 1:2], red[:, :, 0:1]))
            c(V.tensor_tensor(gate_next[:, :, :], gate_next[:, :, :], bcast(red[:, :, 1:2], [P, PH, TOPK]), ALU.mult))

        HALF = SLOTS // 2

        def publish(eng, part):
            c = slice(part * HALF, (part + 1) * HALF)
            ready.on(V.tensor_copy(idx[:, c], idx_next[:, c]))

        def place_of(t, sl):
            if is_first(t):
                j = sl % RING0
                return j, before[j] + 16 * (sl // RING0 + 1)
            j = turn_of[sl % RING]
            base = before[j] + 16 * (first_uses[j] + sl // RING + 1)
            return j, t * (16 * SLOTS // RING) + (base - 16 * SLOTS // RING)

        def heads_at(t):
            return [WINDOW * h if is_first(t) else 4 * h for h in range(PH)]

        def first_heads_at(p):
            return [(h, part) for h in range(1, PH) for part in range(TOPK_PARTS)
                    if p == max(0, WINDOW * (h - 1) - 2 + part)]

        def pool_tile(pool, t):
            for p in range(PAIRS):
                if is_first(t):
                    if p % WINDOW == 0:
                        pool.wait_ge(ready0.sem, p // WINDOW + 1)
                elif p in (0, PAIRS // 2):
                    pool.wait_ge(ready.sem, t * 2 + (-1 + (p > 0)))
                depth = (RING0 if is_first(t) else RING) // 2
                if not is_first(t) or p >= depth:
                    pool.wait_ge(used.sem, t * PAIRS + (PRIME + p - depth + 1))
                elif p == 0:
                    pool.wait_ge(h_out.sem, 16 * n)
                    pool.wait_ge(h_first.sem, 1)
                    pool.wait_ge(norm.turned.sem, 2 * n)
                pool.sem_inc(issued.sem, 1)
                for j in range(2):
                    sl = 2 * p + j
                    i, _count = place_of(t, sl)
                    nc.gpsimd.indirect_dma_start(place[i], None, uv,
                                                 bass.IndirectOffsetOnAxis(ap=idx[:, sl:sl + 1], axis=0)) \
                      .then_inc(gathered[i].sem, 16)

        def vector_tile(dve, t, stream, with_next):
            if not is_first(t):
                publish(dve, 1)
                done_c = chain(dve)
                done_c(V.tensor_copy(gate[:, :], gate_next[:, :, :].rearrange("p h k -> p (h k)")))
                dve.wait_ge(h_in.sem, t * 16)
                h_taken.on(V.tensor_copy(hcur[:, :], spare[:, 0:D]))
                dve.wait_ge(h_taken.sem, t * 1)
            heads = heads_at(t)

            def spread(p):
                dve.wait_ge(gel.sem, t * PAIRS + (p + 1))
                dve.wait_ge(used.sem, t * PAIRS + (PRIME + p - 1))
                for j in range(2):
                    last = V.tensor_scalar(diag[:, p % 2, j, :], m.ident[:, :], act_[:, p % 2, j:j + 1],
                                           gate[:, 2 * p + j:2 * p + j + 1], ALU.mult, ALU.mult)
                dg.on(last)

            for p in range(PAIRS):
                dve.wait_ge(dots.sem, t * PAIRS + (p + 1))
                for j in range(2):
                    i, count = place_of(t, 2 * p + j)
                    dve.wait_ge(gathered[i].sem, count)
                    last = V.tensor_tensor_reduce(out=junk[:, j, :], in0=place[i][:, 0:D], in1=hcur[:, :], scale=1.0,
                                                  scalar=0.0, op0=ALU.mult, op1=ALU.add, accum_out=dot[:, p % 2, j:j + 1])
                dots.on(last)
                if is_first(t):
                    spread(p)
                elif p:
                    spread(p - 1)
                if is_first(t):
                    for h, part in first_heads_at(p - 1):
                        if part == TOPK_PARTS - 1:
                            gate0_norm(dve, h)
                    for h, part in first_heads_at(p):
                        topk_part(dve, 0, TOPK_PARTS * h + part)
                if not with_next:
                    continue
                for h in range(PH):
                    if 1 <= p - heads[h] <= TOPK_PARTS:
                        topk_part(dve, t + 1, TOPK_PARTS * h + p - heads[h] - 1)
                if p == heads[-1] + 5:
                    gates_shift(dve, t + 1)
                if p == max(PAIRS // 2, heads[PH // 2 - 1] + 4) + 3:
                    publish(dve, 0)
                if p == heads[-1] + 9:
                    gates_norm(dve, t + 1)
            if not is_first(t):
                spread(PAIRS - 1)
            if with_next and heads[-1] + 9 >= PAIRS:
                gates_norm(dve, t + 1)
            c = chain(dve)
            dve.wait_ge(used.sem, t * PAIRS + (PRIME + PAIRS))
            dve.wait_ge(sq.sem, t + 1)
            xt = m.x[:, bass.ds(t, 1), :].rearrange("p a d -> p (a d)")
            for j in range(2):
                cols = slice(512 * j, 512 * j + 512)
                c(V.tensor_tensor(prod[:, cols], acc[j][:, :], m.gate2[:, stream, cols], ALU.mult))
            acc_free.on(V.tensor_tensor(xt, xt, prod[:, :], ALU.add))

        def stage_scores_act(act, t, h):
            act.wait_ge(tk.sem, t * PH + (h + 1 - PH + is_next(t)))
            qc.on(nc.scalar.activation(qs[:, 1 if is_next(t) else h % 2, :, :], qt[:, 2 * h:2 * h + 2, bass.ds(t * P, P)], ACT.Copy))

        def scalar_tile(act, t, with_next):
            for p in range(PAIRS):
                if is_first(t):
                    copy_queries(act, p)
                if with_next and p in heads_at(t):
                    stage_scores_act(act, t + 1, heads_at(t).index(p))
                act.wait_ge(dots.sem, t * PAIRS + (p + 2))
                gel.on(nc.scalar.activation(act_[:, p % 2, :], dot[:, p % 2, :], ACT.Gelu_apprx_tanh))
                if is_first(t):
                    for h, part in first_heads_at(p):
                        if part == TOPK_PARTS - 1:
                            exp_gates0(act, h)
                if with_next and p == heads_at(t)[-1] + 6:
                    exp_gates(act, t + 1)
            act.wait_ge(acc_free.sem, t + 2)
            sq.on(nc.scalar.activation(prod[:, :], m.x[:, bass.ds(t, 1), :].rearrange("p a d -> p (a d)"), ACT.Square,
                                       accum_out=m.ssq[:, bass.ds(t, 1)]))

        def exp_gates(act, t):
            act.wait_ge(exi.sem, t * 1)
            ex.on(nc.scalar.activation(gate_next[:, :, :], gate_next[:, :, :], ACT.Exp))

        def exp_gates0(act, h):
            act.wait_ge(exi0.sem, h + 1)
            g = gate[:, h * TOPK:(h + 1) * TOPK]
            ex0.on(nc.scalar.activation(g, g, ACT.Exp))

        def scores(pe, t, h):
            if is_first(t):
                pe.wait_ge(cp0.sem, 2 * (h + 1))
            else:
                pe.wait_ge(qc.sem, t * PH + (h + 1 - PH))
            q = qs[:, 0 if is_first(t) else 1 if is_next(t) else h % 2, :, :]
            for z in range(2):
                last = nc.tensor.matmul(scores_of(t, h)[z], q[:, z, :], keys[:, 2 * h + z, :], start=True, stop=True)
            (sc0 if is_first(t) else sc).on(last)

        def tensor_tile(pe, t, with_next):
            for p in range(PAIRS):
                if is_first(t):
                    for h, z in ended_at(p, "first"):
                        if z == 1:
                            scores(pe, 0, h)
                    products(pe, shares[p])
                if with_next and p in heads_at(t):
                    scores(pe, t + 1, heads_at(t).index(p))
                pe.wait_ge(dg.sem, t * PAIRS + (p + 1))
                if p == 0:
                    pe.wait_ge(acc_free.sem, t + 1)
                for j in range(2):
                    for c in range(2):
                        last = nc.tensor.matmul(acc[c][:, :], diag[:, p % 2, j, :],
                                                place[place_of(t, 2 * p + j)[0]][:, D + 512 * c:D + 512 * c + 512],
                                                start=(p == 0 and j == 0), stop=(p == PAIRS - 1 and j == 1))
                used.on(last)

        def weights(sp, h0, h1):
            for h in range(h0, h1):
                if h >= 2:
                    sp.wait_ge(rest_mm.sem, 2 * (h - 1))
                w_in[h % 2].on(sp.dma_start(wq[h % 2], w_view[:, :, GW * h:GW * (h + 1)]), 16)

        def products(pe, share):
            for kind, h, z, k, c in share:
                t0, cols = (0, P) if kind == "first" else parts[c]
                if kind == "first":
                    out = m.bank[2][:, z * P:(z + 1) * P]
                    if k == z == 0:
                        pe.wait_ge(w_in[h % 2].sem, 16 * (h // 2 + 1))
                        if h:
                            pe.wait_ge(tk0.sem, h)
                else:
                    out = m.bank[4 + 2 * z + c][:, :cols]
                    if (k, c) == (0, 0) and h:
                        pe.wait_ge(rest_cp.sem, len(parts) * (2 * (h - 1) + z + 1))
                last = nc.tensor.matmul(out, wq[h % 2][:, k, z * P:(z + 1) * P], ht[:, k, t0:t0 + cols],
                                        start=(k == 0), stop=(k == KC - 1))
                if ends(kind, k, c):
                    (mm0 if kind == "first" else rest_mm).on(last)

        def ends(kind, k, c):
            return k == KC - 1 and (kind == "first" or c == len(parts) - 1)

        def ended_at(p, which):
            return [(h, z) for kind, h, z, k, c in (shares[p - 1] if p else []) if kind == which and ends(kind, k, c)]

        def stage_first(act, h, z):
            act.wait_ge(mm0.sem, 2 * h + 2)
            if z == 0 and h:
                act.wait_ge(sc0.sem, h)
            cp0.on(nc.scalar.activation(qs[:, 0, z, :], m.bank[2][:, z * P:(z + 1) * P], ACT.Copy))

        def copy_rest(act, h, z):
            act.wait_ge(rest_mm.sem, 2 * h + z + 1)
            for c, (t0, cols) in enumerate(parts):
                rest_cp.on(nc.scalar.activation(qt[:, 2 * h + z, t0:t0 + cols], m.bank[4 + 2 * z + c][:, :cols], ACT.Copy))
            act.wait_ge(rest_cp.sem, rest_cp.n)

        def copy_queries(act, p):
            for h, z in ended_at(p, "first"):
                if z == 1:
                    stage_first(act, h, 0)
                    stage_first(act, h, 1)
            for h, z in ended_at(p, "rest"):
                copy_rest(act, h, z)

        turn = min(n - 1, NTL)

        def every_tile(eng, body):
            body(0, 0, True)
            with eng.Fori(1, turn) as t:
                body(t, 0, True)
            for t in range(turn, n):
                body(t, t // NTL, t + 1 < n)

        @block.sync
        def _(sp):
            weights(sp, 0, 1)
            sp.dma_start(keys[:, :, :], a["peer_keys"][l]).then_inc(k_in.sem, 16)
            for i, t in enumerate(tiles):
                sp.wait_ge(norm.h_done.sem, i + 1)
                h_out.on(sp.dma_start(m.h_out[t * P:(t + 1) * P, :], m.h[:, t, :]), 16)
            sp.wait_ge(h_out.sem, 16 * n)
            sp.wait_ge(norm.turned.sem, 2 * n)
            weights(sp, 1, PH)
            sp.wait_ge(rest_mm.sem, 2 * PH)
            sp.dma_start(spare[:, 0:D], m.h_out[P:2 * P, :]).then_inc(h_in.sem, 16)
            with sp.Fori(1, n - 1) as t:
                sp.wait_ge(h_taken.sem, t * 1)
                sp.dma_start(spare[:, 0:D], m.h_out[bass.ds((t + 1) * P, P), :]).then_inc(h_in.sem, 16)

        @block.gpsimd
        def _(pool):
            every_tile(pool, lambda t, st, nxt: pool_tile(pool, t))
            for j, g in enumerate(gathered):
                g.n += 16 * (first_uses[j] + (n - 1) * SLOTS // RING)

        @block.vector
        def _(dve):
            norm.vector(dve)
            h_first.on(V.tensor_copy(hcur[:, :], m.h[:, 0, :]))
            dve.sem_inc(tk.sem, 2)
            dve.sem_inc(dots.sem, 1)
            dve.sem_inc(acc_free.sem, 1)
            for part in range(TOPK_PARTS):
                topk_part(dve, 0, part)
            gate0_norm(dve, 0)
            every_tile(dve, lambda t, st, nxt: vector_tile(dve, t, st, nxt))

        @block.scalar
        def _(act):
            norm.scalar(act, 0, 1)
            stage_first(act, 0, 0)
            stage_first(act, 0, 1)
            norm.scalar(act, 1)
            exp_gates0(act, 0)
            copy_rest(act, 0, 0)
            copy_rest(act, 0, 1)
            stage_first(act, 1, 0)
            stage_first(act, 1, 1)
            act.sem_inc(sq.sem, 1)
            every_tile(act, lambda t, st, nxt: scalar_tile(act, t, nxt))

        @block.tensor
        def _(pe):
            norm.tensor(pe, 0, 1)
            first = lambda h: [("first", h, z, k, 0) for z in range(2) for k in range(KC)]
            products(pe, first(0))
            pe.wait_ge(k_in.sem, 16)
            scores(pe, 0, 0)
            norm.tensor(pe, 1)
            products(pe, [("rest", 0, z, k, c) for z in range(2) for k in range(KC) for c in range(len(parts))])
            products(pe, first(1))
            scores(pe, 0, 1)
            pe.sem_inc(used.sem, PRIME)
            every_tile(pe, lambda t, st, nxt: tensor_tile(pe, t, nxt))


def stage_final(m, a, out):
    nc = m.nc
    with Stage(m, last=True) as s:
        fg, ssq = s.sb("final_gain", [P, D]), m.ssq[:, 0:NTL]
        g_in, ms, rt, fo, st = (s.sem(x) for x in ("final_gain_loaded", "f_mean", "f_root", "final_done", "stored"))
        block = s.block()

        @block.sync
        def _(sp):
            sp.dma_start(fg[:, :], a["final_g"].broadcast_to([P, D])).then_inc(g_in.sem, 16)
            for t in range(NTL):
                sp.wait_ge(fo.sem, t + 1)
                sp.dma_start(out[t * P:(t + 1) * P, :], m.h[:, t, :]).then_inc(st.sem, 16)
            sp.wait_ge(st.sem, 16 * NTL)

        @block.scalar
        def _(act):
            act.wait_ge(ms.sem, 2)
            rt.on(nc.scalar.activation(ssq[:, :], ssq[:, :], ACT.Sqrt))

        @block.vector
        def _(dve):
            done(dve, ms, nc.vector.tensor_scalar(ssq[:, :], ssq[:, :], 1.0 / D, EPS, ALU.mult, ALU.add))
            ms.on(nc.vector.reciprocal(ssq[:, :], ssq[:, :]))
            dve.wait_ge(rt.sem, 1)
            dve.wait_ge(g_in.sem, 16)
            for t in range(NTL):
                fo.on(nc.vector.scalar_tensor_tensor(out=m.h[:, t, :], in0=m.x[:, t, :], scalar=ssq[:, t:t + 1],
                                                     in1=fg[:, :], op0=ALU.mult, op1=ALU.mult))


def build(nc, a, out, until=None):
    count = [0]

    def go(stage, *args):
        count[0] += 1
        if until is None or count[0] <= until:
            stage(*args)

    with ExitStack() as ctx:
        m = Machine(nc, ctx)
        every = list(range(NT))
        spans = [(0, SEQ), (SEQ, CTX)]
        for l in range(DEPTH):
            tiles = every if l < DEPTH - 1 else every[:NTL]
            out_spans = spans[:2 if l < DEPTH - 1 else 1]
            view = lambda w: w[l].rearrange("(k p) n -> p k n", p=P)
            ht = m.ring[:, 0:KC * TOK].rearrange("p (k t) -> p k t", k=KC)
            rows = m.ring[:, KC * TOK:].rearrange("p (s j d) -> p s j d", s=2, j=N_MOD - 1)
            if l == 0:
                go(stage_modulation, m, a, rows, ht)
            base = rows[:, 0, 0:2, :].rearrange("p c (u n) -> p c u n", u=UNITS)
            wide = rows[:, 1, 0, :].rearrange("p (d f c j h) -> p d f c j h", d=2, f=2, c=2, j=4)
            lc = rows[:, 1, 1, :].rearrange("p (c u h) -> p c u h", c=2, u=UNITS)
            q, k, cb, cc, cx, su = (m.part(i * 2 * TOK, "f t", f=2, t=TOK) for i in (0, 1, 2, 3, 4, 7))
            v, fz = (m.part(i * 2 * TOK, "t n", t=NT, n=GW) for i in (5, 6))
            go(stage_inputs, m, a, l, rows,
               [(7, su, True, spans), (0, q, True, out_spans), (1, k, True, spans), (2, v, False, every),
                (3, cb, True, out_spans), (4, cc, True, out_spans), (5, cx, True, out_spans),
                (6, fz, False, tiles)], view(a["w_in"]), ht, m.seeds, m.tmp, wide, lc, base)
            y = m.h
            htf = ht.rearrange("p k t -> p (k t)")
            end = NTL * 2 * SEQ
            tables = [("dft_lat", htf[:, 0:end].rearrange("p (t c n) -> p t c n", t=NTL, c=2)),
                      ("dft_ctx", htf[:, end:end + 4 * CTX].rearrange("p (t c n) -> p t c n", t=NT - NTL, c=2)),
                      ("dft_chan", htf[:, end + 4 * CTX:end + 4 * CTX + 2 * P].rearrange("p (c n) -> p c n", c=2))]
            go(stage_attention, m, a, l, q, k, v, y, tiles, ht, tables)
            go(stage_conv_fourier, m, a, l, cb, cc, cx, fz, y, tiles, tables)
            go(stage_s5, m, a, l, su, y, tiles, m.seeds, m.tmp[:, 5, :], wide, lc, base, ht)
            go(stage_merge, m, a, l, rows, y, ht, tiles)
            go(stage_peer, m, a, l, rows, ht, view(a["peer_wq"]), tiles)
            if l < DEPTH - 1:
                go(stage_clear, m)
        if until is None:
            stage_final(m, a, out)


def constants():
    i = np.arange(TOPK)
    col = np.arange(GRID_W)
    start = np.clip(col - 8, 0, GRID_W - 16)
    ok = (col[None, :] >= start[:, None]) & (col[None, :] < start[:, None] + 16)
    mask = np.where(ok, 0.0, -1e30).astype(np.float32)

    def dft(n, scale):
        w = 2 * np.pi * (np.outer(np.arange(n), np.arange(n)) % n) / n
        return np.cos(w) * scale, np.sin(w) * scale

    def positions(n):
        t = np.stack(dft(n, 1 / math.sqrt(n * DH)), 1).astype(np.float32)
        return np.ascontiguousarray(t.reshape(n // P, P, 2, n).transpose(1, 0, 2, 3))

    chan = np.zeros((P, 2, P), np.float32)
    c, sn = dft(DH, 1.0)
    for b in range(2):
        r = slice(b * DH, (b + 1) * DH)
        chan[r, 0, r], chan[r, 1, r] = c, -sn
    turn = np.zeros((P, P), np.float32)
    for b in range(2):
        turn[b * GRID_W:(b + 1) * GRID_W, b * GRID_W:(b + 1) * GRID_W] = np.eye(GRID_W)[::-1]
    return {
        "ident": np.eye(P, dtype=np.float32), "flip": turn,
        "iota": np.tile(i.astype(np.float32), (P, 1)),
        "col_mask": np.concatenate([mask, mask]),
        "dft_lat": positions(SEQ), "dft_ctx": positions(CTX), "dft_chan": chan,
    }


def layouts(x, c, ctx, c_ctx, ada_w, ada_b, norm1_g, norm2_g, w_in, na_rpb, conv_w, s5_a_re, s5_a_im, s5_b_re,
            s5_b_im, s5_c_re, s5_c_im, s5_log_dt, s5_d, s5_w_glu, grp_g, w_out, peer_wq, peer_keys, peer_u, peer_v,
            final_g):
    L = DEPTH

    def states(t):
        t = t.reshape(L, 2, 8, P, *t.shape[4:])
        return np.moveaxis(t, 3, 1).reshape(L, P, UNITS, *t.shape[4:])

    log_dt = np.repeat(s5_log_dt[..., None], DH, axis=-1)
    rpb = np.zeros((L, NH, 17, 2 * GRID_W - 1), np.float32)
    rpb[:, :, 1:16, 48:79] = na_rpb
    return {
        "x": x[0], "ctx": ctx[0],
        "cond": np.stack([c[0], c_ctx]).reshape(2, KC, P).transpose(2, 1, 0),
        "ada_w": ada_w, "ada_b": ada_b, "norm1_g": norm1_g, "norm2_g": norm2_g, "w_in": w_in,
        "rpb": rpb, "conv_w": conv_w.reshape(L, 3, 2, P).transpose(0, 3, 2, 1),
        "s5_params": np.stack([states(s5_a_re), states(s5_a_im), states(log_dt)], 2),
        "s5_b": np.stack([states(s5_b_re), states(s5_b_im)], 2),
        "s5_c": np.stack([states(t.transpose(0, 1, 2, 4, 3)) for t in (s5_c_re, s5_c_im)], 2),
        "s5_d": s5_d.reshape(L, 2, P).transpose(0, 2, 1), "s5_w_glu": s5_w_glu,
        "grp_g": grp_g.reshape(L, D), "w_out": w_out, "peer_wq": peer_wq,
        "peer_keys": peer_keys.reshape(L, HALVES, PK, P).transpose(0, 3, 1, 2),
        **{f"peer_uv{l}": np.concatenate([peer_u[l], peer_v[l]], axis=-1) for l in range(L)},
        "final_g": final_g[None, :],
    }


def kernel(**inputs):
    import concourse.bacc as bacc
    from concourse.bass_utils import run_bass_kernel_spmd

    arrays = layouts(**{n: np.asarray(v) for n, v in inputs.items()})
    arrays.update(constants())
    arrays = {n: np.ascontiguousarray(v) for n, v in arrays.items()}
    nc = bacc.Bacc("TRN2", target_bir_lowering=False, num_devices=1)
    aps = {n: nc.dram_tensor(f"in_{n}", v.shape, F32, kind="ExternalInput").ap() for n, v in arrays.items()}
    out = nc.dram_tensor("out", (SEQ, D), F32, kind="ExternalOutput").ap()
    build(nc, aps, out)
    r = run_bass_kernel_spmd(nc, [{f"in_{n}": v for n, v in arrays.items()}], core_ids=[0])
    return r.results[0]["out"].reshape(1, SEQ, D)
```
